# Optimizing a Trainium2 kernel written in Bass

```python
import jax
import jax.numpy as jnp
from jax import lax
import numpy as np
import jax, jax.numpy as jnp

D_MODEL = 1024
BATCH = 1
SEQ = 512
DEPTH = 2

CHUNK = 64
Q_BLOCK = 128
MEM_LEN = 256

MLA_HEADS = 8
QK_NOPE_DIM = 64
QK_ROPE_DIM = 32
V_HEAD_DIM = 64
Q_LORA_RANK = 256
KV_LORA_RANK = 256
MLA_WIDTH = MLA_HEADS * V_HEAD_DIM
CONV_WIDTH = D_MODEL - MLA_WIDTH
CONV_TAPS = 31
IN_COLS = Q_LORA_RANK + KV_LORA_RANK + QK_ROPE_DIM + 2 * CONV_WIDTH

XA_HEADS = 4
XA_HEAD_DIM = D_MODEL // XA_HEADS

FFN_HIDDEN = ((8 * D_MODEL + 3 * 256 - 1) // (3 * 256)) * 256

ALPHA = (2.0 * DEPTH) ** 0.25
BETA = (8.0 * DEPTH) ** -0.25

ROPE_BASE = 10000.0
LN_EPS = 1e-5
RMS_EPS = 1e-6


def layer_norm(x, g, b):
    xf = x.astype(jnp.float32)
    mu = jnp.mean(xf, axis=-1, keepdims=True)
    var = jnp.mean(jnp.square(xf - mu), axis=-1, keepdims=True)
    y = (xf - mu) * lax.rsqrt(var + LN_EPS)
    return (y * g.astype(jnp.float32) + b.astype(jnp.float32)).astype(x.dtype)

def rms_norm(x, g):
    xf = x.astype(jnp.float32)
    y = xf * lax.rsqrt(jnp.mean(jnp.square(xf), axis=-1, keepdims=True) + RMS_EPS)
    return (y * g.astype(jnp.float32)).astype(x.dtype)

def rope_cos_sin(positions, dim):
    inv_freq = ROPE_BASE ** (-jnp.arange(0, dim, 2, dtype=jnp.float32) / dim)
    ang = positions.astype(jnp.float32)[..., None] * inv_freq
    return jnp.cos(ang), jnp.sin(ang)

def apply_rope(x, cos, sin):
    half = x.shape[-1] // 2
    x1 = x[..., :half].astype(jnp.float32)
    x2 = x[..., half:].astype(jnp.float32)
    return jnp.concatenate([x1 * cos - x2 * sin, x1 * sin + x2 * cos], axis=-1).astype(x.dtype)

def mla_group(c_q, c_kv, k_r, cos, sin, q_norm_g, w_uq, kv_norm_g, w_ukv):
    B, S, _ = c_q.shape
    q = (rms_norm(c_q, q_norm_g) @ w_uq).reshape(B, S, MLA_HEADS, QK_NOPE_DIM + QK_ROPE_DIM)
    q_nope, q_rope = q[..., :QK_NOPE_DIM], q[..., QK_NOPE_DIM:]
    q_rope = apply_rope(q_rope, cos[:, :, None, :], sin[:, :, None, :])
    kv = (rms_norm(c_kv, kv_norm_g) @ w_ukv).reshape(B, S, MLA_HEADS, QK_NOPE_DIM + V_HEAD_DIM)
    k_nope, v = kv[..., :QK_NOPE_DIM], kv[..., QK_NOPE_DIM:]
    k_rope = apply_rope(k_r, cos, sin)
    scale = (QK_NOPE_DIM + QK_ROPE_DIM) ** -0.5
    outs = []
    for start in range(0, S, Q_BLOCK):
        end = start + Q_BLOCK
        s = (jnp.einsum('bqhd,bkhd->bhqk', q_nope[:, start:end], k_nope[:, :end])
             + jnp.einsum('bqhr,bkr->bhqk', q_rope[:, start:end], k_rope[:, :end]))
        q_chunk = jnp.arange(start, end) // CHUNK
        k_chunk = jnp.arange(end) // CHUNK
        mask = k_chunk[None, :] <= q_chunk[:, None]
        s = jnp.where(mask[None, None], s.astype(jnp.float32) * scale, -jnp.inf)
        p = jax.nn.softmax(s, axis=-1).astype(v.dtype)
        outs.append(jnp.einsum('bhqk,bkhd->bqhd', p, v[:, :end]))
    o = jnp.concatenate(outs, axis=1)
    return o.reshape(B, S, MLA_WIDTH)

def conformer_conv_group(u, dw_w, dw_b, norm_g, norm_b):
    a, g = jnp.split(u, 2, axis=-1)
    h = a * jax.nn.sigmoid(g)
    h = jnp.pad(h, ((0, 0), (CONV_TAPS - 1, 0), (0, 0)))
    h = lax.conv_general_dilated(
        h, dw_w[:, None, :], window_strides=(1,), padding='VALID',
        dimension_numbers=('NWC', 'WIO', 'NWC'), feature_group_count=CONV_WIDTH) + dw_b
    h = layer_norm(h, norm_g, norm_b)
    return jax.nn.silu(h)

def hybrid_mixer(x, cos, sin, w_in, b_in, q_norm_g, w_uq, kv_norm_g, w_ukv,
                 dw_w, dw_b, cn_g, cn_b, w_o):
    proj = x @ w_in + b_in
    o1 = Q_LORA_RANK
    o2 = o1 + KV_LORA_RANK
    o3 = o2 + QK_ROPE_DIM
    c_q, c_kv, k_r, u = proj[..., :o1], proj[..., o1:o2], proj[..., o2:o3], proj[..., o3:]
    y_att = mla_group(c_q, c_kv, k_r, cos, sin, q_norm_g, w_uq, kv_norm_g, w_ukv)
    y_conv = conformer_conv_group(u, dw_w, dw_b, cn_g, cn_b)
    return jnp.concatenate([y_att, y_conv], axis=-1) @ w_o

def memory_cross_attention(x, mem, w_q, w_kv, w_o):
    B, S, D = x.shape
    M = mem.shape[1]
    q = (x @ w_q).reshape(B, S, XA_HEADS, XA_HEAD_DIM)
    kv = (mem @ w_kv).reshape(B, M, 2, XA_HEADS, XA_HEAD_DIM)
    k, v = kv[:, :, 0], kv[:, :, 1]
    s = jnp.einsum('bshd,bmhd->bhsm', q, k).astype(jnp.float32) * (XA_HEAD_DIM ** -0.5)
    p = jax.nn.softmax(s, axis=-1).astype(v.dtype)
    o = jnp.einsum('bhsm,bmhd->bshd', p, v).reshape(B, S, D)
    return o @ w_o

def swiglu_ffn(x, w_in, w_down):
    gu = x @ w_in
    g, up = gu[..., :FFN_HIDDEN], gu[..., FFN_HIDDEN:]
    return (jax.nn.silu(g) * up) @ w_down

def first_inputs(seed: int = 0) -> dict:
    key = jax.random.key(seed)
    ks = jax.random.split(key, 32)
    L, D = DEPTH, D_MODEL

    def normal(k, shape, fan_in, scale=1.0):
        return jax.random.normal(k, shape, jnp.float32) * (scale * fan_in ** -0.5)

    def gain(k, shape):
        return 1.0 + 0.02 * jax.random.normal(k, shape, jnp.float32)

    def small(k, shape):
        return 0.02 * jax.random.normal(k, shape, jnp.float32)

    x = jax.random.normal(ks[0], (BATCH, SEQ, D), jnp.float32)
    mem = jax.random.normal(ks[1], (BATCH, MEM_LEN, D), jnp.float32)
    offset = jax.random.randint(ks[2], (BATCH, 1), 0, 4096, dtype=jnp.int32)
    positions = offset + jnp.arange(SEQ, dtype=jnp.int32)[None, :]

    w_uk = normal(ks[7], (L, KV_LORA_RANK, MLA_HEADS, QK_NOPE_DIM), KV_LORA_RANK)
    w_uv = normal(ks[8], (L, KV_LORA_RANK, MLA_HEADS, V_HEAD_DIM), KV_LORA_RANK, BETA)
    mla_w_ukv = jnp.concatenate([w_uk, w_uv], axis=-1).reshape(
        L, KV_LORA_RANK, MLA_HEADS * (QK_NOPE_DIM + V_HEAD_DIM))
    xa_w_k = normal(ks[18], (L, D, D), D)
    xa_w_v = normal(ks[19], (L, D, D), D, BETA)
    xa_w_kv = jnp.concatenate([xa_w_k, xa_w_v], axis=-1)

    return {
        "x": x,
        "mem": mem,
        "positions": positions,
        "mix_w_in": normal(ks[3], (L, D, IN_COLS), D),
        "mix_b_in": small(ks[4], (L, IN_COLS)),
        "mla_q_norm": gain(ks[5], (L, Q_LORA_RANK)),
        "mla_w_uq": normal(ks[6], (L, Q_LORA_RANK, MLA_HEADS * (QK_NOPE_DIM + QK_ROPE_DIM)), Q_LORA_RANK),
        "mla_kv_norm": gain(ks[9], (L, KV_LORA_RANK)),
        "mla_w_ukv": mla_w_ukv,
        "conv_dw_w": normal(ks[10], (L, CONV_TAPS, CONV_WIDTH), CONV_TAPS),
        "conv_dw_b": small(ks[11], (L, CONV_WIDTH)),
        "conv_norm_g": gain(ks[12], (L, CONV_WIDTH)),
        "conv_norm_b": small(ks[13], (L, CONV_WIDTH)),
        "mix_w_o": normal(ks[14], (L, D, D), D, BETA),
        "ln1_g": gain(ks[15], (L, D)),
        "ln1_b": small(ks[16], (L, D)),
        "xa_w_q": normal(ks[17], (L, D, D), D),
        "xa_w_kv": xa_w_kv,
        "xa_w_o": normal(ks[20], (L, D, D), D, BETA),
        "ln2_g": gain(ks[21], (L, D)),
        "ln2_b": small(ks[22], (L, D)),
        "ffn_w_in": normal(ks[23], (L, D, 2 * FFN_HIDDEN), D),
        "ffn_w_down": normal(ks[24], (L, FFN_HIDDEN, D), FFN_HIDDEN, BETA),
        "ln3_g": gain(ks[25], (L, D)),
        "ln3_b": small(ks[26], (L, D)),
    }

def first_block(x, mem, positions, mix_w_in, mix_b_in, mla_q_norm, mla_w_uq, mla_kv_norm,
              mla_w_ukv, conv_dw_w, conv_dw_b, conv_norm_g, conv_norm_b, mix_w_o,
              ln1_g, ln1_b, xa_w_q, xa_w_kv, xa_w_o, ln2_g, ln2_b,
              ffn_w_in, ffn_w_down, ln3_g, ln3_b):
    cos, sin = rope_cos_sin(positions, QK_ROPE_DIM)
    for l in range(DEPTH):
        y = hybrid_mixer(x, cos, sin, mix_w_in[l], mix_b_in[l], mla_q_norm[l], mla_w_uq[l],
                         mla_kv_norm[l], mla_w_ukv[l], conv_dw_w[l], conv_dw_b[l],
                         conv_norm_g[l], conv_norm_b[l], mix_w_o[l])
        x = layer_norm(ALPHA * x + y, ln1_g[l], ln1_b[l])
        y = memory_cross_attention(x, mem, xa_w_q[l], xa_w_kv[l], xa_w_o[l])
        x = layer_norm(ALPHA * x + y, ln2_g[l], ln2_b[l])
        y = swiglu_ffn(x, ffn_w_in[l], ffn_w_down[l])
        x = layer_norm(ALPHA * x + y, ln3_g[l], ln3_b[l])
    return x


DEPTH_2 = 1

HEAD_DIM = 64
ATTN_PAIRS = ((128, 1), (512, 4), (2048, 16))
ATTN_GROUPS = 3
ATTN_HEADS_PER_GROUP = 8
ATTN_BLOCK = 64
ROPE_THETA = 10000.0
RET_HEADS = 8
RET_QK_DIM = 64
RET_V_DIM = 128
RET_CHUNK = 128
MOE_GROUPS = 8
MOE_EXPERTS_PER_GROUP = 8
MOE_N_EXPERTS = MOE_GROUPS * MOE_EXPERTS_PER_GROUP
MOE_TOP_K = 2
MOE_HIDDEN = 512
MOE_BLOCK = 128
NORM_EPS = 1e-6

ATTN_W = ATTN_GROUPS * ATTN_HEADS_PER_GROUP * HEAD_DIM
ATTN_OUT_W = ATTN_HEADS_PER_GROUP * HEAD_DIM
RET_QK_W = RET_HEADS * RET_QK_DIM
RET_V_W = RET_HEADS * RET_V_DIM
IN_SPLIT_POINTS = (ATTN_W, 2 * ATTN_W, 3 * ATTN_W,
                   3 * ATTN_W + RET_QK_W, 3 * ATTN_W + 2 * RET_QK_W,
                   3 * ATTN_W + 2 * RET_QK_W + RET_V_W,
                   3 * ATTN_W + 2 * RET_QK_W + 2 * RET_V_W)
IN_W = IN_SPLIT_POINTS[-1] + 2 * D_MODEL


def rms_norm_2(x, w):
    xf = x.astype(jnp.float32)
    y = xf * lax.rsqrt(jnp.mean(xf * xf, axis=-1, keepdims=True) + NORM_EPS)
    return (y * w.astype(jnp.float32)).astype(x.dtype)

def rotary_tables(seq_len):
    inv_freq = 1.0 / (ROPE_THETA ** (jnp.arange(0, HEAD_DIM, 2, dtype=jnp.float32) / HEAD_DIM))
    ang = jnp.arange(seq_len, dtype=jnp.float32)[:, None] * inv_freq[None, :]
    return jnp.cos(ang), jnp.sin(ang)

def apply_rotary(t, cos, sin):
    t1, t2 = jnp.split(t.astype(jnp.float32), 2, axis=-1)
    c = cos[None, :, None, :]
    s = sin[None, :, None, :]
    return jnp.concatenate([t1 * c - t2 * s, t1 * s + t2 * c], axis=-1)

def dilated_window_attention(q, k, v, dilation, half):
    B, S, H, Dh = q.shape
    L = S // dilation
    nb = -(-L // ATTN_BLOCK)
    Lp = nb * ATTN_BLOCK
    N = B * dilation

    def strided(t):
        t = t.reshape(B, L, dilation, H, Dh).transpose(0, 2, 3, 1, 4)
        return t.reshape(N, H, L, Dh)

    qb = jnp.pad(strided(q), ((0, 0), (0, 0), (0, Lp - L), (0, 0))).reshape(N, H, nb, ATTN_BLOCK, Dh)

    def band(t):
        tp = jnp.pad(strided(t), ((0, 0), (0, 0), (ATTN_BLOCK, Lp - L + ATTN_BLOCK), (0, 0)))
        tb = tp.reshape(N, H, nb + 2, ATTN_BLOCK, Dh)
        return jnp.concatenate([tb[:, :, :-2], tb[:, :, 1:-1], tb[:, :, 2:]], axis=3)

    kw = band(k)
    vw = band(v)
    scores = jnp.einsum('nhbqd,nhbkd->nhbqk', qb, kw) * (Dh ** -0.5)
    blk = jnp.arange(nb)[:, None] * ATTN_BLOCK
    q_pos = blk + jnp.arange(ATTN_BLOCK)[None, :]
    k_pos = blk - ATTN_BLOCK + jnp.arange(3 * ATTN_BLOCK)[None, :]
    rel = k_pos[:, None, :] - q_pos[:, :, None]
    in_range = (k_pos[:, None, :] >= 0) & (k_pos[:, None, :] < L)
    valid = (jnp.abs(rel) <= half) & (in_range | (rel == 0))
    scores = jnp.where(valid[None, None], scores, -jnp.inf)
    m = jnp.max(scores, axis=-1, keepdims=True)
    p = jnp.exp(scores - m)
    denom = jnp.sum(p, axis=-1, keepdims=True)
    out = jnp.einsum('nhbqk,nhbkd->nhbqd', p, vw) / denom
    lse = (m + jnp.log(denom))[..., 0]
    out = out.reshape(N, H, Lp, Dh)[:, :, :L].reshape(B, dilation, H, L, Dh)
    out = out.transpose(0, 3, 1, 2, 4).reshape(B, S, H, Dh)
    lse = lse.reshape(N, H, Lp)[:, :, :L].reshape(B, dilation, H, L)
    lse = lse.transpose(0, 3, 1, 2).reshape(B, S, H)
    return out, lse

def retention_chunkwise(q, k, v, log_g):
    B, H, S, Dk = q.shape
    Dv = v.shape[-1]
    C = RET_CHUNK
    nc = S // C
    qc = q.reshape(B, H, nc, C, Dk)
    kc = k.reshape(B, H, nc, C, Dk)
    vc = v.reshape(B, H, nc, C, Dv)
    idx = jnp.arange(C, dtype=jnp.float32)
    rel = idx[:, None] - idx[None, :]
    decay = jnp.where(rel[None] >= 0, jnp.exp(jnp.maximum(rel[None], 0.0) * log_g[:, None, None]), 0.0)
    scores = jnp.einsum('bhnqd,bhnkd->bhnqk', qc, kc) * decay[None, :, None]
    inner = jnp.einsum('bhnqk,bhnkv->bhnqv', scores, vc)
    zeta = jnp.exp((C - 1 - idx)[None, :] * log_g[:, None])
    kv = jnp.einsum('bhnkd,bhnkv->nbhdv', kc * zeta[None, :, None, :, None], vc)
    chunk_decay = jnp.exp(C * log_g)[None, :, None, None]

    def step(state, kv_chunk):
        return chunk_decay * state + kv_chunk, state

    _, prev_states = lax.scan(step, jnp.zeros((B, H, Dk, Dv), jnp.float32), kv)
    xi = jnp.exp((idx + 1.0)[None, :] * log_g[:, None])
    cross = jnp.einsum('bhnqd,nbhdv->bhnqv', qc * xi[None, :, None, :, None], prev_states)
    return (inner + cross).reshape(B, H, S, Dv)

def hybrid_mixer_2(xn, w_in, b_branch_gate, ret_decay_fwd, ret_decay_bwd, ret_gn_w,
                 w_attn_branch, w_ret_branch, w_out, cos, sin):
    B, S, _ = xn.shape
    proj = jnp.einsum('bsd,de->bse', xn, w_in)
    q_a, k_a, v_a, q_r, k_r, v_r, g_r, gate_logits = jnp.split(proj, IN_SPLIT_POINTS, axis=-1)

    n_a = ATTN_GROUPS * ATTN_HEADS_PER_GROUP
    q_a = apply_rotary(q_a.reshape(B, S, n_a, HEAD_DIM), cos, sin).reshape(B, S, ATTN_GROUPS, ATTN_HEADS_PER_GROUP, HEAD_DIM)
    k_a = apply_rotary(k_a.reshape(B, S, n_a, HEAD_DIM), cos, sin).reshape(B, S, ATTN_GROUPS, ATTN_HEADS_PER_GROUP, HEAD_DIM)
    v_a = v_a.astype(jnp.float32).reshape(B, S, ATTN_GROUPS, ATTN_HEADS_PER_GROUP, HEAD_DIM)
    outs = []
    lses = []
    for g, (window, dilation) in enumerate(ATTN_PAIRS):
        o, l = dilated_window_attention(q_a[:, :, g], k_a[:, :, g], v_a[:, :, g], dilation, window // (2 * dilation))
        outs.append(o)
        lses.append(l)
    mix_w = jax.nn.softmax(jnp.stack(lses, axis=0), axis=0)
    y_att = jnp.einsum('gbsh,gbshd->bshd', mix_w, jnp.stack(outs, axis=0)).reshape(B, S, ATTN_OUT_W)

    q_r = apply_rotary(q_r.reshape(B, S, RET_HEADS, RET_QK_DIM), cos, sin).transpose(0, 2, 1, 3)
    k_r = (apply_rotary(k_r.reshape(B, S, RET_HEADS, RET_QK_DIM), cos, sin) * (RET_QK_DIM ** -0.5)).transpose(0, 2, 1, 3)
    v_r = v_r.astype(jnp.float32).reshape(B, S, RET_HEADS, RET_V_DIM).transpose(0, 2, 1, 3)
    log_g_fwd = jax.nn.log_sigmoid(ret_decay_fwd.astype(jnp.float32))
    log_g_bwd = jax.nn.log_sigmoid(ret_decay_bwd.astype(jnp.float32))
    ret_f = retention_chunkwise(q_r, k_r, v_r, log_g_fwd)
    ret_b = jnp.flip(retention_chunkwise(jnp.flip(q_r, 2), jnp.flip(k_r, 2), jnp.flip(v_r, 2), log_g_bwd), 2)
    ret = ret_f + ret_b
    mu = jnp.mean(ret, axis=-1, keepdims=True)
    var = jnp.mean(jnp.square(ret - mu), axis=-1, keepdims=True)
    ret = (ret - mu) * lax.rsqrt(var + NORM_EPS)
    ret = ret.transpose(0, 2, 1, 3).reshape(B, S, RET_V_W) * ret_gn_w.astype(jnp.float32)
    y_ret = jax.nn.silu(g_r.astype(jnp.float32)) * ret

    gates = jax.nn.sigmoid((gate_logits + b_branch_gate).astype(jnp.float32))
    g_att, g_ret = jnp.split(gates, 2, axis=-1)
    merged = (g_att * jnp.einsum('bse,ed->bsd', y_att, w_attn_branch.astype(jnp.float32))
              + g_ret * jnp.einsum('bse,ed->bsd', y_ret, w_ret_branch.astype(jnp.float32)))
    return jnp.einsum('bsd,de->bse', merged.astype(xn.dtype), w_out)

def hierarchical_moe(x2, w_group, b_group, w_expert, b_expert, w1, w3, w2):
    T, D = x2.shape
    xf = x2.astype(jnp.float32)
    group_p = jax.nn.softmax(xf @ w_group.astype(jnp.float32) + b_group.astype(jnp.float32), axis=-1)
    g_w, g_idx = lax.top_k(group_p, 1)
    exp_logits = (xf @ w_expert.astype(jnp.float32) + b_expert.astype(jnp.float32)).reshape(T, MOE_GROUPS, MOE_EXPERTS_PER_GROUP)
    sel_logits = jnp.take_along_axis(exp_logits, g_idx[:, :, None], axis=1)[:, 0]
    e_w, e_idx = lax.top_k(jax.nn.softmax(sel_logits, axis=-1), MOE_TOP_K)
    e_w = e_w / jnp.sum(e_w, axis=-1, keepdims=True)
    gate = (g_w * e_w).reshape(-1)
    eid = (g_idx * MOE_EXPERTS_PER_GROUP + e_idx).reshape(-1).astype(jnp.int32)
    tok = jnp.repeat(jnp.arange(T, dtype=jnp.int32), MOE_TOP_K)
    A = T * MOE_TOP_K

    order = jnp.argsort(eid)
    s_eid = eid[order]
    s_tok = tok[order]
    s_gate = gate[order]
    counts = jnp.bincount(eid, length=MOE_N_EXPERTS)
    starts = jnp.cumsum(counts) - counts
    padded = (counts + MOE_BLOCK - 1) // MOE_BLOCK * MOE_BLOCK
    p_ends = jnp.cumsum(padded)
    p_starts = p_ends - padded
    dest = p_starts[s_eid] + (jnp.arange(A, dtype=jnp.int32) - starts[s_eid])
    n_blocks = -(-A // MOE_BLOCK) + MOE_N_EXPERTS
    slot_tok = jnp.full((n_blocks * MOE_BLOCK,), T, jnp.int32).at[dest].set(s_tok)
    blk_eid = jnp.clip(jnp.searchsorted(p_ends, jnp.arange(n_blocks) * MOE_BLOCK, side='right'), 0, MOE_N_EXPERTS - 1)
    x_pad = jnp.concatenate([x2, jnp.zeros((1, D), x2.dtype)], axis=0)
    x_slots = x_pad[slot_tok].reshape(n_blocks, MOE_BLOCK, D)

    def expert_block(args):
        xb, e = args
        hid = jax.nn.silu(xb @ w1[e]) * (xb @ w3[e])
        return hid @ w2[e]

    y_slots = lax.map(expert_block, (x_slots, blk_eid)).reshape(n_blocks * MOE_BLOCK, D)
    y_assign = y_slots[dest].astype(jnp.float32) * s_gate[:, None]
    return jax.ops.segment_sum(y_assign, s_tok, num_segments=T).astype(x2.dtype)

def second_inputs(seed: int = 0) -> dict:
    key = jax.random.key(seed)
    ks = jax.random.split(key, 20)
    L = DEPTH_2
    f32 = jnp.float32

    def nrm(k, shape, scale):
        return jax.random.normal(k, shape, f32) * scale

    heads = jnp.arange(RET_HEADS, dtype=f32)
    decay_logit = jnp.log(2.0 ** (5.0 + heads) - 1.0)
    return {
        'x': nrm(ks[0], (BATCH, SEQ, D_MODEL), 1.0),
        'norm_mix_w': 1.0 + nrm(ks[1], (L, D_MODEL), 0.02),
        'w_in': nrm(ks[2], (L, D_MODEL, IN_W), D_MODEL ** -0.5),
        'b_branch_gate': nrm(ks[3], (L, 2 * D_MODEL), 0.02),
        'ret_decay_fwd': decay_logit[None] + nrm(ks[4], (L, RET_HEADS), 0.05),
        'ret_decay_bwd': decay_logit[None] + nrm(ks[5], (L, RET_HEADS), 0.05),
        'ret_gn_w': 1.0 + nrm(ks[6], (L, RET_V_W), 0.02),
        'w_attn_branch': nrm(ks[7], (L, ATTN_OUT_W, D_MODEL), ATTN_OUT_W ** -0.5),
        'w_ret_branch': nrm(ks[8], (L, RET_V_W, D_MODEL), RET_V_W ** -0.5),
        'w_out': nrm(ks[9], (L, D_MODEL, D_MODEL), D_MODEL ** -0.5),
        'norm_moe_w': 1.0 + nrm(ks[10], (L, D_MODEL), 0.02),
        'moe_w_group': nrm(ks[11], (L, D_MODEL, MOE_GROUPS), D_MODEL ** -0.5),
        'moe_b_group': nrm(ks[12], (L, MOE_GROUPS), 0.01),
        'moe_w_expert': nrm(ks[13], (L, D_MODEL, MOE_N_EXPERTS), D_MODEL ** -0.5),
        'moe_b_expert': nrm(ks[14], (L, MOE_N_EXPERTS), 0.01),
        'moe_w1': nrm(ks[15], (L, MOE_N_EXPERTS, D_MODEL, MOE_HIDDEN), D_MODEL ** -0.5),
        'moe_w3': nrm(ks[16], (L, MOE_N_EXPERTS, D_MODEL, MOE_HIDDEN), D_MODEL ** -0.5),
        'moe_w2': nrm(ks[17], (L, MOE_N_EXPERTS, MOE_HIDDEN, D_MODEL), MOE_HIDDEN ** -0.5),
        'norm_final_w': 1.0 + nrm(ks[18], (D_MODEL,), 0.02),
    }

def second_block(x, norm_mix_w, w_in, b_branch_gate, ret_decay_fwd, ret_decay_bwd, ret_gn_w,
              w_attn_branch, w_ret_branch, w_out, norm_moe_w, moe_w_group, moe_b_group,
              moe_w_expert, moe_b_expert, moe_w1, moe_w3, moe_w2, norm_final_w):
    B, S, D = x.shape
    cos, sin = rotary_tables(S)
    h = x
    for l in range(DEPTH_2):
        xn = rms_norm_2(h, norm_mix_w[l])
        mix = hybrid_mixer_2(xn, w_in[l], b_branch_gate[l], ret_decay_fwd[l], ret_decay_bwd[l], ret_gn_w[l],
                           w_attn_branch[l], w_ret_branch[l], w_out[l], cos, sin)
        h = h + mix.astype(h.dtype)
        hn = rms_norm_2(h, norm_moe_w[l])
        ffn = hierarchical_moe(hn.reshape(B * S, D), moe_w_group[l], moe_b_group[l], moe_w_expert[l],
                               moe_b_expert[l], moe_w1[l], moe_w3[l], moe_w2[l])
        h = h + ffn.reshape(B, S, D).astype(h.dtype)
    return rms_norm_2(h, norm_final_w)


def setup_inputs(seed=0):
    out = dict(first_inputs(seed))
    for name, value in second_inputs(seed + 1).items():
        if name != "x":
            out[name + "_2"] = value
    return out


def reference(
    x, mem, positions, mix_w_in, mix_b_in, mla_q_norm, mla_w_uq, mla_kv_norm, mla_w_ukv,
    conv_dw_w, conv_dw_b, conv_norm_g, conv_norm_b, mix_w_o, ln1_g, ln1_b, xa_w_q, xa_w_kv,
    xa_w_o, ln2_g, ln2_b, ffn_w_in, ffn_w_down, ln3_g, ln3_b, norm_mix_w_2, w_in_2,
    b_branch_gate_2, ret_decay_fwd_2, ret_decay_bwd_2, ret_gn_w_2, w_attn_branch_2,
    w_ret_branch_2, w_out_2, norm_moe_w_2, moe_w_group_2, moe_b_group_2, moe_w_expert_2,
    moe_b_expert_2, moe_w1_2, moe_w3_2, moe_w2_2, norm_final_w_2,
):
    x = first_block(
        x, mem, positions, mix_w_in, mix_b_in, mla_q_norm, mla_w_uq, mla_kv_norm, mla_w_ukv,
        conv_dw_w, conv_dw_b, conv_norm_g, conv_norm_b, mix_w_o, ln1_g, ln1_b, xa_w_q, xa_w_kv,
        xa_w_o, ln2_g, ln2_b, ffn_w_in, ffn_w_down, ln3_g, ln3_b,
    )
    return second_block(
        x, norm_mix_w_2, w_in_2, b_branch_gate_2, ret_decay_fwd_2, ret_decay_bwd_2, ret_gn_w_2,
        w_attn_branch_2, w_ret_branch_2, w_out_2, norm_moe_w_2, moe_w_group_2, moe_b_group_2,
        moe_w_expert_2, moe_b_expert_2, moe_w1_2, moe_w3_2, moe_w2_2, norm_final_w_2,
    )


_drawn_inputs = setup_inputs


def setup_inputs(seed=0):
    import zlib

    import numpy as np

    out = dict(_drawn_inputs(seed))
    spreads = {}
    factors = {'mix_b_in': 4.368,
     'mla_q_norm': 8.0,
     'mla_kv_norm': 8.0,
     'conv_dw_b': 3.391,
     'conv_norm_g': 4.239,
     'conv_norm_b': 5.552,
     'norm_mix_w_2': 2.918,
     'b_branch_gate_2': 8.0,
     'ret_gn_w_2': 5.31,
     'norm_moe_w_2': 2.952,
     'moe_b_group_2': 6.906,
     'moe_b_expert_2': 7.187,
     'norm_final_w_2': 2.786}
    for name, (base, spread) in spreads.items():
        noise = np.random.default_rng([zlib.crc32(name.encode()), seed]).standard_normal(out[name].shape)
        drawn = base * np.exp(spread * noise) if base else spread * noise
        out[name] = jnp.asarray(drawn.astype(out[name].dtype))
    for name, factor in factors.items():
        out[name] = (out[name] * factor).astype(out[name].dtype)
    return out
```

```python
from contextlib import ExitStack

import numpy as np

import concourse.bass as bass
from concourse import mybir

F32 = mybir.dt.float32
I32 = mybir.dt.int32
BF16 = mybir.dt.bfloat16
F16 = mybir.dt.float16
ALU = mybir.AluOpType
ACT = mybir.ActivationFunctionType
AX = mybir.AxisListType

P = 128
S = 512
NT = S // P
D = 1024
KD = D // P
DEPTH = 2
BANK = 512

MEM = 256
MT = MEM // P
HEADS, NOPE, ROPE, VDIM = 8, 64, 32, 64
QKD = NOPE + ROPE
RANK = 256
CONV = 512
CT = CONV // P
TAPS = 31
XH = 4
XHD = D // XH
FFN = 2816
FT = FFN // P
ALPHA = float((2.0 * DEPTH) ** 0.25)
LN_EPS, RMS_EPS = 1e-5, 1e-6
KV_CHUNK = 64

AH, AHD, NG = 8, 64, 3
DIL = 4
WINDOWS = ((128, 1), (512, 4), (2048, 16))
RH, RQK, RV = 8, 64, 128
GROUPS, PER_GROUP = 8, 8
EXPERTS = GROUPS * PER_GROUP
EH = 512
CAP = 64
MORE = (2 * S - CAP) // CAP
BLOCKS = EXPERTS + MORE
NEG = -1.0e30

PC_LAYER = 1 + 2 * CT + 4 + CT * TAPS + 3 * CT
PC_KR, PC_UA, PC_UG, PC_QN, PC_W = 0, 1, 1 + CT, 1 + 2 * CT, 5 + 2 * CT
PC_DWB = PC_W + CT * TAPS
PC_CNG, PC_CNB = PC_DWB + CT, PC_DWB + 2 * CT
PC_GATE = DEPTH * PC_LAYER
PC_ALL = PC_GATE + 2 * KD


class Pool_:

    def __init__(self, buffers):
        self.free = [(b, None) for b in buffers]

    def take(self):
        assert self.free, "no buffer is free here"
        return self.free.pop(0)

    def give(self, buffer, after):
        self.free.append((buffer, after))


class Program:

    ENGINES = ("sync", "scalar", "vector", "tensor", "gpsimd")

    def __init__(self, nc, ctx):
        self.nc, self.ctx = nc, ctx
        self.queue = {e: [] for e in self.ENGINES}
        self.waited = {e: {} for e in self.ENGINES}
        self.reached = {}
        self.done = {}
        self.names = {}
        self.last_pool = None

    def semaphore(self, name):
        sem = self.ctx.enter_context(self.nc.semaphore(name))
        self.reached[name] = 0
        self.names[name] = sem
        return name

    def stage(self, name):
        for e in ("scalar", "vector", "tensor", "gpsimd"):
            self.done[e] = self.semaphore(f"{name}_{e}_done")

    def put(self, engine, waits, make, sem, by):
        def flat(ws):
            for w in ws:
                if isinstance(w, list):
                    yield from flat(w)
                elif w is not None:
                    yield w

        needed = []
        for w in flat(waits):
            if self.waited[engine].get(w[0], 0) < w[1]:
                self.waited[engine][w[0]] = w[1]
                needed = [x for x in needed if x[0] != w[0]] + [w]
        self.reached[sem] += by
        self.queue[engine].append((needed, make, sem, by))
        return (sem, self.reached[sem])

    def op(self, engine, make, *waits):
        return self.put(engine, waits, make, self.done[engine], 1)

    def pe(self, make, *waits):
        return self.op("tensor", make, *waits)

    def act(self, make, *waits):
        return self.op("scalar", make, *waits)

    def dve(self, make, *waits):
        return self.op("vector", make, *waits)

    def pool(self, make, *waits):
        self.last_pool = self.op("gpsimd", make, self.last_pool, *waits)
        return self.last_pool

    def dma(self, engine, sem, out, in_, *waits):
        return self.put(engine, waits, lambda e: e.dma_start(out, in_), sem, 16)

    def branch_if(self, flag, ready):
        for e in self.ENGINES:
            self.queue[e].append(([], None, flag, ready))
            self.waited[e][ready[0]] = max(ready[1], self.waited[e].get(ready[0], 0))
        self.before = ({e: dict(w) for e, w in self.waited.items()}, self.last_pool)

    def join(self, names):
        for e in self.ENGINES:
            for n in names:
                if self.reached[n]:
                    self.raw(e, lambda q, n=n, v=self.reached[n]: q.wait_ge(self.names[n], v))

    def branch_end(self):
        for e in self.ENGINES:
            self.queue[e].append(([], None, None, None))
        self.waited, self.last_pool = self.before

    def raw(self, engine, make):
        self.queue[engine].append(([], make, None, 0))

    def emit(self, block):
        def play(name):
            def body(e):
                guard = None
                for needed, make, sem, by in self.queue[name]:
                    if make is None and sem is not None:
                        e.wait_ge(self.names[by[0]], by[1])
                        guard = e.If(e.value_load(sem) > 0)
                        guard.__enter__()
                        continue
                    if make is None:
                        guard.__exit__(None, None, None)
                        continue
                    for s, v in needed:
                        e.wait_ge(self.names[s], v)
                    ins = make(e)
                    if sem is not None:
                        ins.then_inc(self.names[sem], by)
            return body

        for name in self.ENGINES:
            getter = {"sync": block.sync, "scalar": block.scalar, "vector": block.vector,
                      "tensor": block.tensor, "gpsimd": block.gpsimd}[name]
            getter(play(name))


def both_blocks(nc, a, result):
    ctx = ExitStack()
    with ctx:
        p = Program(nc, ctx)

        def sb(name, shape, dt=F32):
            return ctx.enter_context(nc.sbuf_tensor(name, shape, dt))

        psum = [ctx.enter_context(nc.psum_tensor(f"bank{i}", [P, BANK], F32)) for i in range(8)]
        banks = Pool_(psum)

        x_tok = sb("x_tok", [P, NT, D])
        xT = sb("xT", [P, KD, S])
        memT = sb("memT", [P, KD, MEM])
        ident = sb("ident", [P, P])
        swap_a = sb("swap_a", [P, P])
        swap_q = sb("swap_q", [QKD, QKD])
        cols = sb("cols", [P, PC_ALL])
        gain = sb("gain", [P, D])
        shift = sb("shift", [P, D])
        stat = sb("stat", [P, NT, 2, 6])
        mean_var = sb("mean_var", [P, NT, 2])
        root = sb("root", [P, NT, 8])
        power = sb("power", [P, 8])
        small = sb("small", [P, 64])
        SLOT = KD * BANK
        slots = [sb(f"panel{i}", [P, SLOT]) for i in range(4)]
        work = sb("work", [P, 91 * 256])

        taken = [0]

        def carve_from(offset):
            taken[0] = offset

        def carve(*free, parts=P, dt=F32):
            n = int(np.prod(free))
            words = n if dt in (F32, I32) else (n + 1) // 2
            lo = taken[0]
            taken[0] += words
            assert taken[0] <= 91 * 256, taken[0] / 256
            v = work[0:parts, lo:lo + words]
            if dt != F32:
                v = v.bitcast(dt)
            if len(free) == 2:
                v = v.rearrange("p (a b) -> p a b", a=free[0])
            if len(free) == 3:
                v = v.rearrange("p (a b c) -> p a b c", a=free[0], b=free[1])
            return v

        setup = p.semaphore("setup_loads")
        norm_sem = p.semaphore("norm_param_loads")
        side_sem = p.semaphore("side_loads")
        out_sem = p.semaphore("stores")

        slot_sems = {}
        panels = Pool_([])

        def add_slot(name, slot, free=None):
            slot_sems[id(slot)] = p.semaphore(f"panel_{name}_landed")
            panels.give(slot, free)

        for i, s in enumerate(slots):
            add_slot(str(i), s)

        class Panel:

            def __init__(self, *parts):
                self.slot, before = panels.take()
                self.views, at = [], 0
                for w, k in parts:
                    t, n = k // P, w.shape[-1]
                    v = self.slot[:, at:at + t * n].rearrange("p (t n) -> p t n", t=t)
                    self.landed = p.dma("sync", slot_sems[id(self.slot)], v,
                                        w.rearrange("(t p) n -> p t n", p=P), before)
                    self.views.append(v)
                    at += t * n
                self.w = self.views[0]

            def release(self, after):
                panels.give(self.slot, after)

        def panel(w, k0, k1, c0, c1):
            return Panel((w[k0:k1, c0:c1], k1 - k0))

        def product_T(bank, w, c0, m, rhs, kt, n=S, row=0):
            def make(e):
                for k in range(kt):
                    ins = e.matmul(bank[row:row + m, 0:n], w[:, k, c0:c0 + m], rhs(k),
                                   start=(k == 0), stop=(k == kt - 1))
                return ins
            return make

        def product_tok(bank, w, lhs, kt, c0=0, n=BANK, first=True, last=True):
            def make(e):
                for k in range(kt):
                    ins = e.matmul(bank[:, 0:n], lhs(k), w[:, k, c0:c0 + n],
                                   start=(first and k == 0), stop=(last and k == kt - 1))
                return ins
            return make

        def tok_of(t, i):
            return lambda k: t[:, k, i * P:(i + 1) * P]

        flip = [0]

        def evacuate(dst, src, *waits, engines=("scalar", "vector")):
            flip[0] += 1
            name = engines[flip[0] % len(engines)]
            if name == "scalar":
                return p.act(lambda e: e.activation(dst, src, ACT.Copy), *waits)
            return p.dve(lambda e: e.tensor_copy(dst, src), *waits)

        def transposed(src_of, dst_of, n_blocks, *waits, engines=("scalar", "vector"), before=None):
            toks = []
            for b in range(0, n_blocks, 4):
                m = min(4, n_blocks - b)
                bank, bank_free = banks.take()

                def make(e, b=b, m=m, bank=bank):
                    for j in range(m):
                        ins = e.transpose(bank[:, j * P:(j + 1) * P], src_of(b + j), ident[:, :])
                    return ins
                t = p.pe(make, bank_free, *waits)
                c = evacuate(dst_of(b, m), bank[:, 0:m * P].rearrange("p (j c) -> p j c", j=m), t, before,
                             engines=engines)
                banks.give(bank, c)
                toks.append(c)
            return toks

        def rows_to_T(i, *waits, src=None, dst=None, engines=("scalar",), before=None):
            src, dst = (x_tok if src is None else src), (xT if dst is None else dst)
            return transposed(lambda k: src[:, i, k * P:(k + 1) * P],
                              lambda b, m: dst[:, b:b + m, i * P:(i + 1) * P],
                              src.shape[2] // P, *waits, engines=engines, before=before)

        def inverse_root(i, n, var, scale, eps, *waits):
            t = p.dve(lambda e: e.tensor_scalar(root[:, i, 0:n], var, scale, eps, ALU.mult, ALU.add), *waits)
            return p.pool(lambda e: e.tensor_tensor(root[:, i, 0:n], root[:, i, 0:n], power[:, 0:n], ALU.pow), t, t_power)

        state = {"x": [None] * NT, "xT": [None] * NT, "norm_free": None, "xT_free": None}

        def load_norm(g, b):
            t = p.dma("scalar", norm_sem, gain[:, :], g.partition_broadcast(P), state["norm_free"])
            if b is not None:
                t = p.dma("scalar", norm_sem, shift[:, :], b.partition_broadcast(P))
            return t

        def residual_norm(i, halves, loaded):
            t = []
            for n, (bank, ready) in enumerate(halves):
                xs = x_tok[:, i, n * BANK:(n + 1) * BANK]
                c = p.dve(lambda e, xs=xs, bank=bank: e.scalar_tensor_tensor(
                    out=xs, in0=xs, scalar=ALPHA, in1=bank[:, :], op0=ALU.mult, op1=ALU.add), ready, state["x"][i])
                banks.give(bank, c)
                t.append(c)
            for n in range(2):
                c = p.dve(lambda e, n=n: e.bn_stats(stat[:, i, n, :], x_tok[:, i, n * BANK:(n + 1) * BANK]), t[n])
            c = p.dve(lambda e: e.bn_aggr(mean_var[:, i, :], stat[:, i, :, :].rearrange("p a b -> p (a b)")), c)
            r = inverse_root(i, 1, mean_var[:, i, 1:2], 1.0, LN_EPS, c)
            x = x_tok[:, i, :]
            c = p.dve(lambda e: e.tensor_scalar(x, x, mean_var[:, i, 0:1], root[:, i, 0:1],
                                                ALU.subtract, ALU.mult), r)
            c = p.dve(lambda e: e.tensor_tensor(x, x, gain[:, :], ALU.mult), c, loaded)
            c = p.dve(lambda e: e.tensor_tensor(x, x, shift[:, :], ALU.add), c)
            state["x"][i] = c
            state["norm_free"] = c

        def project_out(w, kt, lhs, lhs_ready, norm, between=None):
            loaded = load_norm(*norm)
            open_ = {}
            for half in range(2):
                for k0 in range(0, kt, KD):
                    k1 = min(k0 + KD, kt)
                    pn = panel(w, k0 * P, k1 * P, half * BANK, (half + 1) * BANK)
                    for i in range(NT):
                        if k0 == 0:
                            open_[half, i] = banks.take()
                        bank, bank_free = open_[half, i]
                        t = p.pe(product_tok(bank, pn.w, lambda k, i=i, k0=k0: lhs(k0 + k, i), k1 - k0,
                                             first=(k0 == 0), last=(k1 == kt)),
                                 pn.landed, bank_free, lhs_ready)
                        open_[half, i] = (bank, t)
                        if half == 1 and k1 == kt:
                            residual_norm(i, [open_[0, i], open_[1, i]], loaded)
                    pn.release(t)
            last_read = t
            if between:
                between()
            for i in range(NT):
                state["xT"][i] = rows_to_T(i, state["x"][i], before=last_read)

        p.stage("setup")
        for dst, src in ((ident, a["c_ident"]), (swap_a, a["c_swap_a"]), (swap_q, a["c_swap_q"]),
                         (cols, a["cols"])):
            t_setup = p.dma("scalar", setup, dst[:, :], src)
        t_power = p.pool(lambda e: e.memset(power[:, :], -0.5))
        t_setup = p.dma("scalar", setup, x_tok[:, :, :], a["x"][0].rearrange("(t p) d -> p t d", p=P))
        carve_from(0)
        mem_tok = carve(MT, D)
        angle = carve(S, parts=QKD)
        turns = carve(S, parts=QKD)
        pos_i = carve(S, parts=QKD, dt=I32)
        freq = carve(1, parts=QKD)
        t_setup = p.dma("scalar", setup, mem_tok, a["mem"][0].rearrange("(t p) d -> p t d", p=P))
        t_setup = p.dma("scalar", setup, pos_i, a["positions"][0].partition_broadcast(QKD))
        t_setup = p.dma("scalar", setup, freq, a["c_freq"])

        carve_from(91 * 256 - 2 * S - S)
        cos_q = carve(S, parts=QKD)
        sin_q = carve(S, parts=QKD)
        mask_q = carve(S)
        ROPE_AT = 91 * 256 - 3 * S
        t_setup = p.dma("scalar", setup, mask_q, a["c_mask_q"])

        for m in range(MT):
            t_mem = transposed(lambda k, m=m: mem_tok[:, m, k * P:(k + 1) * P],
                               lambda b, n, m=m: memT[:, b:b + n, m * P:(m + 1) * P], KD, t_setup)
        for i in range(NT):
            state["xT"][i] = rows_to_T(i, t_setup)
            state["x"][i] = t_setup

        TWO_PI = 2.0 * np.pi
        PI_1 = 6.28125
        PI_2 = float(np.float32(np.round((TWO_PI - PI_1) * 2 ** 21) / 2 ** 21))
        PI_3 = float(TWO_PI - PI_1 - PI_2)
        MAGIC = 1.5 * 2 ** 23
        EDGE = 3.1415925
        t = p.dve(lambda e: e.tensor_copy(angle, pos_i), t_setup)
        t = p.dve(lambda e: e.tensor_scalar(angle, angle, freq, None, ALU.mult), t)
        t = p.dve(lambda e: e.tensor_scalar(turns, angle, 1.0 / TWO_PI, MAGIC, ALU.mult, ALU.add), t)
        t = p.dve(lambda e: e.tensor_scalar(turns, turns, MAGIC, None, ALU.subtract), t)
        for part in (PI_1, PI_2, PI_3):
            t = p.dve(lambda e, part=part: e.scalar_tensor_tensor(
                out=angle, in0=turns, scalar=-part, in1=angle, op0=ALU.mult, op1=ALU.add), t)
        t = p.dve(lambda e: e.tensor_scalar(sin_q, angle, EDGE, -EDGE, ALU.min, ALU.max), t)
        t_s = p.act(lambda e: e.activation(sin_q, sin_q, ACT.Sin), t)
        t = p.dve(lambda e: e.tensor_scalar(angle, angle, float(np.pi / 2), None, ALU.add), t)
        t = p.dve(lambda e: e.tensor_scalar(turns, angle, float(np.pi), -TWO_PI, ALU.is_gt, ALU.mult), t)
        t = p.dve(lambda e: e.tensor_tensor(angle, angle, turns, ALU.add), t)
        t = p.dve(lambda e: e.tensor_scalar(cos_q, angle, EDGE, -EDGE, ALU.min, ALU.max), t)
        t_rope = [t_s, p.act(lambda e: e.activation(cos_q, cos_q, ACT.Sin), t)]
        work_free = [t, t_rope[1]] + t_mem

        def first_block_layer(layer, work_free):
            p.stage(f"mixer{layer}")
            col = lambda c, n=1, lo=0, hi=P: cols[lo:hi, layer * PC_LAYER + c:layer * PC_LAYER + c + n]
            carve_from(0)
            c_tok = carve(NT, 2 * RANK)
            cT = carve(4, S)
            k_ropeT = carve(S, parts=QKD)
            v_tok = carve(NT, HEADS * VDIM)
            gate_acc = carve(CT, S)
            PAD = TAPS - 1
            hT = carve(CT, PAD + S)
            yT = carve(KD, S)
            heads_q = Pool_([carve(S, parts=QKD) for _ in range(2)])
            heads_k = Pool_([carve(S, parts=QKD) for _ in range(2)])
            raws = Pool_([carve(S, parts=QKD) for _ in range(2)])
            probs = Pool_([carve(S) for _ in range(3)])
            probsT = Pool_([carve(NT, P) for _ in range(3)])
            bias_c = probsT.free[0][0].rearrange("p a b -> p (a b)")
            kr_w = probs.free[0][0].rearrange("p (t n) -> p t n", t=KD)[:, :, 0:ROPE]
            assert taken[0] <= ROPE_AT, taken[0] / 256
            w_in, b_in = a["mix_w_in"][layer], a["mix_b_in"][layer]

            t_bias = p.dma("scalar", side_sem, bias_c, b_in[0:BANK].partition_broadcast(P), work_free)
            t_bias = p.dma("scalar", side_sem, kr_w,
                           w_in[:, BANK:BANK + ROPE].rearrange("(t p) n -> p t n", p=P))

            pn = panel(w_in, 0, D, 0, BANK)
            t_c = []
            for i in range(NT):
                bank, bank_free = banks.take()
                t = p.pe(product_tok(bank, pn.w, tok_of(xT, i), KD), pn.landed, bank_free, state["xT"][i])
                row = c_tok[:, i, :]
                c = p.dve(lambda e, row=row, bank=bank: e.tensor_tensor(row, bank[:, :], bias_c, ALU.add),
                          t, t_bias, work_free)
                banks.give(bank, c)
                for n in range(2):
                    bank, bank_free = banks.take()
                    q = p.act(lambda e, i=i, n=n, bank=bank: e.activation(
                        bank[:, 0:RANK], c_tok[:, i, n * RANK:(n + 1) * RANK], ACT.Square,
                        accum_out=small[:, i * 2 + n:i * 2 + n + 1]), c, bank_free)
                    banks.give(bank, q)
                r = inverse_root(i, 2, small[:, i * 2:i * 2 + 2], 1.0 / RANK, RMS_EPS, q)
                for n in range(2):
                    c = p.dve(lambda e, i=i, n=n: e.tensor_scalar(
                        c_tok[:, i, n * RANK:(n + 1) * RANK], c_tok[:, i, n * RANK:(n + 1) * RANK],
                        root[:, i, n:n + 1], None, ALU.mult), r)
                t_c.append(c)
            pn.release(t)

            bank, bank_free = banks.take()
            t = p.pe(product_T(bank, kr_w, 0, ROPE, lambda k: xT[:, k, :], KD, row=NOPE),
                     t_bias, bank_free, state["xT"])
            kr = k_ropeT[NOPE:QKD, :]
            c = p.act(lambda e, bank=bank: e.activation(kr, bank[NOPE:QKD, :], ACT.Identity,
                                                        bias=col(PC_KR, 1, NOPE, QKD)), t, work_free)
            banks.give(bank, c)
            bank, bank_free = banks.take()
            t = p.pe(lambda e, bank=bank: e.matmul(bank[NOPE:QKD, :], swap_q[NOPE:QKD, NOPE:QKD], kr,
                                                   start=True, stop=True), c, bank_free)
            raw_k, raw_free = raws.take()
            t1 = p.dve(lambda e, bank=bank, r=raw_k: e.tensor_tensor(r[NOPE:QKD, :], bank[NOPE:QKD, :],
                                                                     sin_q[NOPE:QKD, :], ALU.mult),
                       t, raw_free, t_rope)
            banks.give(bank, t1)
            t2 = p.dve(lambda e: e.tensor_tensor(kr, kr, cos_q[NOPE:QKD, :], ALU.mult), t, t1)
            t_kr = p.dve(lambda e, r=raw_k: e.tensor_tensor(kr, kr, r[NOPE:QKD, :], ALU.add), t2)
            raws.give(raw_k, t_kr)
            probs.free[0] = (probs.free[0][0], t)
            probsT.free[0] = (probsT.free[0][0], t_c[-1])

            zero = p.pool(lambda e: e.memset(hT[:, :, 0:PAD], 0.0), work_free)
            U0 = BANK + ROPE
            pg, pa = panel(w_in, 0, D, U0 + CONV, U0 + 2 * CONV), panel(w_in, 0, D, U0, U0 + CONV)
            t_g = []
            for c4 in range(CT):
                bank, bank_free = banks.take()
                t = p.pe(product_T(bank, pg.w, c4 * P, P, lambda k: xT[:, k, :], KD),
                         pg.landed, bank_free, state["xT"])
                c = p.act(lambda e, c4=c4, bank=bank: e.activation(
                    gate_acc[:, c4, :], bank[:, :], ACT.Sigmoid, bias=col(PC_UG + c4)), t, work_free)
                banks.give(bank, c)
                t_g.append(c)
            pg.release(t)
            t_h = []
            for c4 in range(CT):
                bank, bank_free = banks.take()
                t = p.pe(product_T(bank, pa.w, c4 * P, P, lambda k: xT[:, k, :], KD), pa.landed, bank_free)
                c = p.dve(lambda e, c4=c4, bank=bank: e.scalar_tensor_tensor(
                    out=hT[:, c4, PAD:PAD + S], in0=bank[:, :], scalar=col(PC_UA + c4),
                    in1=gate_acc[:, c4, :], op0=ALU.add, op1=ALU.mult), t, t_g[c4], work_free)
                banks.give(bank, c)
                t_h.append(c)
            pa.release(t)
            x_read = t

            t_cT = []
            for k in range(4):
                bank, bank_free = banks.take()

                def make(e, k=k, bank=bank):
                    for i in range(NT):
                        ins = e.transpose(bank[:, i * P:(i + 1) * P], c_tok[:, i, k * P:(k + 1) * P], ident[:, :])
                    return ins
                t = p.pe(make, bank_free, t_c)
                c = p.act(lambda e, k=k, bank=bank: e.activation(cT[:, k, :], bank[:, :], ACT.Copy,
                                                                 scale=col(PC_QN + k)), t, work_free)
                banks.give(bank, c)
                t_cT.append(c)
            c_read = t

            conv = []
            t_acc = [None] * CT
            for j in range(TAPS):
                for c4 in range(CT):
                    conv.append((j, c4))

            def convolve(n):
                for _ in range(min(n, len(conv))):
                    j, c4 = conv.pop(0)
                    src, acc, w = hT[:, c4, j:j + S], gate_acc[:, c4, :], col(PC_W + c4 * TAPS + j)
                    if j == 0:
                        t_acc[c4] = p.dve(lambda e, src=src, acc=acc, w=w, c4=c4: e.tensor_scalar(
                            acc, src, w, col(PC_DWB + c4), ALU.mult, ALU.add), t_h[c4], zero)
                    else:
                        t_acc[c4] = p.dve(lambda e, src=src, acc=acc, w=w: e.scalar_tensor_tensor(
                            out=acc, in0=src, scalar=w, in1=acc, op0=ALU.mult, op1=ALU.add), t_acc[c4])

            uq = Panel((a["mla_w_uq"][layer], RANK), (a["mla_w_ukv"][layer], RANK))
            w_q, w_kv = uq.views
            for i in range(NT):
                bank, bank_free = banks.take()

                def make(e, i=i, bank=bank):
                    for k in range(2):
                        ins = e.matmul(bank[:, :], cT[:, 2 + k, i * P:(i + 1) * P],
                                       w_kv[:, k, :].rearrange("p (h two d) -> p h two d", two=2, d=VDIM)[:, :, 1, :],
                                       start=(k == 0), stop=(k == 1))
                    return ins
                t = p.pe(make, uq.landed, bank_free, t_cT)
                t_v = evacuate(v_tok[:, i, :], bank[:, :], t, work_free, engines=("scalar",))
                banks.give(bank, t_v)

            def head_qk(h):
                q, q_free = heads_q.take()
                k_, k_free = heads_k.take()
                raw, raw_free = raws.take()
                bank, bank_free = banks.take()
                t = p.pe(lambda e: product_T(bank, w_q, h * QKD, QKD, lambda k: cT[:, k, :], 2)(e),
                         uq.landed, bank_free, t_cT)
                c = p.act(lambda e: e.activation(raw, bank[0:QKD, :], ACT.Copy), t, raw_free)
                banks.give(bank, c)
                bank2, bank_free = banks.take()
                t = p.pe(lambda e: e.matmul(bank2[0:QKD, :], swap_q[:, :], raw, start=True, stop=True), c, bank_free)
                t1 = p.dve(lambda e: e.tensor_tensor(q, bank2[0:QKD, :], sin_q, ALU.mult), t, q_free)
                banks.give(bank2, t1)
                t2 = p.pool(lambda e: e.tensor_tensor(raw, raw, cos_q, ALU.mult), t)
                t_q = p.dve(lambda e: e.tensor_tensor(q, q, raw, ALU.add), t1, t2)
                raws.give(raw, t_q)
                bank3, bank_free = banks.take()
                t = p.pe(lambda e: product_T(bank3, w_kv, h * 2 * NOPE, NOPE, lambda k: cT[:, 2 + k, :], 2)(e),
                         bank_free)
                c = p.act(lambda e: e.activation(k_[0:NOPE, :], bank3[0:NOPE, :], ACT.Copy), t, k_free)
                banks.give(bank3, c)
                c2 = p.pool(lambda e: e.tensor_copy(k_[NOPE:QKD, :], kr), t_kr, k_free)
                return q, k_, [t_q, c, c2], t

            steps = [(h, i) for h in range(HEADS) for i in range(NT)]
            qk, live, acc_bank = {}, {}, {}
            t_y = []
            for n in range(len(steps) + 4):
                if n < len(steps):
                    h, i = steps[n]
                    if i == 0:
                        qk[h] = head_qk(h)
                    q, k_, ready, uq_read = qk[h]
                    end = (i + 1) * P
                    bank, bank_free = banks.take()
                    t = p.pe(lambda e, bank=bank, q=q, k_=k_, i=i, end=end: e.matmul(
                        bank[:, 0:end], q[:, i * P:end], k_[:, 0:end], start=True, stop=True), ready, bank_free)
                    if i == NT - 1:
                        heads_q.give(q, t)
                        heads_k.give(k_, t)
                    pr, pr_free = probs.take()
                    st = small[:, 8 + 4 * (n % 4):12 + 4 * (n % 4)]
                    c = p.dve(lambda e, pr=pr, bank=bank, end=end, st=st: e.tensor_tensor_reduce(
                        out=pr[:, 0:end], in0=bank[:, 0:end], in1=mask_q[:, S - end:S], scale=1.0, scalar=NEG,
                        op0=ALU.add, op1=ALU.max, accum_out=st[:, 0:1]), t, pr_free)
                    banks.give(bank, c)
                    c = p.dve(lambda e, st=st: e.tensor_scalar(st[:, 1:2], st[:, 0:1], -(QKD ** -0.5), None,
                                                               ALU.mult), c)
                    c = p.act(lambda e, pr=pr, end=end, st=st: e.activation(
                        pr[:, 0:end], pr[:, 0:end], ACT.Exp, bias=st[:, 1:2], scale=QKD ** -0.5,
                        accum_out=st[:, 2:3]), c)
                    live[n] = [pr, st, c]
                if 1 <= n <= len(steps):
                    h, i = steps[n - 1]
                    end = (i + 1) * P
                    pr, st, c = live[n - 1]
                    c = p.dve(lambda e, st=st: e.reciprocal(st[:, 3:4], st[:, 2:3]), c)
                    c = p.dve(lambda e, pr=pr, st=st, end=end: e.tensor_scalar(
                        pr[:, 0:end], pr[:, 0:end], st[:, 3:4], None, ALU.mult), c)
                    live[n - 1][2] = c
                if 2 <= n <= len(steps) + 1:
                    h, i = steps[n - 2]
                    pr, st, c = live[n - 2]
                    bank, bank_free = banks.take()
                    pt, pt_free = probsT.take()

                    def make(e, pr=pr, bank=bank, i=i):
                        for j in range(i + 1):
                            ins = e.transpose(bank[:, j * P:(j + 1) * P], pr[:, j * P:(j + 1) * P], ident[:, :])
                        return ins
                    t = p.pe(make, c, bank_free)
                    probs.give(pr, t)
                    c = p.act(lambda e, pt=pt, bank=bank, i=i: e.activation(
                        pt[:, 0:i + 1, :], bank[:, 0:(i + 1) * P].rearrange("p (j c) -> p j c", c=P), ACT.Copy),
                        t, pt_free)
                    banks.give(bank, c)
                    live[n - 2] += [pt, c]
                if 3 <= n <= len(steps) + 2:
                    h, i = steps[n - 3]
                    pt, c = live[n - 3][3:]
                    if i == 0 and h % 2 == 0:
                        acc_bank[h // 2] = banks.take()
                    bank, bank_free = acc_bank[h // 2]
                    row = (h % 2) * VDIM

                    def make(e, pt=pt, i=i, h=h, row=row, bank=bank):
                        for j in range(i + 1):
                            ins = e.matmul(bank[row:row + VDIM, i * P:(i + 1) * P],
                                           v_tok[:, j, h * VDIM:(h + 1) * VDIM], pt[:, j, :],
                                           start=(j == 0), stop=(j == i))
                        return ins
                    t = p.pe(make, c, bank_free, t_v)
                    probsT.give(pt, t)
                    if i == NT - 1 and h % 2 == 1:
                        t_y.append(evacuate(yT[:, h // 2, :], bank[:, :], t, work_free, engines=("scalar",)))
                        banks.give(bank, t_y[-1])
                    del live[n - 3]
                convolve(4)
            convolve(len(conv))
            uq.release(uq_read)

            t_z = []
            for i in range(NT):
                bank, bank_free = banks.take()

                def make(e, i=i, bank=bank):
                    for c4 in range(CT):
                        ins = e.transpose(bank[:, c4 * P:(c4 + 1) * P], gate_acc[:, c4, i * P:(i + 1) * P],
                                          ident[:, :])
                    return ins
                t = p.pe(make, bank_free, t_acc)
                c = p.dve(lambda e, i=i, bank=bank: e.bn_stats(stat[:, i, 0, :], bank[:, :]), t)
                c = p.dve(lambda e, i=i: e.bn_aggr(mean_var[:, i, :], stat[:, i, 0, :]), c)
                r = inverse_root(i, 1, mean_var[:, i, 1:2], 1.0, LN_EPS, c)
                c = p.dve(lambda e, i=i, bank=bank: e.tensor_scalar(
                    c_tok[:, i, :], bank[:, :], mean_var[:, i, 0:1], root[:, i, 0:1], ALU.subtract, ALU.mult),
                    r, c_read)
                banks.give(bank, c)
                t_z.append(c)
            for c4 in range(CT):
                bank, bank_free = banks.take()

                def make(e, c4=c4, bank=bank):
                    for i in range(NT):
                        ins = e.transpose(bank[:, i * P:(i + 1) * P], c_tok[:, i, c4 * P:(c4 + 1) * P], ident[:, :])
                    return ins
                t = p.pe(make, bank_free, t_z)
                c = p.act(lambda e, c4=c4, bank=bank: e.activation(
                    yT[:, CT + c4, :], bank[:, :], ACT.Silu, bias=col(PC_CNB + c4), scale=col(PC_CNG + c4)), t)
                banks.give(bank, c)
                t_y.append(c)

            mixer_end = taken[0]
            carve_from(0)
            mem_kT = carve(KD, MEM)
            mem_v = carve(MT, D)
            xq = None
            w_kv2 = a["xa_w_kv"][layer]
            t_kv = []
            after_attention = [t_y[CT - 1], t_y[-1], t]

            def memory_kv():
                p.stage(f"cross{layer}")
                for n in range(2):
                    pk = panel(w_kv2, 0, D, n * BANK, (n + 1) * BANK)
                    for c4 in range(4):
                        bank, bank_free = banks.take()
                        t = p.pe(product_T(bank, pk.w, c4 * P, P, lambda k: memT[:, k, :], KD, n=MEM),
                                 pk.landed, bank_free, t_mem)
                        t_kv.append(evacuate(mem_kT[:, n * 4 + c4, :], bank[:, 0:MEM], t, after_attention,
                                             engines=("scalar",)))
                        banks.give(bank, t_kv[-1])
                    pk.release(t)
                for n in range(2):
                    pv = panel(w_kv2, 0, D, D + n * BANK, D + (n + 1) * BANK)
                    for m in range(MT):
                        bank, bank_free = banks.take()
                        t = p.pe(product_tok(bank, pv.w, tok_of(memT, m), KD), pv.landed, bank_free)
                        t_kv.append(evacuate(mem_v[:, m, n * BANK:(n + 1) * BANK], bank[:, :], t, after_attention,
                                             engines=("scalar",)))
                        banks.give(bank, t_kv[-1])
                    pv.release(t)

            project_out(a["mix_w_o"][layer], KD, lambda k, i: yT[:, k, i * P:(i + 1) * P], t_y,
                        (a["ln1_g"][layer], a["ln1_b"][layer]), between=memory_kv)
            y_read = state["xT"][-1]

            carve_from(16 * 256)
            qT = carve(KD, S)
            oT = carve(KD, S)
            xprobs = Pool_([carve(MEM) for _ in range(4)])
            xprobsT = Pool_([carve(MT, S) for _ in range(2)])
            assert taken[0] <= ROPE_AT
            t_q = []
            for n in range(2):
                pq = panel(a["xa_w_q"][layer], 0, D, n * BANK, (n + 1) * BANK)
                for c4 in range(4):
                    bank, bank_free = banks.take()
                    t = p.pe(product_T(bank, pq.w, c4 * P, P, lambda k: xT[:, k, :], KD),
                             pq.landed, bank_free, state["xT"])
                    t_q.append(evacuate(qT[:, n * 4 + c4, :], bank[:, :], t, y_read))
                    banks.give(bank, t_q[-1])
                pq.release(t)
            steps = [(h, i) for h in range(XH) for i in range(NT)]
            live, head_T, t_o = {}, {}, []
            for n in range(len(steps) + 3):
                if n < len(steps):
                    h, i = steps[n]
                    bank, bank_free = banks.take()

                    def make(e, h=h, i=i, bank=bank):
                        for k in range(2):
                            ins = e.matmul(bank[:, 0:MEM], qT[:, 2 * h + k, i * P:(i + 1) * P],
                                           mem_kT[:, 2 * h + k, :], start=(k == 0), stop=(k == 1))
                        return ins
                    t = p.pe(make, bank_free, t_q[2 * h:2 * h + 2], t_kv)
                    pr, pr_free = xprobs.take()
                    st = small[:, 24 + 4 * (n % 4):28 + 4 * (n % 4)]
                    c = p.dve(lambda e, bank=bank, st=st: e.tensor_reduce(
                        st[:, 0:1], bank[:, 0:MEM], AX.X, ALU.max), t)
                    c = p.dve(lambda e, st=st: e.tensor_scalar(st[:, 1:2], st[:, 0:1], -(XHD ** -0.5), None,
                                                               ALU.mult), c)
                    c = p.act(lambda e, pr=pr, bank=bank, st=st: e.activation(
                        pr, bank[:, 0:MEM], ACT.Exp, bias=st[:, 1:2], scale=XHD ** -0.5,
                        accum_out=st[:, 2:3]), c, pr_free, y_read)
                    banks.give(bank, c)
                    live[n] = [pr, st, c]
                if 1 <= n <= len(steps):
                    pr, st, c = live[n - 1]
                    c = p.dve(lambda e, st=st: e.reciprocal(st[:, 3:4], st[:, 2:3]), c)
                    c = p.dve(lambda e, pr=pr, st=st: e.tensor_scalar(pr, pr, st[:, 3:4], None, ALU.mult), c)
                    live[n - 1][2] = c
                if 2 <= n <= len(steps) + 1:
                    h, i = steps[n - 2]
                    pr, st, c = live.pop(n - 2)
                    bank, bank_free = banks.take()
                    if i == 0:
                        head_T[h] = [*xprobsT.take(), []]
                    pt, pt_free, written = head_T[h]

                    def make(e, pr=pr, bank=bank):
                        for m in range(MT):
                            ins = e.transpose(bank[:, m * P:(m + 1) * P], pr[:, m * P:(m + 1) * P], ident[:, :])
                        return ins
                    t = p.pe(make, c, bank_free)
                    xprobs.give(pr, t)
                    c = evacuate(pt[:, :, i * P:(i + 1) * P], bank[:, 0:MEM].rearrange("p (m c) -> p m c", m=MT),
                                 t, pt_free)
                    banks.give(bank, c)
                    written.append(c)
                    if i == NT - 1:
                        for v in range(2):
                            bank, bank_free = banks.take()

                            def make(e, h=h, v=v, bank=bank, pt=pt):
                                for m in range(MT):
                                    ins = e.matmul(bank[:, :], mem_v[:, m, h * XHD + v * P:h * XHD + (v + 1) * P],
                                                   pt[:, m, :], start=(m == 0), stop=(m == MT - 1))
                                return ins
                            t = p.pe(make, bank_free, written)
                            t_o.append(evacuate(oT[:, 2 * h + v, :], bank[:, :], t, y_read))
                            banks.give(bank, t_o[-1])
                        xprobsT.give(pt, t)
            project_out(a["xa_w_o"][layer], KD, lambda k, i: oT[:, k, i * P:(i + 1) * P], t_o,
                        (a["ln2_g"][layer], a["ln2_b"][layer]))
            work_free = state["xT"][-1]

            p.stage(f"ffn{layer}")
            carve_from(0)
            hidT = carve(FT, S)
            tmp = Pool_([carve(S) for _ in range(3)])
            w1 = a["ffn_w_in"][layer]
            t_hid = []
            for c0 in range(0, FFN, BANK):
                c1 = min(c0 + BANK, FFN)
                pg, pu = panel(w1, 0, D, c0, c1), panel(w1, 0, D, FFN + c0, FFN + c1)
                for c in range(0, c1 - c0, P):
                    bg, bg_free = banks.take()
                    bu, bu_free = banks.take()
                    tg = p.pe(product_T(bg, pg.w, c, P, lambda k: xT[:, k, :], KD), pg.landed, bg_free, state["xT"])
                    tu = p.pe(product_T(bu, pu.w, c, P, lambda k: xT[:, k, :], KD), pu.landed, bu_free)
                    g, g_free = tmp.take()
                    ta = p.act(lambda e, g=g, bg=bg: e.activation(g, bg[:, :], ACT.Silu), tg, g_free, work_free)
                    dst = hidT[:, (c0 + c) // P, :]
                    tm = p.dve(lambda e, g=g, bu=bu, dst=dst: e.tensor_tensor(dst, g, bu[:, :], ALU.mult),
                               ta, tu, work_free)
                    tmp.give(g, tm)
                    banks.give(bg, ta)
                    banks.give(bu, tm)
                    t_hid.append(tm)
                pg.release(tg)
                pu.release(tu)
            project_out(a["ffn_w_down"][layer], FT, lambda k, i: hidT[:, k, i * P:(i + 1) * P], t_hid,
                        (a["ln3_g"][layer], a["ln3_b"][layer]))
            return state["xT"][-1]

        for layer in range(DEPTH):
            work_free = first_block_layer(layer, work_free)

        w2in = a["w_in_2"][0]
        A_COLS = 3 * NG * AH * AHD
        QR0, KR0 = A_COLS, A_COLS + RH * RQK
        VR0 = KR0 + RH * RQK
        GR0 = VR0 + RH * RV
        GT0 = GR0 + RH * RV

        def rms_rows(i, out_row, loaded, dump, dump_free=None):
            q = p.act(lambda e: e.activation(dump, x_tok[:, i, :], ACT.Square,
                                             accum_out=small[:, 40 + i:41 + i]), state["x"][i], dump_free)
            r = inverse_root(i, 1, small[:, 40 + i:41 + i], 1.0 / D, RMS_EPS, q)
            c = p.dve(lambda e: e.scalar_tensor_tensor(out=out_row, in0=x_tok[:, i, :], scalar=root[:, i, 0:1],
                                                       in1=gain[:, :], op0=ALU.mult, op1=ALU.mult), r, loaded)
            state["norm_free"] = c
            return c

        def dilated_attention(work_free):
            p.stage("attention")
            carve_from(0)
            y_attT = carve(NT, S)
            xTp = carve(KD, S)
            masks = carve(NT * S + 2 * P, dt=BF16)
            cos_a, sin_a = carve(S), carve(S)
            raws = Pool_([carve(S) for _ in range(2)])
            probs = Pool_([carve(6 * P) for _ in range(3)])
            probsT = Pool_([carve(6, P) for _ in range(2)])
            pair_at = taken[0]
            qs = Pool_([carve(NG, S) for _ in range(2)])
            ks = Pool_([carve(NG, S) for _ in range(2)])
            vs = Pool_([carve(NT, NG * P) for _ in range(2)])
            carve_from(pair_at)
            xn_tok = carve(NT, D)
            dump = carve(D)
            loaded = load_norm(a["norm_mix_w_2"][0], None)
            t_const = p.dma("scalar", side_sem, masks.bitcast(mybir.dt.uint16), a["c_mask_a"], work_free)
            t_const = p.dma("scalar", side_sem, cos_a, a["c_cos_a"])
            t_const = p.dma("scalar", side_sem, sin_a, a["c_sin_a"])
            t_x, t_n = [], []
            for i in range(NT):
                n = rms_rows(i, xn_tok[:, i, :], loaded, dump, [work_free, t_n])
                t_n = n
                for b in range(0, KD, 4):
                    bank, bank_free = banks.take()

                    def make(e, b=b, i=i, bank=bank):
                        for j in range(4):
                            ins = e.transpose(bank[:, j * P:(j + 1) * P], xn_tok[:, i, (b + j) * P:(b + j + 1) * P],
                                              ident[:, :])
                        return ins
                    t = p.pe(make, bank_free, n)
                    src = bank[:, :].rearrange("p (j c) -> p j c", j=4)
                    c = p.act(lambda e, src=src, b=b, i=i: e.activation(
                        xT[:, b:b + 4, i * P:(i + 1) * P], src, ACT.Copy), t)
                    c2 = None
                    for j in range(4):
                        dst = xTp[:, b + j, :].rearrange("p (r a) -> p r a", r=DIL)[:, :, i * 32:(i + 1) * 32]
                        sj = bank[:, j * P:(j + 1) * P].rearrange("p (a r) -> p r a", r=DIL)
                        c2 = p.dve(lambda e, dst=dst, sj=sj: e.tensor_copy(dst, sj), c, work_free)
                    banks.give(bank, c2)
                    t_x += [c, c2]
            xn_read = t

            weights = {}

            def rotated(buf, buf_free, g, w, landed):
                bank, bank_free = banks.take()
                t = p.pe(product_T(bank, w, g * P, P, lambda k: xTp[:, k, :], KD), landed, bank_free, t_x)
                raw, raw_free = raws.take()
                c = p.act(lambda e: e.activation(raw, bank[:, :], ACT.Copy), t, raw_free)
                banks.give(bank, c)
                bank2, bank_free = banks.take()
                t2 = p.pe(lambda e: e.matmul(bank2[:, :], swap_a[:, :], raw, start=True, stop=True), c, bank_free)
                t1 = p.dve(lambda e: e.tensor_tensor(buf[:, g, :], bank2[:, :], sin_a, ALU.mult), t2, buf_free, t_const)
                banks.give(bank2, t1)
                m = p.pool(lambda e: e.tensor_tensor(raw, raw, cos_a, ALU.mult), t2, t_const)
                c = p.dve(lambda e: e.tensor_tensor(buf[:, g, :], buf[:, g, :], raw, ALU.add), t1, m)
                raws.give(raw, c)
                return t, c

            ready = {}

            def projections(pair):
                ready[pair] = ([None] * 3, [])
                state_ = {}

                def piece(kind, g):
                    if kind < 2:
                        if g == 0:
                            state_["pn"] = panel(a["w_attn_2"], 0, D, (pair * 3 + kind) * 384,
                                                 (pair * 3 + kind + 1) * 384)
                            ready[pair][0][kind], state_["free"] = (qs, ks)[kind].take()
                        pn, buf, free = state_["pn"], ready[pair][0][kind], state_["free"]
                        t, c = rotated(buf, [free, xn_read], g, pn.w, pn.landed)
                        if g == NG - 1:
                            pn.release(t)
                    else:
                        if g == 0:
                            state_["pn"] = panel(a["w_attn_2"], 0, D, (pair * 3 + 2) * 384, (pair * 3 + 3) * 384)
                            ready[pair][0][2], state_["free"] = vs.take()
                        pn, v, v_free = state_["pn"], ready[pair][0][2], state_["free"]
                        bank, bank_free = banks.take()
                        t = p.pe(product_tok(bank, pn.w, tok_of(xTp, g), KD, n=384), pn.landed, bank_free)
                        c = p.act(lambda e: e.activation(v[:, g, :], bank[:, 0:384], ACT.Copy), t, v_free, xn_read)
                        banks.give(bank, c)
                        if g == NT - 1:
                            pn.release(t)
                    ready[pair][1].append(c)

                return [lambda kind=kind, g=g: piece(kind, g)
                        for kind in range(3) for g in range(NT if kind == 2 else NG)]

            for piece in projections(0):
                piece()
            later = []
            steps = [(pair, hh, r) for pair in range(4) for hh in range(2) for r in range(DIL)]
            live, acc, t_y = {}, {}, []
            for n in range(len(steps) + 4):
                if n < len(steps):
                    pair, hh, r = steps[n]
                    if hh == 0 and r == 0:
                        assert not later
                        later = projections(pair + 1) if pair + 1 < 4 else []
                    (q, k_, v), t_qkv = ready[pair]
                    lo = hh * AHD
                    near, near_free = banks.take()
                    far, far_free = banks.take()

                    def make(e, q=q, k_=k_, r=r, lo=lo, near=near, far=far):
                        mine = slice(r * P, (r + 1) * P)
                        e.matmul(near[:, :], q[lo:lo + AHD, 0, mine], k_[lo:lo + AHD, 0, :], start=True, stop=True)
                        for g in (1, 2):
                            ins = e.matmul(far[:, (g - 1) * P:g * P], q[lo:lo + AHD, g, mine],
                                           k_[lo:lo + AHD, g, mine], start=True, stop=True)
                        return ins
                    t = p.pe(make, t_qkv, near_free, far_free)
                    if hh == 1 and r == DIL - 1:
                        qs.give(q, t)
                        ks.give(k_, t)
                    pr, pr_free = probs.take()
                    st = small[:, 4 * (n % 4):4 * (n % 4) + 4]
                    c = p.dve(lambda e, pr=pr, near=near, r=r, st=st: e.tensor_tensor_reduce(
                        out=pr[:, 0:S], in0=near[:, :], in1=masks[:, r * S:(r + 1) * S], scale=1.0, scalar=NEG,
                        op0=ALU.add, op1=ALU.max, accum_out=st[:, 0:1]), t, pr_free, t_const)
                    banks.give(near, c)
                    c = p.dve(lambda e, pr=pr, far=far, st=st: e.tensor_tensor_reduce(
                        out=pr[:, S:6 * P], in0=far[:, 0:2 * P], in1=masks[:, NT * S:], scale=1.0,
                        scalar=st[:, 0:1], op0=ALU.add, op1=ALU.max, accum_out=st[:, 1:2]), c)
                    banks.give(far, c)
                    c = p.dve(lambda e, st=st: e.tensor_scalar(st[:, 2:3], st[:, 1:2], -(AHD ** -0.5), None,
                                                               ALU.mult), c)
                    c = p.act(lambda e, pr=pr, st=st: e.activation(
                        pr, pr, ACT.Exp, bias=st[:, 2:3], scale=AHD ** -0.5, accum_out=st[:, 3:4]), c)
                    live[n] = [pr, st, c]
                if 1 <= n <= len(steps):
                    pr, st, c = live[n - 1]
                    c = p.dve(lambda e, st=st: e.reciprocal(st[:, 0:1], st[:, 3:4]), c)
                    c = p.dve(lambda e, pr=pr, st=st: e.tensor_scalar(pr, pr, st[:, 0:1], None, ALU.mult), c)
                    live[n - 1][2] = c
                if later:
                    later.pop(0)()
                if 2 <= n <= len(steps) + 1:
                    pr, st, c = live[n - 2]
                    pt, pt_free = probsT.take()
                    got = []
                    for b, m in ((0, 4), (4, 2)):
                        bank, bank_free = banks.take()

                        def make(e, pr=pr, bank=bank, b=b, m=m):
                            for j in range(m):
                                ins = e.transpose(bank[:, j * P:(j + 1) * P], pr[:, (b + j) * P:(b + j + 1) * P],
                                                  ident[:, :])
                            return ins
                        t = p.pe(make, c, bank_free)
                        got.append(p.act(lambda e, pt=pt, bank=bank, b=b, m=m: e.activation(
                            pt[:, b:b + m, :], bank[:, 0:m * P].rearrange("p (j c) -> p j c", j=m), ACT.Copy),
                            t, pt_free))
                        banks.give(bank, got[-1])
                    probs.give(pr, t)
                    live[n - 2] += [pt, got]
                if later and n % 2:
                    later.pop(0)()
                if 3 <= n <= len(steps) + 2:
                    pair, hh, r = steps[n - 3]
                    pt, got = live.pop(n - 3)[3:]
                    v = ready[pair][0][2]
                    if hh == 0 and r == 0:
                        acc[pair] = banks.take()
                    bank, bank_free = acc[pair]
                    lo = hh * AHD

                    def make(e, pt=pt, v=v, r=r, lo=lo, bank=bank):
                        tiles = [(0, 0), (0, 1), (0, 2), (0, 3), (1, r), (2, r)]
                        for j, (g, kt_) in enumerate(tiles):
                            ins = e.matmul(bank[lo:lo + AHD, r * P:(r + 1) * P],
                                           v[:, kt_, g * P + lo:g * P + lo + AHD], pt[:, j, :],
                                           start=(j == 0), stop=(j == 5))
                        return ins
                    t = p.pe(make, got, bank_free)
                    probsT.give(pt, t)
                    if hh == 1 and r == DIL - 1:
                        vs.give(v, t)
                        dst = y_attT[:, pair, :].rearrange("p (a r) -> p r a", r=DIL)
                        c = p.act(lambda e, dst=dst, bank=bank: e.activation(
                            dst, bank[:, :].rearrange("p (r a) -> p r a", r=DIL), ACT.Copy), t, work_free)
                        banks.give(bank, c)
                        t_y.append(c)
            return y_attT, t_y, t_x

        def retention(y_att_at, t_x, work_free):
            p.stage("retention")
            carve_from(y_att_at)
            y_ret = carve(NT, D)
            qr_at = taken[0]
            q_r, k_r = carve(4, S), carve(4, S)
            vr_at = taken[0]
            v_r = carve(NT, D)
            weigh = carve(NT, S)
            WIDE = S + (NT - 1) * P
            ahead, behind, twice = (carve(WIDE, dt=F16) for _ in range(3))
            tables = Pool_([carve(WIDE) for _ in range(2)])
            raws = Pool_([weigh[:, j, :] for j in range(2)])
            cos_r, sin_r = weigh[:, 2, :], weigh[:, 3, :]
            lg = small[:, 44:60]

            t_const = p.dma("scalar", side_sem, ahead, a["c_ahead"], work_free)
            for dst, src in ((behind, a["c_behind"]), (twice, a["c_twice"]), (cos_r, a["c_cos_r"]),
                             (sin_r, a["c_sin_r"])):
                t_const = p.dma("scalar", side_sem, dst, src)
            t_const = t_dec = p.dma("scalar", side_sem, root[:, 0:2, :], a["decays"].partition_broadcast(P), work_free)
            loaded = load_norm(a["ret_gn_w_2"][0], None)

            d_ = root[:, 0:2, :].rearrange("p a b -> p (a b)")
            sc = tables.free[0][0]
            y_, u_, l_, e_, m_ = (sc[:, j * 16:(j + 1) * 16] for j in range(5))
            t = p.dve(lambda e: e.scalar_tensor_tensor(out=y_, in0=d_, scalar=-1.0, in1=d_, op0=ALU.mult, op1=ALU.min), t_dec, work_free)
            t = p.act(lambda e: e.activation(y_, y_, ACT.Exp), t)
            t = p.dve(lambda e: e.tensor_scalar(u_, y_, 1.0, None, ALU.add), t)
            tl = p.act(lambda e: e.activation(l_, u_, ACT.Ln), t)
            t = p.dve(lambda e: e.tensor_scalar(e_, u_, 1.0, None, ALU.is_equal), t)
            t = p.dve(lambda e: e.scalar_tensor_tensor(out=m_, in0=u_, scalar=-1.0, in1=e_, op0=ALU.add,
                                                       op1=ALU.add), t)
            t = p.dve(lambda e: e.reciprocal(m_, m_), t)
            t = p.dve(lambda e: e.tensor_tensor(l_, l_, e_, ALU.add), t, tl)
            t = p.dve(lambda e: e.tensor_tensor(l_, l_, m_, ALU.mult), t)
            t = p.dve(lambda e: e.tensor_tensor(l_, l_, y_, ALU.mult), t)
            t_lg = p.dve(lambda e: e.scalar_tensor_tensor(out=lg, in0=d_, scalar=0.0, in1=l_, op0=ALU.min,
                                                          op1=ALU.subtract), t)
            tables.free[0] = (sc, t_lg)

            t_yr = {}
            for n in range(2):
                pn = panel(w2in, 0, D, GR0 + n * BANK, GR0 + (n + 1) * BANK)
                for i in range(NT):
                    bank, bank_free = banks.take()
                    t = p.pe(product_tok(bank, pn.w, tok_of(xT, i), KD), pn.landed, bank_free, t_x)
                    dst = y_ret[:, i, n * BANK:(n + 1) * BANK]
                    c = p.act(lambda e, dst=dst, bank=bank: e.activation(dst, bank[:, :], ACT.Silu), t, work_free)
                    banks.give(bank, c)
                    t_yr[i, n] = p.dve(lambda e, dst=dst, n=n: e.tensor_tensor(
                        dst, dst, gain[:, n * BANK:(n + 1) * BANK], ALU.mult), c, loaded)
                pn.release(t)
            state["norm_free"] = t_yr[NT - 1, 1]
            t_qk = []
            for c0, buf in ((QR0, q_r), (KR0, k_r)):
                pn = panel(w2in, 0, D, c0, c0 + BANK)
                for c4 in range(4):
                    bank, bank_free = banks.take()
                    t = p.pe(product_T(bank, pn.w, c4 * P, P, lambda k: xT[:, k, :], KD), pn.landed, bank_free)
                    raw, raw_free = raws.take()
                    c = p.act(lambda e, raw=raw, bank=bank: e.activation(raw, bank[:, :], ACT.Copy), t, raw_free,
                              work_free)
                    banks.give(bank, c)
                    bank2, bank_free = banks.take()
                    t2 = p.pe(lambda e, raw=raw, bank2=bank2: e.matmul(bank2[:, :], swap_a[:, :], raw, start=True,
                                                                      stop=True), c, bank_free)
                    t1 = p.dve(lambda e, dst=buf[:, c4, :], bank2=bank2: e.tensor_tensor(
                        dst, bank2[:, :], sin_r, ALU.mult), t2, work_free, t_const)
                    banks.give(bank2, t1)
                    m = p.pool(lambda e, raw=raw: e.tensor_tensor(raw, raw, cos_r, ALU.mult), t2, t_const)
                    c = p.dve(lambda e, dst=buf[:, c4, :], raw=raw: e.tensor_tensor(dst, dst, raw, ALU.add), t1, m)
                    raws.give(raw, c)
                    t_qk.append(c)
                pn.release(t)
            t_v = []
            for n in range(2):
                pn = panel(w2in, 0, D, VR0 + n * BANK, VR0 + (n + 1) * BANK)
                for i in range(NT):
                    bank, bank_free = banks.take()
                    t = p.pe(product_tok(bank, pn.w, tok_of(xT, i), KD), pn.landed, bank_free)
                    t_v.append(p.act(lambda e, i=i, n=n, bank=bank: e.activation(
                        v_r[:, i, n * BANK:(n + 1) * BANK], bank[:, :], ACT.Copy), t, work_free))
                    banks.give(bank, t_v[-1])
                pn.release(t)

            def decay_table(h):
                tab, tab_free = tables.take()
                t = p.dve(lambda e: e.tensor_scalar(tab, behind, lg[:, 8 + h:9 + h], None, ALU.mult),
                          tab_free, t_const, t_lg)
                t = p.dve(lambda e: e.scalar_tensor_tensor(out=tab, in0=ahead, scalar=lg[:, h:h + 1], in1=tab,
                                                           op0=ALU.mult, op1=ALU.add), t)
                t = p.act(lambda e: e.activation(tab, tab, ACT.Exp), t)
                return tab, p.dve(lambda e: e.tensor_tensor(tab, tab, twice, ALU.mult), t)

            t_weigh, t_out = [None] * NT, []
            nxt = decay_table(0)
            for h in range(RH):
                lo = (h % 2) * RQK
                tab, t_tab = nxt
                got = []
                for j in range(NT):
                    bank, bank_free = banks.take()
                    t = p.pe(lambda e, j=j, h=h, lo=lo, bank=bank: e.matmul(
                        bank[:, :], k_r[lo:lo + RQK, h // 2, j * P:(j + 1) * P], q_r[lo:lo + RQK, h // 2, :],
                        start=True, stop=True), bank_free, t_qk)
                    at = (NT - 1 - j) * P
                    c = p.dve(lambda e, j=j, at=at, bank=bank, tab=tab: e.tensor_tensor(
                        weigh[:, j, :], bank[:, :], tab[:, at:at + S], ALU.mult), t, t_tab, t_weigh[j], t_qk)
                    banks.give(bank, c)
                    got.append(c)
                tables.give(tab, c)
                if h + 1 < RH:
                    nxt = decay_table(h + 1)
                bank, bank_free = banks.take()
                for i in range(NT):
                    def make(e, i=i, h=h, bank=bank):
                        for j in range(NT):
                            ins = e.matmul(bank[:, i * P:(i + 1) * P], weigh[:, j, i * P:(i + 1) * P],
                                           v_r[:, j, h * RV:(h + 1) * RV], start=(j == 0), stop=(j == NT - 1))
                        return ins
                    t = p.pe(make, got, bank_free, t_v)
                t_weigh = [t] * NT
                for i in range(NT):
                    c = p.dve(lambda e, i=i, bank=bank: e.bn_stats(stat[:, i, 0, :], bank[:, i * P:(i + 1) * P]), t)
                    c = p.dve(lambda e, i=i: e.bn_aggr(mean_var[:, i, :], stat[:, i, 0, :]), c)
                rt = root[:, h % 4, 0:NT]
                c = p.dve(lambda e, rt=rt: e.tensor_scalar(rt, mean_var[:, :, 1], RMS_EPS, None, ALU.add), c, t_lg)
                r_ = p.pool(lambda e, rt=rt: e.tensor_tensor(rt, rt, power[:, 0:NT], ALU.pow), c)
                for i in range(NT):
                    dst = y_ret[:, i, h * RV:(h + 1) * RV]
                    c = p.dve(lambda e, i=i, dst=dst, bank=bank: e.scalar_tensor_tensor(
                        out=dst, in0=bank[:, i * P:(i + 1) * P], scalar=mean_var[:, i, 0:1], in1=dst,
                        op0=ALU.subtract, op1=ALU.mult), t_yr[i, h // 4], t)
                    c = p.dve(lambda e, i=i, dst=dst, rt=rt: e.tensor_scalar(dst, dst, rt[:, i:i + 1], None,
                                                                            ALU.mult), c, r_)
                banks.give(bank, c)
                t_out.append(c)
            carve_from(vr_at)
            y_retT = carve(KD, S)
            t_T = []
            for i in range(NT):
                t_T += rows_to_T(i, t_out, src=y_ret, dst=y_retT, before=[t_weigh], engines=("scalar", "vector"))
            return y_retT, t_T, qr_at

        def merge(y_attT, t_att, y_retT, t_ret, merged_at, t_x):
            p.stage("merge")
            carve_from(merged_at)
            mT = carve(KD, S)
            carve_from(merged_at + 2 * NT * S + KD * S)
            gates = Pool_([carve(S) for _ in range(4)])
            t_m = []
            for n in range(2):
                pga = panel(w2in, 0, D, GT0 + n * BANK, GT0 + (n + 1) * BANK)
                pgr = panel(w2in, 0, D, GT0 + D + n * BANK, GT0 + D + (n + 1) * BANK)
                pa = panel(a["w_attn_branch_2"][0], 0, NT * P, n * BANK, (n + 1) * BANK)
                pr = panel(a["w_ret_branch_2"][0], 0, D, n * BANK, (n + 1) * BANK)
                for c4 in range(4):
                    done = []
                    for pg, pw, yT_, ty, kt_, gc in ((pga, pa, y_attT, t_att, NT, 0), (pgr, pr, y_retT, t_ret, KD, KD)):
                        bg, bg_free = banks.take()
                        t = p.pe(product_T(bg, pg.w, c4 * P, P, lambda k: xT[:, k, :], KD), pg.landed, bg_free, t_x)
                        g, g_free = gates.take()
                        bias = cols[:, PC_GATE + gc + n * 4 + c4:PC_GATE + gc + n * 4 + c4 + 1]
                        ta = p.act(lambda e, g=g, bg=bg, bias=bias: e.activation(g, bg[:, :], ACT.Sigmoid, bias=bias),
                                   t, g_free, t_ret)
                        banks.give(bg, ta)
                        bw, bw_free = banks.take()
                        t = p.pe(product_T(bw, pw.w, c4 * P, P, lambda k, y=yT_: y[:, k, :], kt_),
                                 pw.landed, bw_free, ty)
                        c = p.dve(lambda e, g=g, bw=bw: e.tensor_tensor(g, g, bw[:, :], ALU.mult), ta, t)
                        banks.give(bw, c)
                        done.append((g, c, t))
                    (g0, c0, _), (g1, c1, t) = done
                    dst = mT[:, n * 4 + c4, :]
                    c = p.dve(lambda e, dst=dst, g0=g0, g1=g1: e.tensor_tensor(dst, g0, g1, ALU.add), c0, c1)
                    gates.give(g0, c)
                    gates.give(g1, c)
                    t_m.append(c)
                for pn in (pga, pgr, pa, pr):
                    pn.release(t)
            for n in range(2):
                pn = panel(a["w_out_2"][0], 0, D, n * BANK, (n + 1) * BANK)
                for i in range(NT):
                    bank, bank_free = banks.take()
                    t = p.pe(product_tok(bank, pn.w, tok_of(mT, i), KD), pn.landed, bank_free, t_m)
                    xs = x_tok[:, i, n * BANK:(n + 1) * BANK]
                    c = p.dve(lambda e, xs=xs, bank=bank: e.tensor_tensor(xs, xs, bank[:, :], ALU.add), t,
                              state["x"][i])
                    banks.give(bank, c)
                    if n == 1:
                        state["x"][i] = c
                pn.release(t)
            return t

        def experts(work_free):
            p.stage("router")
            carve_from(0)
            hn = carve(NT, D)
            tri, ones = carve(P), carve(P)
            router_w = carve(KD, GROUPS + EXPERTS)
            router_b = carve(GROUPS + EXPERTS)
            down8, iota64 = carve(8), carve(EXPERTS)
            logits = carve(NT, GROUPS + EXPERTS)
            g8, s8, t8, oh_g = (carve(NT, 8) for _ in range(4))
            ohs = [carve(NT, 8) for _ in range(2)]
            v4 = [carve(NT) for _ in range(12)]
            picks = [carve(NT, EXPERTS) for _ in range(2)]
            both, rank, wide = (carve(NT, EXPERTS) for _ in range(3))
            local = carve(NT, EXPERTS)
            extra, ends, begins = (carve(EXPERTS) for _ in range(3))
            e15 = carve(MORE, EXPERTS)
            more_f, more_i = carve(MORE + 1), carve(MORE + 1, dt=I32)
            slot_f = [carve(NT) for _ in range(2)]
            slot_i = [carve(NT, dt=I32) for _ in range(2)]
            gates = [carve(NT) for _ in range(2)]
            loop_at = taken[0]
            dump = carve(D)
            loaded = load_norm(a["norm_moe_w_2"][0], None)
            t_const = p.dma("scalar", side_sem, tri, a["c_tri"], work_free)
            for dst, src in ((router_w, a["router_w"].rearrange("(t p) n -> p t n", p=P)),
                             (router_b, a["router_b"].partition_broadcast(P)),
                             (down8, a["c_down8"].partition_broadcast(P)),
                             (iota64, a["c_iota64"].partition_broadcast(P))):
                t_const = p.dma("scalar", side_sem, dst, src)
            t_ones = p.pool(lambda e: e.memset(ones, 1.0), work_free)
            t_hn = None
            hn_done, hT_done = [], []
            for i in range(NT):
                t_hn = rms_rows(i, hn[:, i, :], loaded, dump, [work_free, t_hn])
                hn_done.append(t_hn)
                hT_done += rows_to_T(i, t_hn, src=hn, before=work_free, engines=("scalar",))

            bank, bank_free = banks.take()
            W = GROUPS + EXPERTS

            def make(e, bank=bank):
                for i in range(NT):
                    for k in range(KD):
                        ins = e.matmul(bank[:, i * W:(i + 1) * W], xT[:, k, i * P:(i + 1) * P], router_w[:, k, :],
                                       start=(k == 0), stop=(k == KD - 1))
                return ins
            t = t_router = p.pe(make, bank_free, hT_done, t_const)

            def b3(x, n):
                return x.unsqueeze(2).broadcast_to([P, NT, n])

            def row(x, n):
                return x.unsqueeze(1).broadcast_to([P, NT, n])

            def tt(out, a_, b_, op, *w):
                return p.dve(lambda e: e.tensor_tensor(out, a_, b_, op), *w)

            t = tt(logits, bank[:, 0:NT * W].rearrange("p (i w) -> p i w", i=NT), row(router_b, W), ALU.add, t, t_const)
            banks.give(bank, t)
            lg = logits[:, :, 0:GROUPS]
            gmax, gsum, top, m1, m2 = v4[0], v4[1], v4[2], v4[3], v4[4]

            def argmax_onehot(out, scores, best, t):
                t = p.dve(lambda e: e.tensor_reduce(best, scores, AX.X, ALU.max), t)
                t = tt(t8, scores, b3(best, 8), ALU.is_equal, t)
                t = tt(t8, t8, row(down8, 8), ALU.mult, t)
                t = p.dve(lambda e: e.tensor_reduce(top, t8, AX.X, ALU.max), t)
                return tt(out, row(down8, 8), b3(top, 8), ALU.is_equal, t)

            t = argmax_onehot(oh_g, lg, gmax, t)
            t = tt(g8, lg, b3(gmax, 8), ALU.subtract, t)
            t = p.act(lambda e: e.activation(g8, g8, ACT.Exp), t)
            t = p.dve(lambda e: e.tensor_reduce(gsum, g8, AX.X, ALU.add), t)
            t = p.dve(lambda e: e.reciprocal(gsum, gsum), t)
            for i in range(NT):
                view = logits[:, i, GROUPS:].rearrange("p (g e) -> p e g", g=GROUPS)
                out = wide[:, i, :].rearrange("p (e g) -> p e g", e=PER_GROUP)
                t = tt(out, view, oh_g[:, i, :].unsqueeze(1).broadcast_to([P, PER_GROUP, GROUPS]), ALU.mult, t)
            t = p.dve(lambda e: e.tensor_reduce(s8.rearrange("p i e -> p (i e)"),
                                                wide.rearrange("p i (e g) -> p (i e) g", e=PER_GROUP),
                                                AX.X, ALU.add), t)
            t = argmax_onehot(ohs[0], s8, m1, t)
            t = p.dve(lambda e: e.scalar_tensor_tensor(out=s8, in0=ohs[0], scalar=NEG, in1=s8, op0=ALU.mult,
                                                       op1=ALU.add), t)
            t = argmax_onehot(ohs[1], s8, m2, t)
            d_, r_ = v4[5], v4[6]
            t = tt(d_, m2, m1, ALU.subtract, t)
            t = p.act(lambda e: e.activation(d_, d_, ACT.Exp), t)
            t = p.dve(lambda e: e.tensor_scalar(r_, d_, 1.0, None, ALU.add), t)
            t = p.dve(lambda e: e.reciprocal(r_, r_), t)
            t = tt(gates[0], gsum, r_, ALU.mult, t)
            t = tt(gates[1], gates[0], d_, ALU.mult, t)
            for n in range(2):
                for i in range(NT):
                    out = picks[n][:, i, :].rearrange("p (g e) -> p g e", g=GROUPS)
                    t = tt(out, oh_g[:, i, :].unsqueeze(2).broadcast_to([P, GROUPS, PER_GROUP]),
                           ohs[n][:, i, :].unsqueeze(1).broadcast_to([P, GROUPS, PER_GROUP]), ALU.mult, t)
            t_both = tt(both, picks[0], picks[1], ALU.add, t)
            bank, bank_free = banks.take()

            def make_rank(e, bank=bank):
                for i in range(NT + 1):
                    for j in range(min(i, NT - 1) + 1):
                        last = min(i, NT - 1)
                        ins = e.matmul(bank[:, i * EXPERTS:(i + 1) * EXPERTS], tri if j == i else ones,
                                       both[:, j, :], start=(j == 0), stop=(j == last))
                return ins
            t = p.pe(make_rank, bank_free, t_both, t_ones)
            t = p.dve(lambda e: e.tensor_copy(rank.rearrange("p i e -> p (i e)"), bank[:, 0:NT * EXPERTS]), t)
            count = bank[:, NT * EXPERTS:(NT + 1) * EXPERTS]
            t = p.dve(lambda e: e.scalar_tensor_tensor(out=local, in0=rank, scalar=1.0, in1=both, op0=ALU.add,
                                                       op1=ALU.mult), t)
            t_local = p.dve(lambda e: e.tensor_scalar(local, local, -1.0, None, ALU.add), t)
            t = p.dve(lambda e: e.tensor_scalar(extra, count, float(CAP), None, ALU.is_gt), t_local)
            for m in range(2, S // CAP):
                t = p.dve(lambda e, m=m: e.scalar_tensor_tensor(out=extra, in0=count, scalar=float(m * CAP),
                                                                in1=extra, op0=ALU.is_gt, op1=ALU.add), t)
            banks.give(bank, t)
            t = p.dve(lambda e: e.tensor_tensor_scan(ends, ones[:, 0:EXPERTS], extra, 0.0, ALU.mult, ALU.add), t, t_ones)
            t = tt(begins, ends, extra, ALU.subtract, t)
            t = p.dve(lambda e: e.tensor_tensor(e15, ends.unsqueeze(1).broadcast_to([P, MORE, EXPERTS]),
                                                iota64[:, 0:MORE].unsqueeze(2).broadcast_to([P, MORE, EXPERTS]),
                                                ALU.is_le), t)
            t = p.dve(lambda e: e.tensor_reduce(more_f[:, 0:MORE], e15, AX.X, ALU.add), t)
            t = p.dve(lambda e: e.tensor_scalar(more_f[:, 0:MORE], more_f[:, 0:MORE], float(EXPERTS - 1), None,
                                                ALU.min), t)
            t = p.dve(lambda e: e.tensor_copy(more_f[:, MORE:MORE + 1], ends[:, EXPERTS - 1:EXPERTS]), t)
            t_more = p.dve(lambda e: e.tensor_copy(more_i, more_f), t)
            t_slot = []
            rk, ex, bg, fl = v4[7], v4[8], v4[9], v4[10]
            t = t_more
            for n in range(2):
                for out, by in ((rk, rank), (ex, row(iota64, EXPERTS)), (bg, row(begins, EXPERTS))):
                    t = tt(wide, picks[n], by, ALU.mult, t)
                    t = p.dve(lambda e, out=out: e.tensor_reduce(out, wide, AX.X, ALU.add), t)
                t = p.dve(lambda e: e.tensor_scalar(fl, rk, float(CAP), None, ALU.is_ge), t)
                t = p.dve(lambda e: e.scalar_tensor_tensor(out=bg, in0=bg, scalar=float(EXPERTS - 1), in1=ex,
                                                           op0=ALU.add, op1=ALU.subtract), t)
                t = tt(bg, bg, fl, ALU.mult, t)
                t = tt(bg, bg, ex, ALU.add, t)
                t = p.dve(lambda e, n=n: e.scalar_tensor_tensor(out=slot_f[n], in0=bg, scalar=float(CAP), in1=rk,
                                                                op0=ALU.mult, op1=ALU.add), t)
                t = p.dve(lambda e, n=n: e.tensor_copy(slot_i[n], slot_f[n]), t)
                t_slot.append(t)

            p.stage("experts")
            carve_from(loop_at)
            chosen = Pool_([carve(NT, CAP) for _ in range(2)])
            rows_ = Pool_([carve(BANK) for _ in range(2)])
            xeT = Pool_([carve(4, 2, CAP) for _ in range(2)])
            silus = Pool_([carve(BANK, parts=CAP) for _ in range(2)])
            hids = Pool_([carve(EH, parts=CAP) for _ in range(2)])
            hidT = Pool_([carve(EH // P, CAP) for _ in range(2)])
            outs = Pool_([carve(BANK) for _ in range(3)])
            for name_, slot, free in (("xT", xT[:, :, :].rearrange("p k s -> p (k s)"), t_router),
                                      ("work0", carve(SLOT), [t_router, work_free, hn_done, t_const]),
                                      ("work1", carve(SLOT), [t_router, work_free, hn_done, t_const])):
                add_slot(name_, slot, free)
            reuse = [t_slot, hn_done]
            def gather_rows(choose):
                ch, ch_free = chosen.take()
                c = choose(ch, [ch_free, reuse])
                bank, bank_free = banks.take()

                def make(e):
                    for i in range(NT):
                        for half in range(2):
                            ins = e.matmul(bank[half * CAP:(half + 1) * CAP, :], ch[:, i, :],
                                           hn[:, i, half * BANK:(half + 1) * BANK],
                                           start=(i == 0), stop=(i == NT - 1))
                    return ins
                t = p.pe(make, c, bank_free)
                chosen.give(ch, t)
                r, r_free = rows_.take()
                c = p.act(lambda e: e.activation(r, bank[:, :], ACT.Copy), t, r_free, reuse)
                banks.give(bank, c)
                return r, c

            def rows_transposed(r, ready):
                bank, bank_free = banks.take()

                def make(e):
                    for j in range(4):
                        ins = e.transpose(bank[:, j * P:(j + 1) * P], r[:, j * P:(j + 1) * P], ident[:, :])
                    return ins
                t = p.pe(make, ready, bank_free)
                rows_.give(r, t)
                x, x_free = xeT.take()
                c = p.dve(lambda e: e.tensor_copy(x.rearrange("p a b c -> p (a b c)"), bank[:, :]), t, x_free, reuse)
                banks.give(bank, c)
                return x, c

            def hidden(x, ready, wg, wu, landed):
                bank, bank_free = banks.take()

                def make(e):
                    for k in range(KD):
                        xk = x[:, k % 4, k // 4, :]
                        for n, w in ((0, wg), (1, wu)):
                            ins = e.matmul(bank[n * CAP:(n + 1) * CAP, :], xk, w[:, k, :],
                                           start=(k == 0), stop=(k == KD - 1))
                    return ins
                t = p.pe(make, ready, bank_free, landed)
                xeT.give(x, t)
                s, s_free = silus.take()
                c = p.act(lambda e: e.activation(s, bank[0:CAP, :], ACT.Silu), t, s_free, reuse)
                h, h_free = hids.take()
                c = p.dve(lambda e: e.tensor_tensor(h, s, bank[CAP:2 * CAP, :], ALU.mult), c, h_free, reuse)
                banks.give(bank, c)
                silus.give(s, c)
                return h, c, t

            def hidden_transposed(h, ready):
                bank, bank_free = banks.take()

                def make(e):
                    for j in range(EH // P):
                        ins = e.transpose(bank[:, j * CAP:(j + 1) * CAP], h[:, j * P:(j + 1) * P],
                                          ident[0:CAP, 0:CAP])
                    return ins
                t = p.pe(make, ready, bank_free)
                hids.give(h, t)
                hT_, h_free = hidT.take()
                c = p.act(lambda e: e.activation(hT_.rearrange("p a b -> p (a b)"), bank[:, 0:4 * CAP], ACT.Copy),
                          t, h_free, reuse)
                banks.give(bank, c)
                return hT_, c

            def expert_out(hT_, ready, wd, landed, block, store_sem):
                bank, bank_free = banks.take()

                def make(e):
                    for k in range(EH // P):
                        for half in range(2):
                            ins = e.matmul(bank[half * CAP:(half + 1) * CAP, :], hT_[:, k, :],
                                           wd[:, k, half * BANK:(half + 1) * BANK],
                                           start=(k == 0), stop=(k == EH // P - 1))
                    return ins
                t = p.pe(make, ready, bank_free, landed)
                hidT.give(hT_, t)
                o, o_free = outs.take()
                c = p.act(lambda e: e.activation(o, bank[:, :], ACT.Copy), t, o_free, reuse)
                banks.give(bank, c)
                for half in range(2):
                    s = p.dma("scalar", store_sem, y_slots[block * CAP:(block + 1) * CAP, half * BANK:(half + 1) * BANK],
                              o[half * CAP:(half + 1) * CAP, :], c, t_clear)
                outs.give(o, s)
                return t, s

            store_sems = [p.semaphore(f"block_stores{j}") for j in range(3)]
            w1, w3, w2 = a["moe_w1_2"][0], a["moe_w3_2"][0], a["moe_w2_2"][0]

            def first_choose(ex_):
                def choose(ch, free):
                    t = None
                    for i in range(NT):
                        t = p.dve(lambda e, i=i: e.tensor_scalar(ch[:, i, :], iota64, local[:, i, ex_:ex_ + 1], None,
                                                                 ALU.is_equal), free)
                    return t
                return choose

            rows, xs, hs, hTs, stored = {}, {}, {}, {}, []
            down = {}
            for n in range(EXPERTS + 2):
                if n < EXPERTS:
                    rows[n] = gather_rows(first_choose(n))
                if 1 <= n <= EXPERTS:
                    ex_ = n - 1
                    pg, pu = Panel((w1[ex_], D)), Panel((w3[ex_], D))
                    down[ex_] = Panel((w2[ex_], EH))
                    h, c, t = hidden(*xs.pop(ex_), pg.w, pu.w, [pg.landed, pu.landed])
                    pg.release(t)
                    pu.release(t)
                    hs[ex_] = (h, c)
                if n < EXPERTS:
                    xs[n] = rows_transposed(*rows.pop(n))
                if 2 <= n:
                    ex_ = n - 2
                    pd = down.pop(ex_)
                    t, s = expert_out(*hTs.pop(ex_), pd.w, pd.landed, ex_, store_sems[ex_ % 3])
                    pd.release(t)
                    stored.append(s)
                if 1 <= n <= EXPERTS:
                    hTs[n - 1] = hidden_transposed(*hs.pop(n - 1))

            p.branch_if(more_i[0:1, MORE:MORE + 1], t_more)
            p.stage("more")
            keep = [(pool_, list(pool_.free)) for pool_ in (banks, chosen, rows_, xeT, silus, hids, hidT, outs)]
            more_landed = p.semaphore("more_landed")
            more_stored = [p.semaphore(f"more_stored{j}") for j in range(3)]
            (s1, f1), (s3, f3), (s2, f2) = panels.free[0:3]
            wv1, wv3 = (s_[:, :].rearrange("p (t n) -> p t n", t=KD) for s_ in (s1, s3))
            wv2 = s2[:, :].rearrange("p (t n) -> p t n", t=EH // P)
            t_free = [f1, f3, f2]
            for j in range(MORE):
                def load(dst, w, k, j=j):
                    def make(e):
                        ex_ = e.value_load(more_i[0:1, j:j + 1], min_val=0, max_val=EXPERTS - 1)
                        return e.dma_start(dst, w[bass.ds(ex_, 1)].rearrange("o (t p) n -> p (o t) n", p=P))
                    return make
                for dst, w, k in ((wv1, w1, D), (wv3, w3, D), (wv2, w2, EH)):
                    landed = p.put("sync", [t_free, t_more], load(dst, w, k), more_landed, 16)

                def choose(ch, free, j=j):
                    t = None
                    base = float((EXPERTS + j) * CAP)
                    for i in range(NT):
                        t = p.dve(lambda e, i=i: e.tensor_scalar(ch[:, i, :], iota64, base, slot_f[0][:, i:i + 1],
                                                                 ALU.add, ALU.is_equal), free, t)
                        tmp = wide[:, i, 0:CAP]
                        t = p.dve(lambda e, i=i, tmp=tmp: e.tensor_scalar(tmp, iota64, base, slot_f[1][:, i:i + 1],
                                                                          ALU.add, ALU.is_equal), t)
                        t = p.dve(lambda e, i=i, tmp=tmp: e.tensor_tensor(ch[:, i, :], ch[:, i, :], tmp, ALU.add), t)
                    return t
                r, c = gather_rows(choose)
                x, c = rows_transposed(r, c)
                h, c, t = hidden(x, c, wv1, wv3, landed)
                hT_, c = hidden_transposed(h, c)
                t, s = expert_out(hT_, c, wv2, landed, EXPERTS + j, more_stored[j % 3])
                t_free = [t]
            p.join(["more_scalar_done", "more_vector_done", "more_tensor_done", "more_gpsimd_done",
                    more_landed, *more_stored])
            p.branch_end()
            for pool_, free in keep:
                pool_.free = free

            p.stage("combine")
            carve_from(loop_at)
            fetched = Pool_([carve(D) for _ in range(4)])
            dump = carve(D)
            fetch_sems = [p.semaphore(f"rows_fetched{j}") for j in range(4)]
            results = [carve(D) for _ in range(2)]
            loaded = load_norm(a["norm_final_w_2"], None)
            n_f = 0
            t_res = [None, None]
            loop_free = [t for pool_ in (panels, chosen, rows_, xeT, silus, hids, hidT, outs) for _, t in pool_.free]
            for i in range(NT):
                for n in range(2):
                    f, f_free = fetched.take()
                    sem = fetch_sems[n_f % 4]
                    n_f += 1
                    idx = slot_i[n][:, i:i + 1]
                    t = p.put("gpsimd", [stored, t_clear, t_slot, f_free, loop_free],
                              lambda e, f=f, idx=idx: e.indirect_dma_start(
                                  out=f, out_offset=None, in_=y_slots[:, :],
                                  in_offset=bass.IndirectOffsetOnAxis(ap=idx, axis=0)), sem, 16)
                    x = x_tok[:, i, :]
                    c = p.dve(lambda e, f=f, x=x, i=i, n=n: e.scalar_tensor_tensor(
                        out=x, in0=f, scalar=gates[n][:, i:i + 1], in1=x, op0=ALU.mult, op1=ALU.add),
                        t, state["x"][i])
                    state["x"][i] = c
                    fetched.give(f, c)
                o = results[i % 2]
                c = rms_rows(i, o, loaded, dump, [loop_free, t_res])
                t_res[i % 2] = p.dma("sync", out_sem, result[0, i * P:(i + 1) * P, :], o, c)

        y_slots = nc.dram_tensor("y_slots", [BLOCKS * CAP, D], F32, kind="Internal").ap()
        cleared = p.semaphore("further_slots_cleared")
        parts = MORE * CAP // 8
        p.stage("clear")
        t_clear = p.pool(lambda e: e.memset(shift[0:parts, :], 0.0), state["norm_free"])
        t_clear = p.dma("gpsimd", cleared, y_slots[EXPERTS * CAP:, :].rearrange("(p r) d -> p r d", r=8),
                        shift[0:parts, :].unsqueeze(1).broadcast_to([parts, 8, D]), t_clear)

        y_attT, t_att, t_x = dilated_attention([work_free, state["xT"]])
        used = [t_att, ("attention_vector_done", p.reached["attention_vector_done"]),
                ("attention_tensor_done", p.reached["attention_tensor_done"]),
                ("attention_gpsimd_done", p.reached["attention_gpsimd_done"])]
        y_retT, t_ret, merged_at = retention(NT * S, t_x, used)
        last = merge(y_attT, t_att, y_retT, t_ret, merged_at, t_x)
        experts([last, state["x"]])

        p.raw("gpsimd", lambda e: e.wait_ge(p.names[out_sem], p.reached[out_sem]))
        p.emit(ctx.enter_context(nc.Block()))


def constants():
    f = np.float32
    def swap(blocks, size):
        m = np.zeros((size, size), f)
        for lo, half in blocks:
            for j in range(half):
                m[lo + half + j, lo + j] = -1.0
                m[lo + j, lo + half + j] = 1.0
        return m
    c = {"c_ident": np.eye(P, dtype=f),
         "c_swap_a": swap([(0, 32), (64, 32)], P),
         "c_swap_q": swap([(NOPE, ROPE // 2)], QKD)}
    inv = (np.float32(10000.0) ** (-np.arange(0, ROPE, 2, dtype=f) / np.float32(ROPE))).astype(f)
    c["c_freq"] = np.concatenate([np.zeros(NOPE, f), inv, inv])[:, None].copy()
    mask = np.zeros((P, S), f)
    mask[:KV_CHUNK, S - KV_CHUNK:] = NEG
    c["c_mask_q"] = mask
    token = np.arange(S).reshape(-1, DIL).T.reshape(-1)
    masks = np.zeros((P, NT * S + 2 * P), np.uint16)
    minus = np.uint16(np.array([NEG], f).view(np.uint32)[0] >> 16)
    lane = np.arange(P)
    (w0, _), (w1, d1), (w2, d2) = WINDOWS
    for r in range(DIL):
        far = np.abs((DIL * lane + r)[:, None] - token[None, :]) > w0 // 2
        masks[:, r * S:(r + 1) * S][far] = minus
    apart = DIL * (lane[:, None] - lane[None, :])
    masks[:, NT * S:NT * S + P][(apart % d1 != 0) | (np.abs(apart) > w1 // 2)] = minus
    masks[:, NT * S + P:][(apart % d2 != 0) | (np.abs(apart) > w2 // 2)] = minus
    c["c_mask_a"] = masks
    inv = (1.0 / (np.float32(10000.0) ** (np.arange(0, AHD, 2, dtype=f) / np.float32(AHD)))).astype(f)
    ang = (np.arange(S, dtype=f)[None, :] * inv[lane % (AHD // 2)][:, None]).astype(f)
    cos, sin = np.cos(ang).astype(f), np.sin(ang).astype(f)
    c["c_cos_r"], c["c_sin_r"] = cos, sin
    c["c_cos_a"], c["c_sin_a"] = np.ascontiguousarray(cos[:, token]), np.ascontiguousarray(sin[:, token])
    rel = np.arange(S + (NT - 1) * P)[None, :] - (NT - 1) * P - lane[:, None]
    c["c_ahead"] = np.maximum(rel, 0).astype(np.float16)
    c["c_behind"] = np.maximum(-rel, 0).astype(np.float16)
    c["c_twice"] = ((1 + (rel == 0)) * RQK ** -0.5).astype(np.float16)
    c["c_tri"] = (lane[:, None] < lane[None, :]).astype(f)
    c["c_down8"] = np.arange(8, 0, -1).astype(f)
    c["c_iota64"] = np.arange(EXPERTS).astype(f)
    return c


def columns(inputs):
    out = np.zeros((P, PC_ALL), np.float32)
    tile = lambda v: np.asarray(v).reshape(-1, P).T
    for l in range(DEPTH):
        o = l * PC_LAYER
        b = np.asarray(inputs["mix_b_in"])[l]
        out[NOPE:QKD, o + PC_KR] = b[2 * RANK:2 * RANK + ROPE]
        u = b[2 * RANK + ROPE:]
        out[:, o + PC_UA:o + PC_UA + CT] = tile(u[:CONV])
        out[:, o + PC_UG:o + PC_UG + CT] = tile(u[CONV:])
        out[:, o + PC_QN:o + PC_QN + 2] = tile(np.asarray(inputs["mla_q_norm"])[l])
        out[:, o + PC_QN + 2:o + PC_QN + 4] = tile(np.asarray(inputs["mla_kv_norm"])[l])
        w = np.asarray(inputs["conv_dw_w"])[l].reshape(TAPS, CT, P)
        out[:, o + PC_W:o + PC_W + CT * TAPS] = w.transpose(2, 1, 0).reshape(P, CT * TAPS)
        out[:, o + PC_DWB:o + PC_DWB + CT] = tile(np.asarray(inputs["conv_dw_b"])[l])
        out[:, o + PC_CNG:o + PC_CNG + CT] = tile(np.asarray(inputs["conv_norm_g"])[l])
        out[:, o + PC_CNB:o + PC_CNB + CT] = tile(np.asarray(inputs["conv_norm_b"])[l])
    out[:, PC_GATE:PC_GATE + 2 * KD] = tile(np.asarray(inputs["b_branch_gate_2"])[0])
    return out


_DIRECT = ["x", "mem", "positions", "mix_w_in", "mix_b_in", "mla_w_uq", "mla_w_ukv", "mix_w_o",
           "ln1_g", "ln1_b", "xa_w_q", "xa_w_kv", "xa_w_o", "ln2_g", "ln2_b", "ffn_w_in", "ffn_w_down",
           "ln3_g", "ln3_b", "norm_mix_w_2", "w_in_2", "ret_gn_w_2", "w_attn_branch_2", "w_ret_branch_2",
           "w_out_2", "norm_moe_w_2", "moe_w1_2", "moe_w3_2", "moe_w2_2", "norm_final_w_2"]


def arranged(inputs):
    arrays = {n: np.ascontiguousarray(inputs[n]) for n in _DIRECT}
    arrays["cols"] = columns(inputs)
    w = np.asarray(inputs["w_in_2"])[0][:, :3 * NG * AH * AHD].reshape(D, 3, NG, AH // 2, P)
    arrays["w_attn_2"] = np.ascontiguousarray(w.transpose(0, 3, 1, 2, 4)).reshape(D, -1)
    arrays["decays"] = np.concatenate([inputs["ret_decay_fwd_2"], inputs["ret_decay_bwd_2"]])
    arrays["router_w"] = np.concatenate([inputs["moe_w_group_2"][0], inputs["moe_w_expert_2"][0]], axis=1)
    arrays["router_b"] = np.concatenate([inputs["moe_b_group_2"][0], inputs["moe_b_expert_2"][0]])
    arrays.update(constants())
    return arrays


def kernel(**inputs):
    import concourse.bacc as bacc
    from concourse.bass_utils import run_bass_kernel_spmd

    nc = bacc.Bacc("TRN2", target_bir_lowering=False, num_devices=1)
    arrays = {f"in_{n}": v for n, v in arranged(inputs).items()}
    dram = {n[3:]: nc.dram_tensor(n, v.shape, mybir.dt.from_np(v.dtype), kind="ExternalInput").ap()
            for n, v in arrays.items()}
    out = nc.dram_tensor("out_0", (1, S, D), F32, kind="ExternalOutput").ap()
    both_blocks(nc, dram, out)
    got = run_bass_kernel_spmd(nc, [arrays], core_ids=[0])
    return got.results[0]["out_0"]
```

```python
from contextlib import ExitStack

import numpy as np

import concourse.bass as bass
from concourse import mybir

F32 = mybir.dt.float32
F32R = mybir.dt.float32r
I32 = mybir.dt.int32
BF16 = mybir.dt.bfloat16
F16 = mybir.dt.float16
ALU = mybir.AluOpType
ACT = mybir.ActivationFunctionType
AX = mybir.AxisListType

P = 128
S = 512
NT = S // P
D = 1024
KD = D // P
DEPTH = 2
BANK = 512

MEM = 256
MT = MEM // P
HEADS, NOPE, ROPE, VDIM = 8, 64, 32, 64
QKD = NOPE + ROPE
RANK = 256
CONV = 512
CT = CONV // P
TAPS = 31
XH = 4
XHD = D // XH
FFN = 2816
FT = FFN // P
ALPHA = float((2.0 * DEPTH) ** 0.25)
LN_EPS, RMS_EPS = 1e-5, 1e-6
KV_CHUNK = 64

AH, AHD, NG = 8, 64, 3
DIL = 4
WINDOWS = ((128, 1), (512, 4), (2048, 16))
RH, RQK, RV = 8, 64, 128
GROUPS, PER_GROUP = 8, 8
EXPERTS = GROUPS * PER_GROUP
EH = 512
CAP = 64
MORE = (2 * S - CAP) // CAP
BLOCKS = EXPERTS + MORE
NEG = -1.0e30

PC_LAYER = 1 + 2 * CT + 4 + CT * TAPS + 3 * CT
PC_KR, PC_UA, PC_UG, PC_QN, PC_W = 0, 1, 1 + CT, 1 + 2 * CT, 5 + 2 * CT
PC_DWB = PC_W + CT * TAPS
PC_CNG, PC_CNB = PC_DWB + CT, PC_DWB + 2 * CT
PC_GATE = DEPTH * PC_LAYER
PC_ALL = PC_GATE + 2 * KD


class Pool_:

    def __init__(self, buffers):
        self.free = [(b, None) for b in buffers]

    def take(self):
        assert self.free, "no buffer is free here"
        return self.free.pop(0)

    def give(self, buffer, after):
        self.free.append((buffer, after))


class Program:

    ENGINES = ("sync", "scalar", "vector", "tensor", "gpsimd")

    def __init__(self, nc, ctx):
        self.nc, self.ctx = nc, ctx
        self.queue = {e: [] for e in self.ENGINES}
        self.waited = {e: {} for e in self.ENGINES}
        self.reached = {}
        self.done = {}
        self.names = {}
        self.last_pool = None

    def semaphore(self, name):
        sem = self.ctx.enter_context(self.nc.semaphore(name))
        self.reached[name] = 0
        self.names[name] = sem
        return name

    def stage(self, name):
        for e in ("scalar", "vector", "tensor", "gpsimd"):
            self.done[e] = self.semaphore(f"{name}_{e}_done")

    def put(self, engine, waits, make, sem, by):
        def flat(ws):
            for w in ws:
                if isinstance(w, list):
                    yield from flat(w)
                elif w is not None:
                    yield w

        needed = []
        for w in flat(waits):
            if self.waited[engine].get(w[0], 0) < w[1]:
                self.waited[engine][w[0]] = w[1]
                needed = [x for x in needed if x[0] != w[0]] + [w]
        self.reached[sem] += by
        self.queue[engine].append((needed, make, sem, by))
        return (sem, self.reached[sem])

    def op(self, engine, make, *waits):
        return self.put(engine, waits, make, self.done[engine], 1)

    def pe(self, make, *waits):
        return self.op("tensor", make, *waits)

    def act(self, make, *waits):
        return self.op("scalar", make, *waits)

    def dve(self, make, *waits):
        return self.op("vector", make, *waits)

    def pool(self, make, *waits):
        self.last_pool = self.op("gpsimd", make, self.last_pool, *waits)
        return self.last_pool

    def dma(self, engine, sem, out, in_, *waits):
        return self.put(engine, waits, lambda e: e.dma_start(out, in_), sem, 16)

    def branch_if(self, flag, ready):
        for e in self.ENGINES:
            self.queue[e].append(([], None, flag, ready))
            self.waited[e][ready[0]] = max(ready[1], self.waited[e].get(ready[0], 0))
        self.before = ({e: dict(w) for e, w in self.waited.items()}, self.last_pool)

    def join(self, names):
        for e in self.ENGINES:
            for n in names:
                if self.reached[n]:
                    self.raw(e, lambda q, n=n, v=self.reached[n]: q.wait_ge(self.names[n], v))

    def branch_end(self):
        for e in self.ENGINES:
            self.queue[e].append(([], None, None, None))
        self.waited, self.last_pool = self.before

    def raw(self, engine, make):
        self.queue[engine].append(([], make, None, 0))

    def emit(self, block):
        def play(name):
            def body(e):
                guard = None
                for needed, make, sem, by in self.queue[name]:
                    if make is None and sem is not None:
                        e.wait_ge(self.names[by[0]], by[1])
                        guard = e.If(e.value_load(sem) > 0)
                        guard.__enter__()
                        continue
                    if make is None:
                        guard.__exit__(None, None, None)
                        continue
                    for s, v in needed:
                        e.wait_ge(self.names[s], v)
                    ins = make(e)
                    if sem is not None:
                        ins.then_inc(self.names[sem], by)
            return body

        for name in self.ENGINES:
            getter = {"sync": block.sync, "scalar": block.scalar, "vector": block.vector,
                      "tensor": block.tensor, "gpsimd": block.gpsimd}[name]
            getter(play(name))


def both_blocks(nc, a, result):
    ctx = ExitStack()
    with ctx:
        p = Program(nc, ctx)

        def sb(name, shape, dt=F32):
            return ctx.enter_context(nc.sbuf_tensor(name, shape, dt))

        twins = {}

        def sb_twin(name, shape):
            at = (nc.sbuf_base + 31) // 32 * 32
            t = sb(name, shape)
            twins[t.name] = nc.alloc_sbuf_tensor_at(f"{name}_rounded", shape, F32R, offset=at)
            assert nc.sbuf_base == at + 4 * int(np.prod(shape[1:]))
            return t

        def rounded(x):
            return bass.AP(twins[x.tensor.name], x.offset, x.ap)

        psum = [ctx.enter_context(nc.psum_tensor(f"bank{i}", [P, BANK], F32)) for i in range(8)]
        banks = Pool_(psum)

        x_tok = sb("x_tok", [P, NT, D])
        xT = sb_twin("xT", [P, KD, S])
        memT = sb("memT", [P, KD, MEM])
        ident = sb("ident", [P, P])
        swap_a = sb("swap_a", [P, P])
        swap_q = sb("swap_q", [QKD, QKD])
        cols = sb("cols", [P, PC_ALL])
        gain = sb("gain", [P, D])
        shift = sb("shift", [P, D])
        stat = sb("stat", [P, NT, 2, 6])
        mean_var = sb("mean_var", [P, NT, 2])
        root = sb("root", [P, NT, 8])
        power = sb("power", [P, 8])
        small = sb("small", [P, 64])
        SLOT = KD * BANK // 2
        piece_slots = [sb_twin(f"piece{i}", [P, SLOT]) for i in range(4)]
        high_slots = [sb_twin(f"piece_high{i}", [P, SLOT]) for i in range(2)]
        WORK = 107 * 256
        work = sb_twin("work", [P, WORK])
        XT_LOW_AT = 84 * 256
        xT_low = work[:, XT_LOW_AT:XT_LOW_AT + KD * S].rearrange("p (k s) -> p k s", k=KD)

        taken = [0]

        def carve_from(offset):
            taken[0] = offset

        def carve(*free, parts=P, dt=F32):
            n = int(np.prod(free))
            words = n if dt in (F32, I32) else (n + 1) // 2
            lo = taken[0]
            taken[0] += words
            assert taken[0] <= WORK, taken[0] / 256
            v = work[0:parts, lo:lo + words]
            if dt != F32:
                v = v.bitcast(dt)
            if len(free) == 2:
                v = v.rearrange("p (a b) -> p a b", a=free[0])
            if len(free) == 3:
                v = v.rearrange("p (a b c) -> p a b c", a=free[0], b=free[1])
            return v

        first_sem = p.semaphore("first_loads")
        setup = p.semaphore("setup_loads")
        mem_sem = p.semaphore("memory_load")
        norm_sem = p.semaphore("norm_param_loads")
        side_sem = p.semaphore("side_loads")
        up_sem = p.semaphore("up_projection_loads")
        out_sem = p.semaphore("stores")

        def high_of(dst, src, *waits):
            return p.act(lambda e: e.activation(rounded(dst), src, ACT.Copy), *waits)

        def low_of(dst, src, high, *waits):
            return p.dve(lambda e: e.tensor_tensor(rounded(dst), src, rounded(high).bitcast(F32), ALU.subtract), *waits)

        def split(high, low, src, *waits):
            return low_of(low, src, high, high_of(high, src, *waits))

        def product(out, lhs, rhs, kt, first=True, last=True):
            def make(e):
                for k in range(kt):
                    a_, b_ = lhs(k), rhs(k)
                    if isinstance(a_, tuple):
                        terms = [(rounded(x), rounded(y))
                                 for x, y in ((a_[0], b_[0]), (a_[0], b_[1]), (a_[1], b_[0]))]
                    else:
                        terms = [(a_, b_)]
                    for n, (x, y) in enumerate(terms):
                        ins = e.matmul(out, x, y, start=(first and k == 0 and n == 0),
                                       stop=(last and k == kt - 1 and n == len(terms) - 1))
                return ins
            return make

        def x_all(k):
            return xT[:, k, :], xT_low[:, k, :]

        def x_tile(i):
            return lambda k: (xT[:, k, i * P:(i + 1) * P], xT_low[:, k, i * P:(i + 1) * P])

        def tok_of(t, i):
            return lambda k: t[:, k, i * P:(i + 1) * P]

        slot_sems = {}
        piece_pool, high_pool = Pool_([]), Pool_(high_slots)

        def add_slot(name, slot, free=None):
            slot_sems[id(slot)] = p.semaphore(f"piece_{name}_landed")
            piece_pool.give(slot, free)

        for i, s in enumerate(piece_slots):
            add_slot(str(i), s)

        class Piece:

            def __init__(self, label, w, wants_split):
                self.label, self.wants_split, self.high = label, wants_split, None
                self.slot, before = piece_pool.take()
                k, n = w.shape[-2] // P, w.shape[-1]
                self.kt, self.flat = k, self.slot[:, 0:k * n]
                self.w = self.flat.rearrange("p (t n) -> p t n", t=k)
                self.ready = p.dma("sync", slot_sems[id(self.slot)], self.w,
                                   w.rearrange("(t p) n -> p t n", p=P), before)

            def split(self):
                self.high_slot, before = high_pool.take()
                flat = self.high_slot[:, 0:self.flat.shape[1]]
                self.high = flat.rearrange("p (t n) -> p t n", t=self.kt)
                self.ready = split(flat, self.flat, self.flat, self.ready, before)

            def cols(self, c0, n):
                if self.high is None:
                    return lambda k: self.w[:, k, c0:c0 + n]
                return lambda k: (self.high[:, k, c0:c0 + n], self.w[:, k, c0:c0 + n])

            def release(self, after):
                piece_pool.give(self.slot, after)
                if self.high is not None:
                    high_pool.give(self.high_slot, after)

        plan = []
        loaded_pieces = []

        def look_ahead():
            while plan and piece_pool.free:
                loaded_pieces.append(Piece(*plan.pop(0)))
            nxt = loaded_pieces[0] if loaded_pieces else None
            if nxt is not None and nxt.wants_split and nxt.high is None and high_pool.free:
                nxt.split()

        def take_piece(label):
            look_ahead()
            piece = loaded_pieces.pop(0)
            assert piece.label == label and (piece.high is not None) == piece.wants_split, (label, piece.label)
            look_ahead()
            return piece

        def by_columns(label, w, c0, c1, step=2 * P, wants_split=True):
            for c in range(c0, c1, step):
                plan.append((label, w[:, c:min(c + step, c1)], wants_split))

        def by_rows(label, w, k0, k1, c0, c1, wants_split=True, step=SLOT // BANK):
            for k in range(k0, k1, step):
                plan.append((label, w[k * P:min(k + step, k1) * P, c0:c1], wants_split))

        U0 = 2 * RANK + ROPE
        FFN_HALVES = ((0, FT // 2), (FT // 2, FT))
        for layer in range(DEPTH):
            w = a["mix_w_in"][layer]
            by_rows("latents", w, 0, KD, 0, BANK)
            by_columns("conv gate", w, U0 + CONV, U0 + 2 * CONV)
            by_columns("conv in", w, U0, U0 + CONV)
            by_columns("memory keys", a["xa_w_kv"][layer], 0, D, wants_split=False)
            for half in range(2):
                by_rows("mix out", a["mix_w_o"][layer], 0, KD, half * BANK, (half + 1) * BANK)
            for half in range(2):
                by_rows("memory values", a["xa_w_kv"][layer], 0, KD, D + half * BANK, D + (half + 1) * BANK,
                        wants_split=False)
            by_columns("cross query", a["xa_w_q"][layer], 0, D)
            for half in range(2):
                by_rows("cross out", a["xa_w_o"][layer], 0, KD, half * BANK, (half + 1) * BANK)
            for f0, f1 in FFN_HALVES:
                for f in range(f0, f1, 2):
                    c0, c1 = f * P, min(f + 2, f1) * P
                    by_columns("ffn gate", a["ffn_w_in"][layer], c0, c1)
                    by_columns("ffn up", a["ffn_w_in"][layer], FFN + c0, FFN + c1)
                for half in range(2):
                    by_rows("ffn down", a["ffn_w_down"][layer], f0, f1, half * BANK, (half + 1) * BANK)
        A_COLS = 3 * NG * AH * AHD
        QR0, KR0 = A_COLS, A_COLS + RH * RQK
        VR0 = KR0 + RH * RQK
        GR0 = VR0 + RH * RV
        GT0 = GR0 + RH * RV
        PAIR = 3 * NG * P
        VCOLS = NG * P // 2
        w2in = a["w_in_2"][0]
        for pair in range(AH // 2):
            by_columns("attention qk", a["w_attn_2"], pair * PAIR, pair * PAIR + 2 * NG * P)
            by_columns("attention v", a["w_attn_2"], pair * PAIR + 2 * NG * P, (pair + 1) * PAIR, step=VCOLS)
        for half in range(2):
            by_rows("retention gate", w2in, 0, KD, GR0 + half * BANK, GR0 + (half + 1) * BANK)
        by_columns("retention q", w2in, QR0, KR0)
        by_columns("retention k", w2in, KR0, VR0)
        for half in range(2):
            by_rows("retention v", w2in, 0, KD, VR0 + half * BANK, VR0 + (half + 1) * BANK)
        for c0 in range(0, D, 2 * P):
            c1 = c0 + 2 * P
            by_columns("attention's gate", w2in, GT0 + c0, GT0 + c1)
            by_columns("attention's branch", a["w_attn_branch_2"][0], c0, c1, wants_split=False)
            by_columns("retention's gate", w2in, GT0 + D + c0, GT0 + D + c1)
            by_columns("retention's branch", a["w_ret_branch_2"][0], c0, c1)
        for half in range(2):
            by_rows("mixer out", a["w_out_2"][0], 0, KD, half * BANK, (half + 1) * BANK)
        for ex in range(EXPERTS):
            for name in ("moe_w1_2", "moe_w3_2", "moe_w2_2"):
                w = a[name][0, ex]
                by_rows(name, w, 0, w.shape[0] // P, 0, w.shape[1], wants_split=False, step=SLOT // w.shape[1])

        flip = [0]

        def evacuate(dst, src, *waits, engines=("scalar", "vector")):
            flip[0] += 1
            name = engines[flip[0] % len(engines)]
            if name == "scalar":
                return p.act(lambda e: e.activation(dst, src, ACT.Copy), *waits)
            return p.dve(lambda e: e.tensor_copy(dst, src), *waits)

        def transposed(src_of, dst_of, n_blocks, *waits, low_of_dst=None, before=None):
            toks = []
            for b in range(0, n_blocks, 4):
                m = min(4, n_blocks - b)
                bank, bank_free = banks.take()

                def make(e, b=b, m=m, bank=bank):
                    for j in range(m):
                        ins = e.transpose(bank[:, j * P:(j + 1) * P], src_of(b + j), ident[:, :])
                    return ins
                t = p.pe(make, bank_free, *waits)
                src = bank[:, 0:m * P].rearrange("p (j c) -> p j c", j=m)
                if low_of_dst is None:
                    c = evacuate(dst_of(b, m), src, t, before, engines=("scalar",))
                else:
                    c = split(dst_of(b, m), low_of_dst(b, m), src, t, before)
                banks.give(bank, c)
                toks.append(c)
            return toks

        def rows_to_T(i, *waits, src=None, dst=None, low=None, before=None):
            src = x_tok if src is None else src
            if dst is None:
                dst, low = xT, xT_low
            return transposed(lambda k: src[:, i, k * P:(k + 1) * P],
                              lambda b, m: dst[:, b:b + m, i * P:(i + 1) * P], src.shape[2] // P, *waits,
                              low_of_dst=None if low is None else lambda b, m: low[:, b:b + m, i * P:(i + 1) * P],
                              before=before)

        def inverse_root(i, n, var, scale, eps, *waits):
            t = p.dve(lambda e: e.tensor_scalar(root[:, i, 0:n], var, scale, eps, ALU.mult, ALU.add), *waits)
            return p.pool(lambda e: e.tensor_tensor(root[:, i, 0:n], root[:, i, 0:n], power[:, 0:n], ALU.pow), t, t_power)

        state = {"x": [None] * NT, "xT": [None] * NT, "norm_free": None, "xT_free": None}

        def load_norm(g, b):
            t = p.dma("scalar", norm_sem, gain[:, :], g.partition_broadcast(P), state["norm_free"])
            if b is not None:
                t = p.dma("scalar", norm_sem, shift[:, :], b.partition_broadcast(P))
            return t

        def onto_x(i, half, bank, ready, scale):
            xs = x_tok[:, i, half * BANK:(half + 1) * BANK]
            c = p.dve(lambda e: e.scalar_tensor_tensor(out=xs, in0=xs, scalar=scale, in1=bank[:, :],
                                                       op0=ALU.mult, op1=ALU.add), ready, state["x"][i])
            banks.give(bank, c)
            return c

        def statistics(i, half, ready):
            return p.dve(lambda e: e.bn_stats(stat[:, i, half, :], x_tok[:, i, half * BANK:(half + 1) * BANK]), ready)

        def norm(i, ready, loaded):
            c = p.dve(lambda e: e.bn_aggr(mean_var[:, i, :], stat[:, i, :, :].rearrange("p a b -> p (a b)")), ready)
            r = inverse_root(i, 1, mean_var[:, i, 1:2], 1.0, LN_EPS, c)
            x, off = x_tok[:, i, :], root[:, i, 1:2]
            c = p.dve(lambda e: e.scalar_tensor_tensor(out=off, in0=mean_var[:, i, 0:1], scalar=-1.0,
                                                       in1=root[:, i, 0:1], op0=ALU.mult, op1=ALU.mult), r)
            c = p.act(lambda e: e.activation(x, x, ACT.Identity, scale=root[:, i, 0:1], bias=off), c)
            c = p.dve(lambda e: e.tensor_tensor(x, x, gain[:, :], ALU.mult), c, loaded)
            c = p.dve(lambda e: e.tensor_tensor(x, x, shift[:, :], ALU.add), c)
            state["x"][i] = c
            state["norm_free"] = c

        def project_out(label, kt, lhs, lhs_ready, norm_params=None, scale=ALPHA, between=None, to_T=True):
            loaded = load_norm(*norm_params) if norm_params else None
            sums = {}
            for half in range(2):
                open_ = {}
                for k0 in range(0, kt, SLOT // BANK):
                    pn = take_piece(label)
                    last = k0 + pn.kt == kt
                    for i in range(NT):
                        bank, bank_free = open_[i] if k0 else banks.take()
                        t = p.pe(product(bank[:, :], lambda k, i=i, k0=k0: lhs(k0 + k, i), pn.cols(0, BANK), pn.kt,
                                         first=(k0 == 0), last=last), pn.ready, bank_free, lhs_ready)
                        open_[i] = (bank, t)
                        if last:
                            sums[half, i] = onto_x(i, half, bank, t, scale)
                            if norm_params:
                                sums[half, i] = statistics(i, half, sums[half, i])
                            if half and norm_params:
                                norm(i, [sums[0, i], sums[1, i]], loaded)
                            elif half:
                                state["x"][i] = sums[1, i]
                    pn.release(t)
            last_read = t
            if between:
                between()
            if norm_params and to_T:
                for i in range(NT):
                    state["xT"][i] = rows_to_T(i, state["x"][i], before=last_read)
            return last_read

        p.stage("setup")
        t_first = p.dma("scalar", first_sem, ident[:, :], a["c_ident"])
        t_first = p.dma("scalar", first_sem, x_tok[:, :, :], a["x"][0].rearrange("(t p) d -> p t d", p=P))
        t_power = p.pool(lambda e: e.memset(power[:, :], -0.5))
        carve_from(8 * 256)
        angle = carve(S, parts=QKD)
        turns = carve(S, parts=QKD)
        pos_i = carve(S, parts=QKD, dt=I32)
        freq = carve(1, parts=QKD)
        ROPE_AT = WORK - 3 * S
        carve_from(ROPE_AT)
        cos_q = carve(S, parts=QKD)
        sin_q = carve(S, parts=QKD)
        mask_q = carve(S)
        for dst, src in ((pos_i, a["positions"][0].partition_broadcast(QKD)), (freq, a["c_freq"]),
                         (cols[:, :], a["cols"]), (swap_q[:, :], a["c_swap_q"]), (mask_q, a["c_mask_q"]),
                         (swap_a[:, :], a["c_swap_a"])):
            t_setup = p.dma("scalar", setup, dst, src)
        for i in range(NT):
            state["xT"][i] = rows_to_T(i, t_first)
            state["x"][i] = t_first
        look_ahead()

        t_mem = []

        def load_memory(mem_tok):
            t = p.dma("scalar", mem_sem, mem_tok, a["mem"][0].rearrange("(t p) d -> p t d", p=P))
            return lambda: [t_mem.extend(transposed(
                lambda k, m=m: mem_tok[:, m, k * P:(k + 1) * P],
                lambda b, n, m=m: memT[:, b:b + n, m * P:(m + 1) * P], KD, t)) for m in range(MT)]

        TWO_PI = 2.0 * np.pi
        PI_1 = 6.28125
        PI_2 = float(np.float32(np.round((TWO_PI - PI_1) * 2 ** 21) / 2 ** 21))
        PI_3 = float(TWO_PI - PI_1 - PI_2)
        MAGIC = 1.5 * 2 ** 23
        EDGE = 3.1415925
        t = p.dve(lambda e: e.tensor_copy(angle, pos_i), t_setup)
        t = p.dve(lambda e: e.tensor_scalar(angle, angle, freq, None, ALU.mult), t)
        t = p.dve(lambda e: e.tensor_scalar(turns, angle, 1.0 / TWO_PI, MAGIC, ALU.mult, ALU.add), t)
        t = p.dve(lambda e: e.tensor_scalar(turns, turns, MAGIC, None, ALU.subtract), t)
        for part in (PI_1, PI_2, PI_3):
            t = p.dve(lambda e, part=part: e.scalar_tensor_tensor(
                out=angle, in0=turns, scalar=-part, in1=angle, op0=ALU.mult, op1=ALU.add), t)
        t = p.dve(lambda e: e.tensor_scalar(sin_q, angle, EDGE, -EDGE, ALU.min, ALU.max), t)
        t_s = p.act(lambda e: e.activation(sin_q, sin_q, ACT.Sin), t)
        t = p.dve(lambda e: e.tensor_scalar(angle, angle, float(np.pi / 2), None, ALU.add), t)
        t = p.dve(lambda e: e.tensor_scalar(turns, angle, float(np.pi), -TWO_PI, ALU.is_gt, ALU.mult), t)
        t = p.dve(lambda e: e.tensor_tensor(angle, angle, turns, ALU.add), t)
        t = p.dve(lambda e: e.tensor_scalar(cos_q, angle, EDGE, -EDGE, ALU.min, ALU.max), t)
        t_rope = [t_s, p.act(lambda e: e.activation(cos_q, cos_q, ACT.Sin), t)]
        work_free = [t, t_rope[1]]

        def first_block_layer(layer, work_free):
            p.stage(f"mixer{layer}")
            col = lambda c, n=1, lo=0, hi=P: cols[lo:hi, layer * PC_LAYER + c:layer * PC_LAYER + c + n]
            carve_from(0)
            c_tok = carve(NT, 2 * RANK)
            cT = carve(4, S)
            k_ropeT = carve(S, parts=QKD)
            v_tok = carve(NT, HEADS * VDIM)
            gate_acc = carve(CT, S)
            PAD = TAPS - 1
            hT = carve(CT, PAD + S)
            up_q = carve(2, HEADS * QKD)
            up_kv = carve(2, HEADS * 2 * NOPE)
            heads_at = taken[0]
            heads_q = Pool_([carve(S, parts=QKD) for _ in range(2)])
            heads_k = Pool_([carve(S, parts=QKD) for _ in range(2)])
            raws = Pool_([carve(S, parts=QKD) for _ in range(2)])
            probs = Pool_([carve(S) for _ in range(3)])
            probsT = Pool_([carve(NT, P) for _ in range(3)])
            assert taken[0] <= XT_LOW_AT, taken[0] / 256
            if layer == 0:
                carve_from(heads_at)
                transpose_memory = load_memory(carve(MT, D))
            carve_from(XT_LOW_AT)
            yT = carve(KD, S)
            yT_low = [c_tok[:, k, :] for k in range(CT)] + [gate_acc[:, k, :] for k in range(CT)]
            conv_tok = v_tok
            bias_c = probsT.free[0][0].rearrange("p a b -> p (a b)")
            kr_w, kr_high = (b[:, 0:KD * ROPE] for b, _ in probs.free[0:2])
            w_in, b_in = a["mix_w_in"][layer], a["mix_b_in"][layer]

            t_bias = p.dma("scalar", side_sem, bias_c, b_in[0:BANK].partition_broadcast(P), work_free)
            t_bias = p.dma("scalar", side_sem, kr_w.rearrange("p (t n) -> p t n", t=KD),
                           w_in[:, BANK:BANK + ROPE].rearrange("(t p) n -> p t n", p=P))
            t_up = p.dma("scalar", up_sem, up_q, a["mla_w_uq"][layer].rearrange("(t p) n -> p t n", p=P))
            t_up = p.dma("scalar", up_sem, up_kv, a["mla_w_ukv"][layer].rearrange("(t p) n -> p t n", p=P))

            t_c, open_ = [], {}
            pn = take_piece("latents")
            for i in range(NT):
                open_[i] = banks.take()
                bank, bank_free = open_[i]
                t = p.pe(product(bank[:, :], x_tile(i), pn.cols(0, BANK), pn.kt, last=False), pn.ready, bank_free,
                         state["xT"][i])
            pn.release(t)
            pn = take_piece("latents")
            for i in range(NT):
                bank, _ = open_[i]
                t = p.pe(product(bank[:, :], lambda k, i=i: x_tile(i)(KD // 2 + k), pn.cols(0, BANK), pn.kt,
                                 first=False), pn.ready)
                row = c_tok[:, i, :]
                c = p.dve(lambda e, row=row, bank=bank: e.tensor_tensor(row, bank[:, :], bias_c, ALU.add),
                          t, t_bias, work_free)
                banks.give(bank, c)
                for n in range(2):
                    bank, bank_free = banks.take()
                    q = p.act(lambda e, i=i, n=n, bank=bank: e.activation(
                        bank[:, 0:RANK], c_tok[:, i, n * RANK:(n + 1) * RANK], ACT.Square,
                        accum_out=small[:, i * 2 + n:i * 2 + n + 1]), c, bank_free)
                    banks.give(bank, q)
                r = inverse_root(i, 2, small[:, i * 2:i * 2 + 2], 1.0 / RANK, RMS_EPS, q)
                for n in range(2):
                    c = p.dve(lambda e, i=i, n=n: e.tensor_scalar(
                        c_tok[:, i, n * RANK:(n + 1) * RANK], c_tok[:, i, n * RANK:(n + 1) * RANK],
                        root[:, i, n:n + 1], None, ALU.mult), r)
                t_c.append(c)
            pn.release(t)

            t = split(kr_high, kr_w, kr_w, t_bias, work_free)
            kr3, krh3 = (w.rearrange("p (t n) -> p t n", t=KD) for w in (kr_w, kr_high))
            bank, bank_free = banks.take()
            t = t_krw = p.pe(product(bank[0:ROPE, :], lambda k: (krh3[:, k, :], kr3[:, k, :]), x_all, KD),
                             t, bank_free, state["xT"])
            kr = k_ropeT[NOPE:QKD, :]
            c = p.act(lambda e, bank=bank: e.activation(kr, bank[0:ROPE, :], ACT.Copy), t, work_free)
            banks.give(bank, c)
            c = p.dve(lambda e: e.tensor_scalar(kr, kr, col(PC_KR, 1, NOPE, QKD), None, ALU.add), c)
            bank, bank_free = banks.take()
            t = p.pe(lambda e, bank=bank: e.matmul(bank[NOPE:QKD, :], swap_q[NOPE:QKD, NOPE:QKD], kr,
                                                   start=True, stop=True), c, bank_free)
            raw_k, raw_free = raws.take()
            t1 = p.dve(lambda e, bank=bank, r=raw_k: e.tensor_tensor(r[NOPE:QKD, :], bank[NOPE:QKD, :],
                                                                     sin_q[NOPE:QKD, :], ALU.mult),
                       t, raw_free, t_rope)
            banks.give(bank, t1)
            t2 = p.dve(lambda e: e.tensor_tensor(kr, kr, cos_q[NOPE:QKD, :], ALU.mult), t, t1)
            t_kr = p.dve(lambda e, r=raw_k: e.tensor_tensor(kr, kr, r[NOPE:QKD, :], ALU.add), t2)
            raws.give(raw_k, t_kr)
            probs.free[0:2] = [(b, t_krw) for b, _ in probs.free[0:2]]
            probsT.free[0] = (probsT.free[0][0], t_c[-1])

            zero = p.pool(lambda e: e.memset(hT[:, :, 0:PAD], 0.0), work_free)
            t_g = []
            for c in range(0, CT, 2):
                pn = take_piece("conv gate")
                for c4 in (c, c + 1):
                    bank, bank_free = banks.take()
                    t = p.pe(product(bank[:, :], pn.cols((c4 - c) * P, P), x_all, KD), pn.ready, bank_free)
                    s_ = p.act(lambda e, c4=c4, bank=bank: e.activation(
                        gate_acc[:, c4, :], bank[:, :], ACT.Sigmoid, bias=col(PC_UG + c4)), t, work_free)
                    banks.give(bank, s_)
                    t_g.append(s_)
                pn.release(t)
            t_h = []
            for c in range(0, CT, 2):
                pn = take_piece("conv in")
                for c4 in (c, c + 1):
                    bank, bank_free = banks.take()
                    t = p.pe(product(bank[:, :], pn.cols((c4 - c) * P, P), x_all, KD), pn.ready, bank_free)
                    s_ = p.dve(lambda e, c4=c4, bank=bank: e.scalar_tensor_tensor(
                        out=hT[:, c4, PAD:PAD + S], in0=bank[:, :], scalar=col(PC_UA + c4),
                        in1=gate_acc[:, c4, :], op0=ALU.add, op1=ALU.mult), t, t_g[c4], work_free)
                    banks.give(bank, s_)
                    t_h.append(s_)
                pn.release(t)
            x_read = t
            if layer == 0:
                transpose_memory()
                for heads in (heads_q, heads_k):
                    heads.free = [(b, t_mem) for b, _ in heads.free]

            t_cT = []
            for k in range(4):
                bank, bank_free = banks.take()

                def make(e, k=k, bank=bank):
                    for i in range(NT):
                        ins = e.transpose(bank[:, i * P:(i + 1) * P], c_tok[:, i, k * P:(k + 1) * P], ident[:, :])
                    return ins
                t = p.pe(make, bank_free, t_c)
                c = p.act(lambda e, k=k, bank=bank: e.activation(cT[:, k, :], bank[:, :], ACT.Copy,
                                                                 scale=col(PC_QN + k)), t, work_free)
                banks.give(bank, c)
                t_cT.append(c)
            c_read = t

            conv = []
            t_acc = [None] * CT
            for j in range(TAPS):
                for c4 in range(CT):
                    conv.append((j, c4))

            def convolve(n):
                for _ in range(min(n, len(conv))):
                    j, c4 = conv.pop(0)
                    src, acc, w = hT[:, c4, j:j + S], gate_acc[:, c4, :], col(PC_W + c4 * TAPS + j)
                    if j == 0:
                        t_acc[c4] = p.dve(lambda e, src=src, acc=acc, w=w, c4=c4: e.tensor_scalar(
                            acc, src, w, col(PC_DWB + c4), ALU.mult, ALU.add), t_h[c4], zero)
                    else:
                        t_acc[c4] = p.dve(lambda e, src=src, acc=acc, w=w: e.scalar_tensor_tensor(
                            out=acc, in0=src, scalar=w, in1=acc, op0=ALU.mult, op1=ALU.add), t_acc[c4])

            for i in range(NT):
                bank, bank_free = banks.take()

                def make(e, i=i, bank=bank):
                    for k in range(2):
                        ins = e.matmul(bank[:, :], cT[:, 2 + k, i * P:(i + 1) * P],
                                       up_kv[:, k, :].rearrange("p (h two d) -> p h two d", two=2, d=VDIM)[:, :, 1, :],
                                       start=(k == 0), stop=(k == 1))
                    return ins
                t = p.pe(make, t_up, bank_free, t_cT)
                t_v = evacuate(v_tok[:, i, :], bank[:, :], t, work_free, engines=("scalar",))
                banks.give(bank, t_v)

            def head_qk(h):
                q, q_free = heads_q.take()
                k_, k_free = heads_k.take()
                raw, raw_free = raws.take()
                bank, bank_free = banks.take()
                t = p.pe(product(bank[0:QKD, :], lambda k: up_q[:, k, h * QKD:(h + 1) * QKD],
                                 lambda k: cT[:, k, :], 2), t_up, bank_free, t_cT)
                c = p.act(lambda e: e.activation(raw, bank[0:QKD, :], ACT.Copy), t, raw_free)
                banks.give(bank, c)
                bank3, bank_free = banks.take()
                t_keys = p.pe(product(bank3[0:NOPE, :], lambda k: up_kv[:, k, h * 2 * NOPE:(2 * h + 1) * NOPE],
                                 lambda k: cT[:, 2 + k, :], 2), bank_free)
                c_k = p.act(lambda e: e.activation(k_[0:NOPE, :], bank3[0:NOPE, :], ACT.Copy), t_keys, k_free)
                banks.give(bank3, c_k)
                bank2, bank_free = banks.take()
                t = p.pe(lambda e: e.matmul(bank2[0:QKD, :], swap_q[:, :], raw, start=True, stop=True), c, bank_free)
                t1 = p.dve(lambda e: e.tensor_tensor(q, bank2[0:QKD, :], sin_q, ALU.mult), t, q_free)
                banks.give(bank2, t1)
                t2 = p.pool(lambda e: e.tensor_tensor(raw, raw, cos_q, ALU.mult), t)
                t_q = p.dve(lambda e: e.tensor_tensor(q, q, raw, ALU.add), t1, t2)
                raws.give(raw, t_q)
                c2 = p.pool(lambda e: e.tensor_copy(k_[NOPE:QKD, :], kr), t_kr, k_free)
                return q, k_, [t_q, c_k, c2]

            steps = [(h, i) for h in range(HEADS) for i in range(NT)]
            qk, live, acc_bank = {}, {}, {}
            t_y = []
            for n in range(len(steps) + 4):
                if n < len(steps):
                    h, i = steps[n]
                    if n == 0:
                        qk[h] = head_qk(h)
                    if i == 1 and h + 1 < HEADS:
                        qk[h + 1] = head_qk(h + 1)
                    q, k_, ready = qk[h]
                    end = (i + 1) * P
                    bank, bank_free = banks.take()
                    t = p.pe(lambda e, bank=bank, q=q, k_=k_, i=i, end=end: e.matmul(
                        bank[:, 0:end], q[:, i * P:end], k_[:, 0:end], start=True, stop=True), ready, bank_free)
                    if i == NT - 1:
                        heads_q.give(q, t)
                        heads_k.give(k_, t)
                    pr, pr_free = probs.take()
                    st = small[:, 8 + 4 * (n % 4):12 + 4 * (n % 4)]
                    c = p.dve(lambda e, pr=pr, bank=bank, end=end, st=st: e.tensor_tensor_reduce(
                        out=pr[:, 0:end], in0=bank[:, 0:end], in1=mask_q[:, S - end:S], scale=1.0, scalar=NEG,
                        op0=ALU.add, op1=ALU.max, accum_out=st[:, 0:1]), t, pr_free)
                    banks.give(bank, c)
                    c = p.dve(lambda e, st=st: e.tensor_scalar(st[:, 1:2], st[:, 0:1], -(QKD ** -0.5), None,
                                                               ALU.mult), c)
                    c = p.act(lambda e, pr=pr, end=end, st=st: e.activation(
                        pr[:, 0:end], pr[:, 0:end], ACT.Exp, bias=st[:, 1:2], scale=QKD ** -0.5,
                        accum_out=st[:, 2:3]), c)
                    live[n] = [pr, st, c]
                if 1 <= n <= len(steps):
                    h, i = steps[n - 1]
                    end = (i + 1) * P
                    pr, st, c = live[n - 1]
                    c = p.dve(lambda e, st=st: e.reciprocal(st[:, 3:4], st[:, 2:3]), c)
                    c = p.act(lambda e, pr=pr, st=st, end=end: e.activation(
                        pr[:, 0:end], pr[:, 0:end], ACT.Copy, scale=st[:, 3:4]), c)
                    live[n - 1][2] = c
                if 2 <= n <= len(steps) + 1:
                    h, i = steps[n - 2]
                    pr, st, c = live[n - 2]
                    bank, bank_free = banks.take()
                    pt, pt_free = probsT.take()

                    def make(e, pr=pr, bank=bank, i=i):
                        for j in range(i + 1):
                            ins = e.transpose(bank[:, j * P:(j + 1) * P], pr[:, j * P:(j + 1) * P], ident[:, :])
                        return ins
                    t = p.pe(make, c, bank_free)
                    probs.give(pr, t)
                    c = p.act(lambda e, pt=pt, bank=bank, i=i: e.activation(
                        pt[:, 0:i + 1, :], bank[:, 0:(i + 1) * P].rearrange("p (j c) -> p j c", c=P), ACT.Copy),
                        t, pt_free)
                    banks.give(bank, c)
                    live[n - 2] += [pt, c]
                if 3 <= n <= len(steps) + 2:
                    h, i = steps[n - 3]
                    pt, c = live[n - 3][3:]
                    if i == 0 and h % 2 == 0:
                        acc_bank[h // 2] = banks.take()
                    bank, bank_free = acc_bank[h // 2]
                    row = (h % 2) * VDIM

                    def make(e, pt=pt, i=i, h=h, row=row, bank=bank):
                        for j in range(i + 1):
                            ins = e.matmul(bank[row:row + VDIM, i * P:(i + 1) * P],
                                           v_tok[:, j, h * VDIM:(h + 1) * VDIM], pt[:, j, :],
                                           start=(j == 0), stop=(j == i))
                        return ins
                    t = p.pe(make, c, bank_free, t_v)
                    probsT.give(pt, t)
                    if i == NT - 1 and h % 2 == 1:
                        t_y.append(split(yT[:, h // 2, :], yT_low[h // 2], bank[:, :], t, x_read, c_read))
                        banks.give(bank, t_y[-1])
                    del live[n - 3]
                convolve(3)
            values_read = t

            carve_from(XT_LOW_AT - KD * MEM)
            mem_kT = carve(KD, MEM)
            carve_from(8 * 256)
            mem_v = carve(MT, D)
            t_kv = []
            p.stage(f"cross{layer}")
            for n in range(KD // 2):
                pn = take_piece("memory keys")
                for c in (2 * n, 2 * n + 1):
                    bank, bank_free = banks.take()
                    t = p.pe(product(bank[:, 0:MEM], pn.cols((c - 2 * n) * P, P), lambda k: memT[:, k, :], KD),
                             pn.ready, bank_free, t_mem)
                    t_kv.append(evacuate(mem_kT[:, c, :], bank[:, 0:MEM], t, values_read, engines=("scalar",)))
                    banks.give(bank, t_kv[-1])
                    convolve(3)
                pn.release(t)
            convolve(len(conv))

            t_z = []
            for i in range(NT):
                bank, bank_free = banks.take()

                def make(e, i=i, bank=bank):
                    for c4 in range(CT):
                        ins = e.transpose(bank[:, c4 * P:(c4 + 1) * P], gate_acc[:, c4, i * P:(i + 1) * P],
                                          ident[:, :])
                    return ins
                t = p.pe(make, bank_free, t_acc)
                c = p.dve(lambda e, i=i, bank=bank: e.bn_stats(stat[:, i, 0, :], bank[:, :]), t)
                c = p.dve(lambda e, i=i: e.bn_aggr(mean_var[:, i, :], stat[:, i, 0, :]), c)
                r = inverse_root(i, 1, mean_var[:, i, 1:2], 1.0, LN_EPS, c)
                c = p.dve(lambda e, i=i, bank=bank: e.tensor_scalar(
                    conv_tok[:, i, :], bank[:, :], mean_var[:, i, 0:1], root[:, i, 0:1], ALU.subtract, ALU.mult),
                    r, values_read)
                banks.give(bank, c)
                t_z.append(c)
            for c4 in range(CT):
                bank, bank_free = banks.take()

                def make(e, c4=c4, bank=bank):
                    for i in range(NT):
                        ins = e.transpose(bank[:, i * P:(i + 1) * P], conv_tok[:, i, c4 * P:(c4 + 1) * P],
                                          ident[:, :])
                    return ins
                t = p.pe(make, bank_free, t_z)
                low = yT_low[CT + c4]
                c = p.act(lambda e, c4=c4, bank=bank, low=low: e.activation(
                    low, bank[:, :], ACT.Silu, bias=col(PC_CNB + c4), scale=col(PC_CNG + c4)), t)
                banks.give(bank, c)
                t_y.append(split(yT[:, CT + c4, :], low, low, c))

            after_attention = [t_y[CT - 1], t_y[-1], t]

            def memory_values():
                for n in range(2):
                    open_ = [banks.take() for m in range(MT)]
                    for k0 in (0, KD // 2):
                        pn = take_piece("memory values")
                        for m, (bank, bank_free) in enumerate(open_):
                            t = p.pe(product(bank[:, :], lambda k, m=m, k0=k0: tok_of(memT, m)(k0 + k),
                                             pn.cols(0, BANK), pn.kt, first=(k0 == 0), last=(k0 > 0)),
                                     pn.ready, bank_free)
                            if k0:
                                t_kv.append(evacuate(mem_v[:, m, n * BANK:(n + 1) * BANK], bank[:, :], t,
                                                     after_attention, engines=("scalar",)))
                                banks.give(bank, t_kv[-1])
                        pn.release(t)

            project_out("mix out", KD, lambda k, i: (yT[:, k, i * P:(i + 1) * P], yT_low[k][:, i * P:(i + 1) * P]), t_y,
                        (a["ln1_g"][layer], a["ln1_b"][layer]), between=memory_values)
            y_read = state["xT"][-1]

            carve_from(16 * 256)
            qT = carve(KD, S)
            oT, oT_low = carve(KD, S), carve(KD, S)
            xprobs = Pool_([carve(MEM) for _ in range(4)])
            xprobsT = Pool_([carve(MT, S) for _ in range(2)])
            assert taken[0] <= XT_LOW_AT
            t_q = []
            for n in range(KD // 2):
                pn = take_piece("cross query")
                for c in (2 * n, 2 * n + 1):
                    bank, bank_free = banks.take()
                    t = p.pe(product(bank[:, :], pn.cols((c - 2 * n) * P, P), x_all, KD),
                             pn.ready, bank_free, state["xT"])
                    t_q.append(evacuate(qT[:, c, :], bank[:, :], t, y_read))
                    banks.give(bank, t_q[-1])
                pn.release(t)
            steps = [(h, i) for h in range(XH) for i in range(NT)]
            live, head_T, t_o = {}, {}, []
            for n in range(len(steps) + 3):
                if n < len(steps):
                    h, i = steps[n]
                    bank, bank_free = banks.take()

                    def make(e, h=h, i=i, bank=bank):
                        for k in range(2):
                            ins = e.matmul(bank[:, 0:MEM], qT[:, 2 * h + k, i * P:(i + 1) * P],
                                           mem_kT[:, 2 * h + k, :], start=(k == 0), stop=(k == 1))
                        return ins
                    t = p.pe(make, bank_free, t_q[2 * h:2 * h + 2], t_kv)
                    pr, pr_free = xprobs.take()
                    st = small[:, 24 + 4 * (n % 4):28 + 4 * (n % 4)]
                    c = p.dve(lambda e, bank=bank, st=st: e.tensor_reduce(
                        st[:, 0:1], bank[:, 0:MEM], AX.X, ALU.max), t)
                    c = p.dve(lambda e, st=st: e.tensor_scalar(st[:, 1:2], st[:, 0:1], -(XHD ** -0.5), None,
                                                               ALU.mult), c)
                    c = p.act(lambda e, pr=pr, bank=bank, st=st: e.activation(
                        pr, bank[:, 0:MEM], ACT.Exp, bias=st[:, 1:2], scale=XHD ** -0.5,
                        accum_out=st[:, 2:3]), c, pr_free, y_read)
                    banks.give(bank, c)
                    live[n] = [pr, st, c]
                if 1 <= n <= len(steps):
                    pr, st, c = live[n - 1]
                    c = p.dve(lambda e, st=st: e.reciprocal(st[:, 3:4], st[:, 2:3]), c)
                    c = p.dve(lambda e, pr=pr, st=st: e.tensor_scalar(pr, pr, st[:, 3:4], None, ALU.mult), c)
                    live[n - 1][2] = c
                if 2 <= n <= len(steps) + 1:
                    h, i = steps[n - 2]
                    pr, st, c = live.pop(n - 2)
                    bank, bank_free = banks.take()
                    if i == 0:
                        head_T[h] = [*xprobsT.take(), []]
                    pt, pt_free, written = head_T[h]

                    def make(e, pr=pr, bank=bank):
                        for m in range(MT):
                            ins = e.transpose(bank[:, m * P:(m + 1) * P], pr[:, m * P:(m + 1) * P], ident[:, :])
                        return ins
                    t = p.pe(make, c, bank_free)
                    xprobs.give(pr, t)
                    c = evacuate(pt[:, :, i * P:(i + 1) * P], bank[:, 0:MEM].rearrange("p (m c) -> p m c", m=MT),
                                 t, pt_free)
                    banks.give(bank, c)
                    written.append(c)
                    if i == NT - 1:
                        for v in range(2):
                            bank, bank_free = banks.take()

                            def make(e, h=h, v=v, bank=bank, pt=pt):
                                for m in range(MT):
                                    ins = e.matmul(bank[:, :], mem_v[:, m, h * XHD + v * P:h * XHD + (v + 1) * P],
                                                   pt[:, m, :], start=(m == 0), stop=(m == MT - 1))
                                return ins
                            t = p.pe(make, bank_free, written)
                            t_o.append(split(oT[:, 2 * h + v, :], oT_low[:, 2 * h + v, :], bank[:, :], t, y_read))
                            banks.give(bank, t_o[-1])
                        xprobsT.give(pt, t)
            project_out("cross out", KD, lambda k, i: (tok_of(oT, i)(k), tok_of(oT_low, i)(k)), t_o,
                        (a["ln2_g"][layer], a["ln2_b"][layer]))
            work_free = state["xT"][-1]

            p.stage(f"ffn{layer}")
            carve_from(0)
            FH = FT // 2
            hidT, hidT_low = carve(FH, S), carve(FH, S)
            gated = Pool_([carve(S) for _ in range(4)])
            assert taken[0] <= XT_LOW_AT
            hid_read = work_free
            for f0, f1 in FFN_HALVES:
                t_hid = []
                for f in range(f0, f1, 2):
                    both = range(f, min(f + 2, f1))
                    pn, gates_ = take_piece("ffn gate"), {}
                    for c in both:
                        bank, bank_free = banks.take()
                        t = p.pe(product(bank[:, :], pn.cols((c - f) * P, P), x_all, KD),
                                 pn.ready, bank_free, state["xT"])
                        g, g_free = gated.take()
                        s_ = p.act(lambda e, g=g, bank=bank: e.activation(g, bank[:, :], ACT.Silu),
                                   t, g_free, work_free)
                        banks.give(bank, s_)
                        gates_[c] = (g, s_)
                    pn.release(t)
                    pn = take_piece("ffn up")
                    for c in both:
                        bank, bank_free = banks.take()
                        t = p.pe(product(bank[:, :], pn.cols((c - f) * P, P), x_all, KD), pn.ready, bank_free)
                        g, s_ = gates_[c]
                        low = hidT_low[:, c - f0, :]
                        s_ = p.dve(lambda e, g=g, bank=bank, low=low: e.tensor_tensor(low, g, bank[:, :], ALU.mult),
                                   s_, t, hid_read)
                        banks.give(bank, s_)
                        gated.give(g, s_)
                        t_hid.append(split(hidT[:, c - f0, :], low, low, s_))
                    pn.release(t)
                first = f0 == 0
                hid_read = project_out(
                    "ffn down", f1 - f0, lambda k, i: (tok_of(hidT, i)(k), tok_of(hidT_low, i)(k)), t_hid,
                    None if first else (a["ln3_g"][layer], a["ln3_b"][layer]),
                    scale=ALPHA if first else 1.0, to_T=(layer + 1 < DEPTH))
            return [hid_read, state["xT"]]

        for layer in range(DEPTH):
            work_free = first_block_layer(layer, work_free)

        def rms_rows(i, out_row, loaded, *row_free, gain=gain):
            q = p.act(lambda e: e.activation(out_row, x_tok[:, i, :], ACT.Square,
                                             accum_out=small[:, 40 + i:41 + i]), state["x"][i], *row_free)
            r = inverse_root(i, 1, small[:, 40 + i:41 + i], 1.0 / D, RMS_EPS, q)
            c = p.dve(lambda e: e.scalar_tensor_tensor(out=out_row, in0=x_tok[:, i, :], scalar=root[:, i, 0:1],
                                                       in1=gain[:, :], op0=ALU.mult, op1=ALU.mult), r, loaded)
            state["norm_free"] = c
            return c

        def dilated_attention(work_free):
            p.stage("attention")
            carve_from(0)
            y_attT = carve(NT, S)
            masks = carve(NT * S + 2 * P, dt=BF16)
            cos_a, sin_a = carve(S), carve(S)
            raws = Pool_([carve(S) for _ in range(2)])
            probs = Pool_([carve(6 * P) for _ in range(3)])
            probsT = Pool_([carve(6, P) for _ in range(2)])
            pair_at = taken[0]
            qs = Pool_([carve(NG, S) for _ in range(2)])
            ks = Pool_([carve(NG, S) for _ in range(2)])
            vs = Pool_([carve(NT, NG * P) for _ in range(2)])
            carve_from(pair_at)
            xn_tok = carve(NT, D)
            assert taken[0] <= 64 * 256
            carve_from(64 * 256)
            mix_gain = carve(D)
            loaded = p.dma("sync", p.semaphore("mix_gain_load"), mix_gain, a["norm_mix_w_2"][0].partition_broadcast(P), state["xT"])
            t_const = p.dma("scalar", side_sem, masks.bitcast(mybir.dt.uint16), a["c_mask_a"], work_free)
            t_const = p.dma("scalar", side_sem, cos_a, a["c_cos_a"])
            t_const = p.dma("scalar", side_sem, sin_a, a["c_sin_a"])
            t_x = []
            for i in range(NT):
                n = rms_rows(i, xn_tok[:, i, :], loaded, work_free, gain=mix_gain)
                for b in range(0, KD, 4):
                    bank, bank_free = banks.take()

                    def make(e, b=b, i=i, bank=bank):
                        for j in range(4):
                            ins = e.transpose(bank[:, j * P:(j + 1) * P], xn_tok[:, i, (b + j) * P:(b + j + 1) * P],
                                              ident[:, :])
                        return ins
                    t = p.pe(make, bank_free, n)
                    high, low = (x[:, b:b + 4, :].rearrange("p j (r a) -> p j r a", r=DIL)[:, :, :, i * 32:(i + 1) * 32]
                                 for x in (xT, xT_low))
                    src = bank[:, :].rearrange("p (j a r) -> p j r a", j=4, r=DIL)
                    c = split(high, low, src, t, work_free)
                    banks.give(bank, c)
                    t_x.append(c)
            xn_read = t

            swaps = []

            def rotated(buf, buf_free, g, w, ready_, done):
                bank, bank_free = banks.take()
                t = p.pe(product(bank[:, :], w, x_all, KD), ready_, bank_free, t_x)
                raw, raw_free = raws.take()
                c = p.act(lambda e: e.activation(raw, bank[:, :], ACT.Copy), t, raw_free)
                banks.give(bank, c)

                def rotate():
                    bank2, bank_free = banks.take()
                    t2 = p.pe(lambda e: e.matmul(bank2[:, :], swap_a[:, :], raw, start=True, stop=True), c, bank_free)
                    t1 = p.dve(lambda e: e.tensor_tensor(buf[:, g, :], bank2[:, :], sin_a, ALU.mult),
                               t2, buf_free, t_const)
                    banks.give(bank2, t1)
                    m = p.pool(lambda e: e.tensor_tensor(raw, raw, cos_a, ALU.mult), t2, t_const)
                    c2 = p.dve(lambda e: e.tensor_tensor(buf[:, g, :], buf[:, g, :], raw, ALU.add), t1, m)
                    raws.give(raw, c2)
                    done.append(c2)
                swaps.append(rotate)
                return t

            ready = {}

            def projections(pair):
                ready[pair] = ([None] * 3, [])
                state_ = {}

                def qk_tile(n):
                    kind, g = n // NG, n % NG
                    if n % 2 == 0:
                        state_["pn"] = take_piece("attention qk")
                    if g == 0:
                        ready[pair][0][kind], state_["free"] = (qs, ks)[kind].take()
                    pn = state_["pn"]
                    before = swaps.pop() if swaps else None
                    t = rotated(ready[pair][0][kind], [state_["free"], xn_read], g,
                                pn.cols(n % 2 * P, P), pn.ready, ready[pair][1])
                    if before:
                        before()
                    if n % 2:
                        pn.release(t)

                def v_tile(half, i):
                    if i == 0:
                        state_["pn"] = take_piece("attention v")
                    if half == 0 and i == 0:
                        ready[pair][0][2], state_["free"] = vs.take()
                    pn, v = state_["pn"], ready[pair][0][2]
                    bank, bank_free = banks.take()
                    t = p.pe(product(bank[:, 0:VCOLS], x_tile(i), pn.cols(0, VCOLS), KD), pn.ready, bank_free)
                    if swaps:
                        swaps.pop()()
                    c = p.act(lambda e: e.activation(v[:, i, half * VCOLS:(half + 1) * VCOLS], bank[:, 0:VCOLS],
                                                     ACT.Copy), t, state_["free"], xn_read)
                    banks.give(bank, c)
                    ready[pair][1].append(c)
                    if i == NT - 1:
                        pn.release(t)

                return ([lambda n=n: qk_tile(n) for n in range(2 * NG)]
                        + [lambda h=h, i=i: v_tile(h, i) for h in range(2) for i in range(NT)])

            for piece in projections(0):
                piece()
            later = []
            steps = [(pair, hh, r) for pair in range(4) for hh in range(2) for r in range(DIL)]
            live, acc, t_y = {}, {}, []
            for n in range(len(steps) + 4):
                if n < len(steps):
                    pair, hh, r = steps[n]
                    if hh == 0 and r == 0:
                        assert not later
                        later = projections(pair + 1) if pair + 1 < 4 else []
                    (q, k_, v), t_qkv = ready[pair]
                    lo = hh * AHD
                    near, near_free = banks.take()
                    far, far_free = banks.take()

                    def make(e, q=q, k_=k_, r=r, lo=lo, near=near, far=far):
                        mine = slice(r * P, (r + 1) * P)
                        e.matmul(near[:, :], q[lo:lo + AHD, 0, mine], k_[lo:lo + AHD, 0, :], start=True, stop=True)
                        for g in (1, 2):
                            ins = e.matmul(far[:, (g - 1) * P:g * P], q[lo:lo + AHD, g, mine],
                                           k_[lo:lo + AHD, g, mine], start=True, stop=True)
                        return ins
                    t = p.pe(make, t_qkv, near_free, far_free)
                    if hh == 1 and r == DIL - 1:
                        qs.give(q, t)
                        ks.give(k_, t)
                    pr, pr_free = probs.take()
                    st = small[:, 4 * (n % 4):4 * (n % 4) + 4]
                    c = p.dve(lambda e, pr=pr, near=near, r=r, st=st: e.tensor_tensor_reduce(
                        out=pr[:, 0:S], in0=near[:, :], in1=masks[:, r * S:(r + 1) * S], scale=1.0, scalar=NEG,
                        op0=ALU.add, op1=ALU.max, accum_out=st[:, 0:1]), t, pr_free, t_const)
                    banks.give(near, c)
                    c = p.dve(lambda e, pr=pr, far=far, st=st: e.tensor_tensor_reduce(
                        out=pr[:, S:6 * P], in0=far[:, 0:2 * P], in1=masks[:, NT * S:], scale=1.0,
                        scalar=st[:, 0:1], op0=ALU.add, op1=ALU.max, accum_out=st[:, 1:2]), c)
                    banks.give(far, c)
                    c = p.dve(lambda e, st=st: e.tensor_scalar(st[:, 2:3], st[:, 1:2], -(AHD ** -0.5), None,
                                                               ALU.mult), c)
                    c = p.act(lambda e, pr=pr, st=st: e.activation(
                        pr, pr, ACT.Exp, bias=st[:, 2:3], scale=AHD ** -0.5, accum_out=st[:, 3:4]), c)
                    live[n] = [pr, st, c]
                if 1 <= n <= len(steps):
                    pr, st, c = live[n - 1]
                    c = p.dve(lambda e, st=st: e.reciprocal(st[:, 0:1], st[:, 3:4]), c)
                    c = p.dve(lambda e, pr=pr, st=st: e.tensor_scalar(pr, pr, st[:, 0:1], None, ALU.mult), c)
                    live[n - 1][2] = c
                if later:
                    later.pop(0)()
                if 2 <= n <= len(steps) + 1:
                    pr, st, c = live[n - 2]
                    pt, pt_free = probsT.take()
                    got = []
                    for b, m in ((0, 4), (4, 2)):
                        bank, bank_free = banks.take()

                        def make(e, pr=pr, bank=bank, b=b, m=m):
                            for j in range(m):
                                ins = e.transpose(bank[:, j * P:(j + 1) * P], pr[:, (b + j) * P:(b + j + 1) * P],
                                                  ident[:, :])
                            return ins
                        t = p.pe(make, c, bank_free)
                        got.append(p.act(lambda e, pt=pt, bank=bank, b=b, m=m: e.activation(
                            pt[:, b:b + m, :], bank[:, 0:m * P].rearrange("p (j c) -> p j c", j=m), ACT.Copy),
                            t, pt_free))
                        banks.give(bank, got[-1])
                    probs.give(pr, t)
                    live[n - 2] += [pt, got]
                if later:
                    later.pop(0)()
                if 3 <= n <= len(steps) + 2:
                    pair, hh, r = steps[n - 3]
                    pt, got = live.pop(n - 3)[3:]
                    v = ready[pair][0][2]
                    if hh == 0 and r == 0:
                        acc[pair] = banks.take()
                    bank, bank_free = acc[pair]
                    lo = hh * AHD

                    def make(e, pt=pt, v=v, r=r, lo=lo, bank=bank):
                        tiles = [(0, 0), (0, 1), (0, 2), (0, 3), (1, r), (2, r)]
                        for j, (g, kt_) in enumerate(tiles):
                            ins = e.matmul(bank[lo:lo + AHD, r * P:(r + 1) * P],
                                           v[:, kt_, g * P + lo:g * P + lo + AHD], pt[:, j, :],
                                           start=(j == 0), stop=(j == 5))
                        return ins
                    t = p.pe(make, got, bank_free)
                    probsT.give(pt, t)
                    if hh == 1 and r == DIL - 1:
                        vs.give(v, t)
                        c = p.act(lambda e, dst=y_attT[:, pair, :], bank=bank: e.activation(
                            dst, bank[:, :], ACT.Copy), t, work_free)
                        banks.give(bank, c)
                        t_y.append(c)
            return y_attT, t_y, t_x

        def retention(y_att_at, t_x, work_free):
            p.stage("retention")
            carve_from(y_att_at)
            y_ret = carve(NT, D)
            qr_at = taken[0]
            q_r, k_r = carve(4, S), carve(4, S)
            v_r = carve(NT, D)
            weigh = carve(7, S)
            WIDE = S + (NT - 1) * P
            ahead, behind, twice = (carve(WIDE, dt=F16) for _ in range(3))
            tables = Pool_([carve(WIDE) for _ in range(2)])
            raws = Pool_([weigh[:, j, :] for j in range(2)])
            cos_r, sin_r = weigh[:, 2, :], weigh[:, 3, :]
            lg = small[:, 44:60]

            t_const = p.dma("scalar", side_sem, ahead, a["c_ahead"], work_free)
            for dst, src in ((behind, a["c_behind"]), (twice, a["c_twice"]), (cos_r, a["c_cos_a"]),
                             (sin_r, a["c_sin_a"])):
                t_const = p.dma("scalar", side_sem, dst, src)
            t_const = t_dec = p.dma("scalar", side_sem, root[:, 0:2, :], a["decays"].partition_broadcast(P), work_free)
            loaded = load_norm(a["ret_gn_w_2"][0], None)

            d_ = root[:, 0:2, :].rearrange("p a b -> p (a b)")
            sc = tables.free[0][0]
            y_, u_, l_, e_, m_ = (sc[:, j * 16:(j + 1) * 16] for j in range(5))
            t = p.dve(lambda e: e.scalar_tensor_tensor(out=y_, in0=d_, scalar=-1.0, in1=d_, op0=ALU.mult, op1=ALU.min), t_dec, work_free)
            t = p.act(lambda e: e.activation(y_, y_, ACT.Exp), t)
            t = p.dve(lambda e: e.tensor_scalar(u_, y_, 1.0, None, ALU.add), t)
            tl = p.act(lambda e: e.activation(l_, u_, ACT.Ln), t)
            t = p.dve(lambda e: e.tensor_scalar(e_, u_, 1.0, None, ALU.is_equal), t)
            t = p.dve(lambda e: e.scalar_tensor_tensor(out=m_, in0=u_, scalar=-1.0, in1=e_, op0=ALU.add,
                                                       op1=ALU.add), t)
            t = p.dve(lambda e: e.reciprocal(m_, m_), t)
            t = p.dve(lambda e: e.tensor_tensor(l_, l_, e_, ALU.add), t, tl)
            t = p.dve(lambda e: e.tensor_tensor(l_, l_, m_, ALU.mult), t)
            t = p.dve(lambda e: e.tensor_tensor(l_, l_, y_, ALU.mult), t)
            t_lg = p.dve(lambda e: e.scalar_tensor_tensor(out=lg, in0=d_, scalar=0.0, in1=l_, op0=ALU.min,
                                                          op1=ALU.subtract), t)
            tables.free[0] = (sc, t_lg)

            t_yr = {}
            def tokens_by(label, done):
                for n in range(2):
                    open_ = [banks.take() for i in range(NT)]
                    for k0 in (0, KD // 2):
                        pn = take_piece(label)
                        for i, (bank, bank_free) in enumerate(open_):
                            t = p.pe(product(bank[:, :], lambda k, i=i, k0=k0: x_tile(i)(k0 + k),
                                             pn.cols(0, BANK), pn.kt, first=(k0 == 0), last=(k0 > 0)),
                                     pn.ready, bank_free, t_x)
                            if k0:
                                banks.give(bank, done(n, i, bank, t))
                        pn.release(t)

            def gate_done(n, i, bank, t):
                dst = y_ret[:, i, n * BANK:(n + 1) * BANK]
                c = p.act(lambda e: e.activation(dst, bank[:, :], ACT.Silu), t, work_free)
                t_yr[i, n] = p.dve(lambda e: e.tensor_tensor(dst, dst, gain[:, n * BANK:(n + 1) * BANK], ALU.mult),
                                   c, loaded)
                return c

            tokens_by("retention gate", gate_done)
            state["norm_free"] = t_yr[NT - 1, 1]
            t_qk = []
            for label, buf in (("retention q", q_r), ("retention k", k_r)):
                for c4 in range(4):
                    if c4 % 2 == 0:
                        pn = take_piece(label)
                    bank, bank_free = banks.take()
                    t = p.pe(product(bank[:, :], pn.cols(c4 % 2 * P, P), x_all, KD), pn.ready, bank_free)
                    if c4 % 2:
                        pn.release(t)
                    raw, raw_free = raws.take()
                    c = p.act(lambda e, raw=raw, bank=bank: e.activation(raw, bank[:, :], ACT.Copy), t, raw_free,
                              work_free)
                    banks.give(bank, c)
                    bank2, bank_free = banks.take()
                    t2 = p.pe(lambda e, raw=raw, bank2=bank2: e.matmul(bank2[:, :], swap_a[:, :], raw, start=True,
                                                                      stop=True), c, bank_free)
                    t1 = p.dve(lambda e, dst=buf[:, c4, :], bank2=bank2: e.tensor_tensor(
                        dst, bank2[:, :], sin_r, ALU.mult), t2, work_free, t_const)
                    banks.give(bank2, t1)
                    m = p.pool(lambda e, raw=raw: e.tensor_tensor(raw, raw, cos_r, ALU.mult), t2, t_const)
                    c = p.dve(lambda e, dst=buf[:, c4, :], raw=raw: e.tensor_tensor(dst, dst, raw, ALU.add), t1, m)
                    raws.give(raw, c)
                    t_qk.append(c)
            t_v = []

            def value_done(n, i, bank, t):
                t_v.append(p.act(lambda e: e.activation(v_r[:, i, n * BANK:(n + 1) * BANK], bank[:, :], ACT.Copy),
                                 t, work_free))
                return t_v[-1]

            tokens_by("retention v", value_done)

            def decay_table(h):
                tab, tab_free = tables.take()
                t = p.dve(lambda e: e.tensor_scalar(tab, behind, lg[:, 8 + h:9 + h], None, ALU.mult),
                          tab_free, t_const, t_lg)
                t = p.dve(lambda e: e.scalar_tensor_tensor(out=tab, in0=ahead, scalar=lg[:, h:h + 1], in1=tab,
                                                           op0=ALU.mult, op1=ALU.add), t)
                t = p.act(lambda e: e.activation(tab, tab, ACT.Exp), t)
                return tab, p.dve(lambda e: e.tensor_tensor(tab, tab, twice, ALU.mult), t)

            weighs = Pool_([weigh[:, j, :] for j in range(7)])
            scored = {}

            def scores(h, j, tab, t_tab):
                lo = (h % 2) * RQK
                bank, bank_free = banks.take()
                t = p.pe(lambda e: e.matmul(bank[:, :], k_r[lo:lo + RQK, h // 2, j * P:(j + 1) * P],
                                            q_r[lo:lo + RQK, h // 2, :], start=True, stop=True), bank_free, t_qk)
                at = (NT - 1 - j) * P
                w, w_free = weighs.take()
                c = p.dve(lambda e: e.tensor_tensor(w, bank[:, :], tab[:, at:at + S], ALU.mult),
                          t, t_tab, w_free, t_qk)
                banks.give(bank, c)
                scored[h].append((w, c))
                if j == NT - 1:
                    tables.give(tab, c)

            t_out = []
            table = decay_table(0)
            scored[0] = []
            for j in range(NT):
                scores(0, j, *table)
            table = decay_table(1)
            for h in range(RH):
                if h + 1 < RH:
                    scored[h + 1] = []
                    for j in range(NT - 1):
                        scores(h + 1, j, *table)
                mine = scored.pop(h)
                bank, bank_free = banks.take()
                for i in range(NT):
                    def make(e, i=i, h=h, bank=bank, mine=mine):
                        for j, (w, _) in enumerate(mine):
                            ins = e.matmul(bank[:, i * P:(i + 1) * P], w[:, i * P:(i + 1) * P],
                                           v_r[:, j, h * RV:(h + 1) * RV], start=(j == 0), stop=(j == NT - 1))
                        return ins
                    t = p.pe(make, [c for _, c in mine], bank_free, t_v)
                for w, _ in mine:
                    weighs.give(w, t)
                t_weigh = t
                if h + 1 < RH:
                    scores(h + 1, NT - 1, *table)
                for i in range(NT):
                    c = p.dve(lambda e, i=i, bank=bank: e.bn_stats(stat[:, i, 0, :], bank[:, i * P:(i + 1) * P]), t)
                    c = p.dve(lambda e, i=i: e.bn_aggr(mean_var[:, i, :], stat[:, i, 0, :]), c)
                rt = root[:, h % 4, 0:NT]
                c = p.dve(lambda e, rt=rt: e.tensor_scalar(rt, mean_var[:, :, 1], RMS_EPS, None, ALU.add), c, t_lg)
                r_ = p.pool(lambda e, rt=rt: e.tensor_tensor(rt, rt, power[:, 0:NT], ALU.pow), c)
                for i in range(NT):
                    dst = y_ret[:, i, h * RV:(h + 1) * RV]
                    c = p.dve(lambda e, i=i, dst=dst, bank=bank: e.scalar_tensor_tensor(
                        out=dst, in0=bank[:, i * P:(i + 1) * P], scalar=mean_var[:, i, 0:1], in1=dst,
                        op0=ALU.subtract, op1=ALU.mult), t_yr[i, h // 4], t)
                    c = p.dve(lambda e, i=i, dst=dst, rt=rt: e.tensor_scalar(dst, dst, rt[:, i:i + 1], None,
                                                                            ALU.mult), c, r_)
                banks.give(bank, c)
                t_out.append(c)
                if h + 2 < RH:
                    table = decay_table(h + 2)
            carve_from(qr_at)
            y_retT, y_retT_low = carve(KD, S), carve(KD, S)
            t_T = []
            for i in range(NT):
                t_T += rows_to_T(i, t_out, src=y_ret, dst=y_retT, low=y_retT_low, before=t_weigh)
            return (y_retT, y_retT_low), t_T, y_att_at, taken[0]

        def merge(y_attT, t_att, y_retT, t_ret, merged_at, merge_tail, t_x):
            p.stage("merge")
            carve_from(merged_at)
            mT = carve(KD, S)
            carve_from(merge_tail)
            mT_low = carve(KD, S)
            gates = Pool_([carve(S) for _ in range(4)])
            assert taken[0] <= XT_LOW_AT
            y_att = lambda k: y_attT[:, k, :]
            y_ret = lambda k: (y_retT[0][:, k, :], y_retT[1][:, k, :])
            t_m = []
            for c0 in range(0, KD, 2):
                halves = []
                for name, y_, ty, kt_, gc in (("attention", y_att, t_att, NT, 0), ("retention", y_ret, t_ret, KD, KD)):
                    pn, mine = take_piece(f"{name}'s gate"), []
                    for c in (c0, c0 + 1):
                        bank, bank_free = banks.take()
                        t = p.pe(product(bank[:, :], pn.cols((c - c0) * P, P), x_all, KD), pn.ready, bank_free, t_x)
                        g, g_free = gates.take()
                        bias = cols[:, PC_GATE + gc + c:PC_GATE + gc + c + 1]
                        s_ = p.act(lambda e, g=g, bank=bank, bias=bias: e.activation(
                            g, bank[:, :], ACT.Sigmoid, bias=bias), t, g_free, t_ret)
                        banks.give(bank, s_)
                        mine.append((g, s_))
                    pn.release(t)
                    pn = take_piece(f"{name}'s branch")
                    for c in (c0, c0 + 1):
                        g, s_ = mine[c - c0]
                        bank, bank_free = banks.take()
                        t = p.pe(product(bank[:, :], pn.cols((c - c0) * P, P), y_, kt_), pn.ready, bank_free, ty)
                        s_ = p.dve(lambda e, g=g, bank=bank: e.tensor_tensor(g, g, bank[:, :], ALU.mult), s_, t)
                        banks.give(bank, s_)
                        halves.append((g, s_))
                    pn.release(t)
                for c in (c0, c0 + 1):
                    (g0, s0), (g1, s1) = halves[c - c0], halves[2 + c - c0]
                    low = mT_low[:, c, :].rearrange("p (a r) -> p r a", r=DIL)
                    b0, b1 = (g.rearrange("p (r a) -> p r a", r=DIL) for g in (g0, g1))
                    s_ = p.dve(lambda e, low=low, b0=b0, b1=b1: e.tensor_tensor(low, b0, b1, ALU.add), s0, s1)
                    gates.give(g0, s_)
                    gates.give(g1, s_)
                    t_m.append(split(mT[:, c, :], mT_low[:, c, :], mT_low[:, c, :], s_))
            t_mixed = project_out("mixer out", KD, lambda k, i: (tok_of(mT, i)(k), tok_of(mT_low, i)(k)), t_m, scale=1.0)
            return [t_mixed, t_m]

        def experts(work_free):
            p.stage("router")
            carve_from(0)
            hn = carve(NT, D)
            tri, ones = carve(P), carve(P)
            router_w = carve(KD, GROUPS + EXPERTS)
            router_b = carve(GROUPS + EXPERTS)
            down8, iota64 = carve(8), carve(EXPERTS)
            logits = carve(NT, GROUPS + EXPERTS)
            g8, s8, t8, oh_g = (carve(NT, 8) for _ in range(4))
            ohs = [carve(NT, 8) for _ in range(2)]
            v4 = [carve(NT) for _ in range(12)]
            picks = [carve(NT, EXPERTS) for _ in range(2)]
            both, rank, wide = (carve(NT, EXPERTS) for _ in range(3))
            local = carve(NT, EXPERTS)
            extra, ends, begins = (carve(EXPERTS) for _ in range(3))
            e15 = carve(MORE, EXPERTS)
            more_f, more_i = carve(MORE + 1), carve(MORE + 1, dt=I32)
            slot_f = [carve(NT) for _ in range(2)]
            slot_i = [carve(NT, dt=I32) for _ in range(2)]
            gates = [carve(NT) for _ in range(2)]
            loop_at = taken[0]
            LOOP_WORDS = 26 * 256
            carve_from(loop_at + LOOP_WORDS)
            for n, slot in enumerate([memT[:, :, :].rearrange("p k s -> p (k s)")]
                                     + [carve(SLOT) for _ in range((WORK - taken[0]) // SLOT)]):
                add_slot(f"more{n}", slot, work_free)
            look_ahead()
            loaded = load_norm(a["norm_moe_w_2"][0], None)
            t_const = p.dma("scalar", side_sem, tri, a["c_tri"], work_free)
            for dst, src in ((router_w, a["router_w"].rearrange("(t p) n -> p t n", p=P)),
                             (router_b, a["router_b"].partition_broadcast(P)),
                             (down8, a["c_down8"].partition_broadcast(P)),
                             (iota64, a["c_iota64"].partition_broadcast(P))):
                t_const = p.dma("scalar", side_sem, dst, src)
            t_ones = p.pool(lambda e: e.memset(ones, 1.0), work_free)
            hn_done, hT_done = [], []
            for i in range(NT):
                t_hn = rms_rows(i, hn[:, i, :], loaded, work_free)
                hn_done.append(t_hn)
                hT_done += rows_to_T(i, t_hn, src=hn, dst=xT, before=work_free)

            bank, bank_free = banks.take()
            W = GROUPS + EXPERTS

            def make(e, bank=bank):
                for i in range(NT):
                    for k in range(KD):
                        ins = e.matmul(bank[:, i * W:(i + 1) * W], xT[:, k, i * P:(i + 1) * P], router_w[:, k, :],
                                       start=(k == 0), stop=(k == KD - 1))
                return ins
            t = t_router = p.pe(make, bank_free, hT_done, t_const)

            def b3(x, n):
                return x.unsqueeze(2).broadcast_to([P, NT, n])

            def row(x, n):
                return x.unsqueeze(1).broadcast_to([P, NT, n])

            def tt(out, a_, b_, op, *w):
                return p.dve(lambda e: e.tensor_tensor(out, a_, b_, op), *w)

            t = tt(logits, bank[:, 0:NT * W].rearrange("p (i w) -> p i w", i=NT), row(router_b, W), ALU.add, t, t_const)
            banks.give(bank, t)
            lg = logits[:, :, 0:GROUPS]
            gmax, gsum, top, m1, m2 = v4[0], v4[1], v4[2], v4[3], v4[4]

            def argmax_onehot(out, scores, best, t):
                t = p.dve(lambda e: e.tensor_reduce(best, scores, AX.X, ALU.max), t)
                t = tt(t8, scores, b3(best, 8), ALU.is_equal, t)
                t = tt(t8, t8, row(down8, 8), ALU.mult, t)
                t = p.dve(lambda e: e.tensor_reduce(top, t8, AX.X, ALU.max), t)
                return tt(out, row(down8, 8), b3(top, 8), ALU.is_equal, t)

            t = argmax_onehot(oh_g, lg, gmax, t)
            t = tt(g8, lg, b3(gmax, 8), ALU.subtract, t)
            t = p.act(lambda e: e.activation(g8, g8, ACT.Exp), t)
            t = p.dve(lambda e: e.tensor_reduce(gsum, g8, AX.X, ALU.add), t)
            t = p.dve(lambda e: e.reciprocal(gsum, gsum), t)
            for i in range(NT):
                view = logits[:, i, GROUPS:].rearrange("p (g e) -> p e g", g=GROUPS)
                out = wide[:, i, :].rearrange("p (e g) -> p e g", e=PER_GROUP)
                t = tt(out, view, oh_g[:, i, :].unsqueeze(1).broadcast_to([P, PER_GROUP, GROUPS]), ALU.mult, t)
            t = p.dve(lambda e: e.tensor_reduce(s8.rearrange("p i e -> p (i e)"),
                                                wide.rearrange("p i (e g) -> p (i e) g", e=PER_GROUP),
                                                AX.X, ALU.add), t)
            t = argmax_onehot(ohs[0], s8, m1, t)
            t = p.dve(lambda e: e.scalar_tensor_tensor(out=s8, in0=ohs[0], scalar=NEG, in1=s8, op0=ALU.mult,
                                                       op1=ALU.add), t)
            t = argmax_onehot(ohs[1], s8, m2, t)
            d_, r_ = v4[5], v4[6]
            t = tt(d_, m2, m1, ALU.subtract, t)
            t = p.act(lambda e: e.activation(d_, d_, ACT.Exp), t)
            t = p.dve(lambda e: e.tensor_scalar(r_, d_, 1.0, None, ALU.add), t)
            t = p.dve(lambda e: e.reciprocal(r_, r_), t)
            t = tt(gates[0], gsum, r_, ALU.mult, t)
            t = tt(gates[1], gates[0], d_, ALU.mult, t)
            for n in range(2):
                for i in range(NT):
                    out = picks[n][:, i, :].rearrange("p (g e) -> p g e", g=GROUPS)
                    t = tt(out, oh_g[:, i, :].unsqueeze(2).broadcast_to([P, GROUPS, PER_GROUP]),
                           ohs[n][:, i, :].unsqueeze(1).broadcast_to([P, GROUPS, PER_GROUP]), ALU.mult, t)
            t_both = tt(both, picks[0], picks[1], ALU.add, t)
            bank, bank_free = banks.take()

            def make_rank(e, bank=bank):
                for i in range(NT + 1):
                    for j in range(min(i, NT - 1) + 1):
                        last = min(i, NT - 1)
                        ins = e.matmul(bank[:, i * EXPERTS:(i + 1) * EXPERTS], tri if j == i else ones,
                                       both[:, j, :], start=(j == 0), stop=(j == last))
                return ins
            t = p.pe(make_rank, bank_free, t_both, t_ones)
            t = p.dve(lambda e: e.tensor_copy(rank.rearrange("p i e -> p (i e)"), bank[:, 0:NT * EXPERTS]), t)
            count = bank[:, NT * EXPERTS:(NT + 1) * EXPERTS]
            t = p.dve(lambda e: e.scalar_tensor_tensor(out=local, in0=rank, scalar=1.0, in1=both, op0=ALU.add,
                                                       op1=ALU.mult), t)
            t_local = p.dve(lambda e: e.tensor_scalar(local, local, -1.0, None, ALU.add), t)
            t = p.dve(lambda e: e.tensor_scalar(extra, count, float(CAP), None, ALU.is_gt), t_local)
            for m in range(2, S // CAP):
                t = p.dve(lambda e, m=m: e.scalar_tensor_tensor(out=extra, in0=count, scalar=float(m * CAP),
                                                                in1=extra, op0=ALU.is_gt, op1=ALU.add), t)
            banks.give(bank, t)
            t = p.dve(lambda e: e.tensor_tensor_scan(ends, ones[:, 0:EXPERTS], extra, 0.0, ALU.mult, ALU.add), t, t_ones)
            t = tt(begins, ends, extra, ALU.subtract, t)
            t = p.dve(lambda e: e.tensor_tensor(e15, ends.unsqueeze(1).broadcast_to([P, MORE, EXPERTS]),
                                                iota64[:, 0:MORE].unsqueeze(2).broadcast_to([P, MORE, EXPERTS]),
                                                ALU.is_le), t)
            t = p.dve(lambda e: e.tensor_reduce(more_f[:, 0:MORE], e15, AX.X, ALU.add), t)
            t = p.dve(lambda e: e.tensor_scalar(more_f[:, 0:MORE], more_f[:, 0:MORE], float(EXPERTS - 1), None,
                                                ALU.min), t)
            t = p.dve(lambda e: e.tensor_copy(more_f[:, MORE:MORE + 1], ends[:, EXPERTS - 1:EXPERTS]), t)
            t_more = p.dve(lambda e: e.tensor_copy(more_i, more_f), t)
            t_slot = []
            rk, ex, bg, fl = v4[7], v4[8], v4[9], v4[10]
            t = t_more
            for n in range(2):
                for out, by in ((rk, rank), (ex, row(iota64, EXPERTS)), (bg, row(begins, EXPERTS))):
                    t = tt(wide, picks[n], by, ALU.mult, t)
                    t = p.dve(lambda e, out=out: e.tensor_reduce(out, wide, AX.X, ALU.add), t)
                t = p.dve(lambda e: e.tensor_scalar(fl, rk, float(CAP), None, ALU.is_ge), t)
                t = p.dve(lambda e: e.scalar_tensor_tensor(out=bg, in0=bg, scalar=float(EXPERTS - 1), in1=ex,
                                                           op0=ALU.add, op1=ALU.subtract), t)
                t = tt(bg, bg, fl, ALU.mult, t)
                t = tt(bg, bg, ex, ALU.add, t)
                t = p.dve(lambda e, n=n: e.scalar_tensor_tensor(out=slot_f[n], in0=bg, scalar=float(CAP), in1=rk,
                                                                op0=ALU.mult, op1=ALU.add), t)
                t = p.dve(lambda e, n=n: e.tensor_copy(slot_i[n], slot_f[n]), t)
                t_slot.append(t)

            p.stage("experts")
            carve_from(loop_at)
            chosen = Pool_([carve(NT, CAP) for _ in range(2)])
            rows_ = Pool_([carve(BANK) for _ in range(2)])
            xeT = Pool_([carve(4, 2, CAP) for _ in range(2)])
            silus = Pool_([carve(BANK, parts=CAP) for _ in range(2)])
            hids = Pool_([carve(EH, parts=CAP) for _ in range(2)])
            hidT = Pool_([carve(EH // P, CAP) for _ in range(2)])
            outs = Pool_([carve(BANK) for _ in range(3)])
            assert taken[0] <= loop_at + LOOP_WORDS
            for n in range(2):
                add_slot(f"xT{n}", xT[:, :, :].rearrange("p k s -> p (k s)")[:, n * SLOT:(n + 1) * SLOT], t_router)
            for n, slot in enumerate(high_slots):
                add_slot(f"high{n}", slot, t_router)
            reuse = [t_slot, hn_done]
            def gather_rows(choose):
                ch, ch_free = chosen.take()
                c = choose(ch, [ch_free, reuse])
                bank, bank_free = banks.take()

                def make(e):
                    for i in range(NT):
                        for half in range(2):
                            ins = e.matmul(bank[half * CAP:(half + 1) * CAP, :], ch[:, i, :],
                                           hn[:, i, half * BANK:(half + 1) * BANK],
                                           start=(i == 0), stop=(i == NT - 1))
                    return ins
                t = p.pe(make, c, bank_free)
                chosen.give(ch, t)
                r, r_free = rows_.take()
                c = p.act(lambda e: e.activation(r, bank[:, :], ACT.Copy), t, r_free, reuse)
                banks.give(bank, c)
                return r, c

            def rows_transposed(r, ready):
                bank, bank_free = banks.take()

                def make(e):
                    for j in range(4):
                        ins = e.transpose(bank[:, j * P:(j + 1) * P], r[:, j * P:(j + 1) * P], ident[:, :])
                    return ins
                t = p.pe(make, ready, bank_free)
                rows_.give(r, t)
                x, x_free = xeT.take()
                c = p.dve(lambda e: e.tensor_copy(x.rearrange("p a b c -> p (a b c)"), bank[:, :]), t, x_free, reuse)
                banks.give(bank, c)
                return x, c

            def hidden(x, ready, wg, wu, landed):
                bank, bank_free = banks.take()

                def make(e):
                    for k in range(KD):
                        xk = x[:, k % 4, k // 4, :]
                        for n, w in ((0, wg), (1, wu)):
                            ins = e.matmul(bank[n * CAP:(n + 1) * CAP, :], xk, w[k // 4][:, k % 4, :],
                                           start=(k == 0), stop=(k == KD - 1))
                    return ins
                t = p.pe(make, ready, bank_free, landed)
                xeT.give(x, t)
                s, s_free = silus.take()
                c = p.act(lambda e: e.activation(s, bank[0:CAP, :], ACT.Silu), t, s_free, reuse)
                h, h_free = hids.take()
                c = p.dve(lambda e: e.tensor_tensor(h, s, bank[CAP:2 * CAP, :], ALU.mult), c, h_free, reuse)
                banks.give(bank, c)
                silus.give(s, c)
                return h, c, t

            def hidden_transposed(h, ready):
                bank, bank_free = banks.take()

                def make(e):
                    for j in range(EH // P):
                        ins = e.transpose(bank[:, j * CAP:(j + 1) * CAP], h[:, j * P:(j + 1) * P],
                                          ident[0:CAP, 0:CAP])
                    return ins
                t = p.pe(make, ready, bank_free)
                hids.give(h, t)
                hT_, h_free = hidT.take()
                c = p.act(lambda e: e.activation(hT_.rearrange("p a b -> p (a b)"), bank[:, 0:4 * CAP], ACT.Copy),
                          t, h_free, reuse)
                banks.give(bank, c)
                return hT_, c

            def expert_out(hT_, ready, wd, landed, block, store_sem):
                bank, bank_free = banks.take()

                def make(e):
                    for k in range(EH // P):
                        for half in range(2):
                            ins = e.matmul(bank[half * CAP:(half + 1) * CAP, :], hT_[:, k, :],
                                           wd[k // 2][:, k % 2, half * BANK:(half + 1) * BANK],
                                           start=(k == 0), stop=(k == EH // P - 1))
                    return ins
                t = p.pe(make, ready, bank_free, landed)
                hidT.give(hT_, t)
                o, o_free = outs.take()
                c = p.act(lambda e: e.activation(o, bank[:, :], ACT.Copy), t, o_free, reuse)
                banks.give(bank, c)
                for half in range(2):
                    s = p.dma("scalar", store_sem, y_slots[block * CAP:(block + 1) * CAP, half * BANK:(half + 1) * BANK],
                              o[half * CAP:(half + 1) * CAP, :], c, t_clear)
                outs.give(o, s)
                return t, s

            store_sems = [p.semaphore(f"block_stores{j}") for j in range(3)]

            def first_choose(ex_):
                def choose(ch, free):
                    t = None
                    for i in range(NT):
                        t = p.dve(lambda e, i=i: e.tensor_scalar(ch[:, i, :], iota64, local[:, i, ex_:ex_ + 1], None,
                                                                 ALU.is_equal), free)
                    return t
                return choose

            rows, xs, hs, hTs, stored = {}, {}, {}, {}, []
            down = {}
            for n in range(EXPERTS + 2):
                if n < EXPERTS:
                    rows[n] = gather_rows(first_choose(n))
                if 1 <= n <= EXPERTS:
                    ex_ = n - 1
                    g, u = ([take_piece(name) for _ in range(2)] for name in ("moe_w1_2", "moe_w3_2"))
                    down[ex_] = [take_piece("moe_w2_2") for _ in range(2)]
                    h, c, t = hidden(*xs.pop(ex_), [q.w for q in g], [q.w for q in u], [q.ready for q in g + u])
                    for q in g + u:
                        q.release(t)
                    hs[ex_] = (h, c)
                if n < EXPERTS:
                    xs[n] = rows_transposed(*rows.pop(n))
                if 2 <= n:
                    ex_ = n - 2
                    pd = down.pop(ex_)
                    t, s = expert_out(*hTs.pop(ex_), [q.w for q in pd], [q.ready for q in pd], ex_,
                                      store_sems[ex_ % 3])
                    for q in pd:
                        q.release(t)
                    stored.append(s)
                if 1 <= n <= EXPERTS:
                    hTs[n - 1] = hidden_transposed(*hs.pop(n - 1))

            p.branch_if(more_i[0:1, MORE:MORE + 1], t_more)
            p.stage("more")
            keep = [(pool_, list(pool_.free)) for pool_ in (banks, chosen, rows_, xeT, silus, hids, hidT, outs)]
            more_landed = p.semaphore("more_landed")
            more_stored = [p.semaphore(f"more_stored{j}") for j in range(3)]
            six = piece_pool.free[0:6]
            t_free = [f for _, f in six]
            views = [s_[:, 0:SLOT].rearrange("p (t n) -> p t n", n=n)
                     for (s_, _), n in zip(six, (EH, EH, EH, EH, D, D))]
            for j in range(MORE):
                def load(dst, w, k, j=j):
                    def make(e):
                        ex_ = e.value_load(more_i[0:1, j:j + 1], min_val=0, max_val=EXPERTS - 1)
                        return e.dma_start(dst, w[bass.ds(ex_, 1), k:k + dst.shape[1] * P, :].rearrange(
                            "o (t p) n -> p (o t) n", p=P))
                    return make
                for n, (dst, name) in enumerate(zip(views, ("moe_w1_2",) * 2 + ("moe_w3_2",) * 2 + ("moe_w2_2",) * 2)):
                    landed = p.put("sync", [t_free, t_more], load(dst, a[name][0], n % 2 * dst.shape[1] * P),
                                   more_landed, 16)

                def choose(ch, free, j=j):
                    t = None
                    base = float((EXPERTS + j) * CAP)
                    for i in range(NT):
                        t = p.dve(lambda e, i=i: e.tensor_scalar(ch[:, i, :], iota64, base, slot_f[0][:, i:i + 1],
                                                                 ALU.add, ALU.is_equal), free, t)
                        tmp = wide[:, i, 0:CAP]
                        t = p.dve(lambda e, i=i, tmp=tmp: e.tensor_scalar(tmp, iota64, base, slot_f[1][:, i:i + 1],
                                                                          ALU.add, ALU.is_equal), t)
                        t = p.dve(lambda e, i=i, tmp=tmp: e.tensor_tensor(ch[:, i, :], ch[:, i, :], tmp, ALU.add), t)
                    return t
                r, c = gather_rows(choose)
                x, c = rows_transposed(r, c)
                h, c, t = hidden(x, c, views[0:2], views[2:4], landed)
                hT_, c = hidden_transposed(h, c)
                t, s = expert_out(hT_, c, views[4:6], landed, EXPERTS + j, more_stored[j % 3])
                t_free = [t]
            p.join(["more_scalar_done", "more_vector_done", "more_tensor_done", "more_gpsimd_done",
                    more_landed, *more_stored])
            p.branch_end()
            for pool_, free in keep:
                pool_.free = free

            p.stage("combine")
            carve_from(loop_at)
            fetched = {(i, n): carve(D) for i in range(NT) for n in range(2)}
            results = [carve(D) for _ in range(NT)]
            loaded = load_norm(a["norm_final_w_2"], None)
            loop_free = [t for pool_ in (piece_pool, chosen, rows_, xeT, silus, hids, hidT, outs) for _, t in pool_.free]
            t_rows = {}
            for (i, n), f in fetched.items():
                idx = slot_i[n][:, i:i + 1]
                t_rows[i, n] = p.put("gpsimd", [stored, t_clear, t_slot, loop_free],
                                     lambda e, f=f, idx=idx: e.indirect_dma_start(
                                         out=f, out_offset=None, in_=y_slots[:, :],
                                         in_offset=bass.IndirectOffsetOnAxis(ap=idx, axis=0)),
                                     p.semaphore(f"rows_fetched{i}_{n}"), 16)
            for i in range(NT):
                x = x_tok[:, i, :]
                for n in range(2):
                    state["x"][i] = p.dve(lambda e, f=fetched[i, n], x=x, i=i, n=n: e.scalar_tensor_tensor(
                        out=x, in0=f, scalar=gates[n][:, i:i + 1], in1=x, op0=ALU.mult, op1=ALU.add),
                        t_rows[i, n], state["x"][i])
                o = results[i]
                c = rms_rows(i, o, loaded, loop_free)
                p.dma("sync", out_sem, result[0, i * P:(i + 1) * P, :], o, c)

        y_slots = nc.dram_tensor("y_slots", [BLOCKS * CAP, D], F32, kind="Internal").ap()
        y_attT, t_att, t_x = dilated_attention([work_free, state["xT"]])
        used = [t_att, ("attention_vector_done", p.reached["attention_vector_done"]),
                ("attention_tensor_done", p.reached["attention_tensor_done"]),
                ("attention_gpsimd_done", p.reached["attention_gpsimd_done"])]

        cleared = p.semaphore("further_slots_cleared")
        parts = MORE * CAP // 8
        p.stage("clear")
        t_clear = p.pool(lambda e: e.memset(shift[0:parts, :], 0.0), state["norm_free"])
        t_clear = p.dma("gpsimd", cleared, y_slots[EXPERTS * CAP:, :].rearrange("(p r) d -> p r d", r=8),
                        shift[0:parts, :].unsqueeze(1).broadcast_to([parts, 8, D]), t_clear)
        y_retT, t_ret, merged_at, merge_tail = retention(NT * S, t_x, used)
        last = merge(y_attT, t_att, y_retT, t_ret, merged_at, merge_tail, t_x)
        experts([last, state["x"]])

        p.raw("gpsimd", lambda e: e.wait_ge(p.names[out_sem], p.reached[out_sem]))
        p.emit(ctx.enter_context(nc.Block()))


def constants():
    f = np.float32
    def swap(blocks, size):
        m = np.zeros((size, size), f)
        for lo, half in blocks:
            for j in range(half):
                m[lo + half + j, lo + j] = -1.0
                m[lo + j, lo + half + j] = 1.0
        return m
    c = {"c_ident": np.eye(P, dtype=f),
         "c_swap_a": swap([(0, 32), (64, 32)], P),
         "c_swap_q": swap([(NOPE, ROPE // 2)], QKD)}
    inv = (np.float32(10000.0) ** (-np.arange(0, ROPE, 2, dtype=f) / np.float32(ROPE))).astype(f)
    c["c_freq"] = np.concatenate([np.zeros(NOPE, f), inv, inv])[:, None].copy()
    mask = np.zeros((P, S), f)
    mask[:KV_CHUNK, S - KV_CHUNK:] = NEG
    c["c_mask_q"] = mask
    token = np.arange(S).reshape(-1, DIL).T.reshape(-1)
    masks = np.zeros((P, NT * S + 2 * P), np.uint16)
    minus = np.uint16(np.array([NEG], f).view(np.uint32)[0] >> 16)
    lane = np.arange(P)
    (w0, _), (w1, d1), (w2, d2) = WINDOWS
    for r in range(DIL):
        far = np.abs((DIL * lane + r)[:, None] - token[None, :]) > w0 // 2
        masks[:, r * S:(r + 1) * S][far] = minus
    apart = DIL * (lane[:, None] - lane[None, :])
    masks[:, NT * S:NT * S + P][(apart % d1 != 0) | (np.abs(apart) > w1 // 2)] = minus
    masks[:, NT * S + P:][(apart % d2 != 0) | (np.abs(apart) > w2 // 2)] = minus
    c["c_mask_a"] = masks
    inv = (1.0 / (np.float32(10000.0) ** (np.arange(0, AHD, 2, dtype=f) / np.float32(AHD)))).astype(f)
    ang = (np.arange(S, dtype=f)[None, :] * inv[lane % (AHD // 2)][:, None]).astype(f)
    cos, sin = np.cos(ang).astype(f), np.sin(ang).astype(f)
    c["c_cos_a"], c["c_sin_a"] = np.ascontiguousarray(cos[:, token]), np.ascontiguousarray(sin[:, token])
    col = np.arange((2 * NT - 1) * P)[None, :]
    rel = DIL * (col % P - lane[:, None]) + col // P - (NT - 1)
    c["c_ahead"] = np.maximum(rel, 0).astype(np.float16)
    c["c_behind"] = np.maximum(-rel, 0).astype(np.float16)
    c["c_twice"] = ((1 + (rel == 0)) * RQK ** -0.5).astype(np.float16)
    c["c_tri"] = (lane[:, None] < lane[None, :]).astype(f)
    c["c_down8"] = np.arange(8, 0, -1).astype(f)
    c["c_iota64"] = np.arange(EXPERTS).astype(f)
    return c


def columns(inputs):
    out = np.zeros((P, PC_ALL), np.float32)
    tile = lambda v: np.asarray(v).reshape(-1, P).T
    for l in range(DEPTH):
        o = l * PC_LAYER
        b = np.asarray(inputs["mix_b_in"])[l]
        out[NOPE:QKD, o + PC_KR] = b[2 * RANK:2 * RANK + ROPE]
        u = b[2 * RANK + ROPE:]
        out[:, o + PC_UA:o + PC_UA + CT] = tile(u[:CONV])
        out[:, o + PC_UG:o + PC_UG + CT] = tile(u[CONV:])
        out[:, o + PC_QN:o + PC_QN + 2] = tile(np.asarray(inputs["mla_q_norm"])[l])
        out[:, o + PC_QN + 2:o + PC_QN + 4] = tile(np.asarray(inputs["mla_kv_norm"])[l])
        w = np.asarray(inputs["conv_dw_w"])[l].reshape(TAPS, CT, P)
        out[:, o + PC_W:o + PC_W + CT * TAPS] = w.transpose(2, 1, 0).reshape(P, CT * TAPS)
        out[:, o + PC_DWB:o + PC_DWB + CT] = tile(np.asarray(inputs["conv_dw_b"])[l])
        out[:, o + PC_CNG:o + PC_CNG + CT] = tile(np.asarray(inputs["conv_norm_g"])[l])
        out[:, o + PC_CNB:o + PC_CNB + CT] = tile(np.asarray(inputs["conv_norm_b"])[l])
    out[:, PC_GATE:PC_GATE + 2 * KD] = tile(np.asarray(inputs["b_branch_gate_2"])[0])
    return out


_DIRECT = ["x", "mem", "positions", "mix_w_in", "mix_b_in", "mla_w_uq", "mla_w_ukv", "mix_w_o",
           "ln1_g", "ln1_b", "xa_w_q", "xa_w_kv", "xa_w_o", "ln2_g", "ln2_b", "ffn_w_in", "ffn_w_down",
           "ln3_g", "ln3_b", "norm_mix_w_2", "w_in_2", "ret_gn_w_2", "w_attn_branch_2", "w_ret_branch_2",
           "w_out_2", "norm_moe_w_2", "moe_w1_2", "moe_w3_2", "moe_w2_2", "norm_final_w_2"]


def arranged(inputs):
    arrays = {n: np.ascontiguousarray(inputs[n]) for n in _DIRECT}
    arrays["cols"] = columns(inputs)
    w = np.asarray(inputs["w_in_2"])[0][:, :3 * NG * AH * AHD].reshape(D, 3, NG, AH // 2, P)
    arrays["w_attn_2"] = np.ascontiguousarray(w.transpose(0, 3, 1, 2, 4)).reshape(D, -1)
    arrays["decays"] = np.concatenate([inputs["ret_decay_fwd_2"], inputs["ret_decay_bwd_2"]])
    arrays["router_w"] = np.concatenate([inputs["moe_w_group_2"][0], inputs["moe_w_expert_2"][0]], axis=1)
    arrays["router_b"] = np.concatenate([inputs["moe_b_group_2"][0], inputs["moe_b_expert_2"][0]])
    arrays.update(constants())
    return arrays


def kernel(**inputs):
    import concourse.bacc as bacc
    from concourse.bass_utils import run_bass_kernel_spmd

    nc = bacc.Bacc("TRN2", target_bir_lowering=False, num_devices=1)
    arrays = {f"in_{n}": v for n, v in arranged(inputs).items()}
    dram = {n[3:]: nc.dram_tensor(n, v.shape, mybir.dt.from_np(v.dtype), kind="ExternalInput").ap()
            for n, v in arrays.items()}
    out = nc.dram_tensor("out_0", (1, S, D), F32, kind="ExternalOutput").ap()
    both_blocks(nc, dram, out)
    got = run_bass_kernel_spmd(nc, [arrays], core_ids=[0])
    return got.results[0]["out_0"]
```
